# Optimizing a Trainium2 kernel written in Bass

```python
import jax, jax.numpy as jnp
from jax import lax
import numpy as np

D_MODEL = 1024
BATCH = 1
SEQ = 512
DEPTH = 1

GRID_W = 64
N_MEM = 256
EPS = 1e-6
Q_BLOCK = 128

NA_HEADS = 8
NA_HEAD_DIM = 64
NA_WIN_R = 8
NA_WIN_C = 16
MLA_HEADS = 8
MLA_NOPE = 64
MLA_ROPE = 32
MLA_V = 64
MLA_Q_RANK = 384
MLA_KV_RANK = 256
ROPE_BASE = 10000.0
MEM_HEADS = 4
MEM_HEAD_DIM = 128
N_EXPERTS = 16
EC_FACTOR = 2
EXPERT_FF = 1024

NA_W = NA_HEADS * NA_HEAD_DIM
MLA_W = MLA_HEADS * MLA_V
MEM_W = MEM_HEADS * MEM_HEAD_DIM
N_BRANCH = 3
IN_SIZES = [NA_W, NA_W, NA_W, MLA_Q_RANK, MLA_KV_RANK, MLA_ROPE, MEM_W, N_BRANCH * D_MODEL]
IN_COLS = int(sum(IN_SIZES))
IN_SPLITS = [int(v) for v in np.cumsum(IN_SIZES)[:-1]]

kernel_name = 'hybrid_na_mla_mem_ec_block'

def rmsnorm(x, g):
    xf = x.astype(jnp.float32)
    y = xf * lax.rsqrt(jnp.mean(xf * xf, axis=-1, keepdims=True) + EPS)
    return (y * g.astype(jnp.float32)).astype(x.dtype)

def rope_1d(x, pos):
    d = x.shape[-1]
    inv = ROPE_BASE ** (-jnp.arange(0, d, 2, dtype=jnp.float32) / d)
    ang = pos.astype(jnp.float32)[:, None] * inv[None, :]
    cos = jnp.cos(ang)[None, :, None, :]
    sin = jnp.sin(ang)[None, :, None, :]
    xf = x.astype(jnp.float32)
    x1, x2 = xf[..., : d // 2], xf[..., d // 2:]
    return jnp.concatenate([x1 * cos - x2 * sin, x1 * sin + x2 * cos], axis=-1).astype(x.dtype)

def axial_rope(x, row, col):
    half = x.shape[-1] // 2
    return jnp.concatenate([rope_1d(x[..., :half], row), rope_1d(x[..., half:], col)], axis=-1)

def neighbourhood_attention(q, k, v, rpb):
    b, s, h, dh = q.shape
    rows = s // GRID_W
    kr = min(NA_WIN_R, rows)
    kc = NA_WIN_C
    q = q.reshape(b, rows, GRID_W, h, dh)
    k = k.reshape(b, rows, GRID_W, h, dh)
    v = v.reshape(b, rows, GRID_W, h, dh)
    cols = jnp.arange(GRID_W)
    col_start = jnp.clip(cols - kc // 2, 0, GRID_W - kc)
    col_idx = col_start[:, None] + jnp.arange(kc)[None, :]
    bias_c = col_idx - cols[:, None] + (NA_WIN_C - 1)
    rpb = rpb.astype(jnp.float32)
    scale = dh ** -0.5

    def row_block(r):
        rs = jnp.clip(r - kr // 2, 0, rows - kr)
        k_band = lax.dynamic_slice_in_dim(k, rs, kr, axis=1)
        v_band = lax.dynamic_slice_in_dim(v, rs, kr, axis=1)
        k_win = k_band[:, :, col_idx]
        v_win = v_band[:, :, col_idx]
        q_row = lax.dynamic_index_in_dim(q, r, axis=1, keepdims=False)
        logits = jnp.einsum('bqhd,brqkhd->bhqrk', q_row, k_win,
                            preferred_element_type=jnp.float32) * scale
        dr = rs + jnp.arange(kr) - r + (NA_WIN_R - 1)
        bias = rpb[:, dr][:, :, bias_c]
        logits = logits + bias.transpose(0, 2, 1, 3)[None]
        p = jax.nn.softmax(logits.reshape(b, h, GRID_W, kr * kc), axis=-1)
        p = p.reshape(b, h, GRID_W, kr, kc).astype(v.dtype)
        return jnp.einsum('bhqrk,brqkhd->bqhd', p, v_win)

    out = lax.map(row_block, jnp.arange(rows))
    return out.transpose(1, 0, 2, 3, 4).reshape(b, s, h * dh)

def blocked_attention(q, k, v, scale):
    b, s, h, d = q.shape
    dv = v.shape[-1]
    nb = s // Q_BLOCK
    qb = q.reshape(b, nb, Q_BLOCK, h, d).transpose(1, 0, 2, 3, 4)

    def one(qblk):
        logits = jnp.einsum('bqhd,bkhd->bhqk', qblk, k,
                            preferred_element_type=jnp.float32) * scale
        p = jax.nn.softmax(logits, axis=-1).astype(v.dtype)
        return jnp.einsum('bhqk,bkhd->bqhd', p, v)

    out = lax.map(one, qb)
    return out.transpose(1, 0, 2, 3, 4).reshape(b, s, h * dv)

def latent_attention(c_q, c_kv, k_rope, q_norm, kv_norm, w_uq, w_ukv, row, col):
    b, s, _ = c_q.shape
    q = (rmsnorm(c_q, q_norm) @ w_uq).reshape(b, s, MLA_HEADS, MLA_NOPE + MLA_ROPE)
    q_nope, q_pe = q[..., :MLA_NOPE], q[..., MLA_NOPE:]
    q = jnp.concatenate([q_nope, axial_rope(q_pe, row, col)], axis=-1)
    kv = (rmsnorm(c_kv, kv_norm) @ w_ukv).reshape(b, s, MLA_HEADS, MLA_NOPE + MLA_V)
    k_nope, v = kv[..., :MLA_NOPE], kv[..., MLA_NOPE:]
    k_pe = axial_rope(k_rope[:, :, None, :], row, col)
    k = jnp.concatenate([k_nope, jnp.broadcast_to(k_pe, (b, s, MLA_HEADS, MLA_ROPE))], axis=-1)
    return blocked_attention(q, k, v, (MLA_NOPE + MLA_ROPE) ** -0.5)

def memory_attention(q, mem, g_mem, w_mem_kv):
    b, s, _ = q.shape
    m = mem.shape[1]
    kv = rmsnorm(mem, g_mem) @ w_mem_kv
    k = kv[..., :MEM_W].reshape(b, m, MEM_HEADS, MEM_HEAD_DIM)
    v = kv[..., MEM_W:].reshape(b, m, MEM_HEADS, MEM_HEAD_DIM)
    q = q.reshape(b, s, MEM_HEADS, MEM_HEAD_DIM)
    logits = jnp.einsum('bshd,bmhd->bhsm', q, k,
                        preferred_element_type=jnp.float32) * (MEM_HEAD_DIM ** -0.5)
    p = jax.nn.softmax(logits, axis=-1).astype(v.dtype)
    return jnp.einsum('bhsm,bmhd->bshd', p, v).reshape(b, s, MEM_W)

def expert_choice_ffn(x, w_router, b_router, w_gate, w_up, w_down):
    b, s, d = x.shape
    cap = EC_FACTOR * s // N_EXPERTS
    logits = jnp.einsum('bsd,de->bse', x, w_router,
                        preferred_element_type=jnp.float32) + b_router.astype(jnp.float32)
    aff = jax.nn.softmax(logits, axis=-1)
    g, idx = lax.top_k(aff.transpose(0, 2, 1), cap)
    xs = jax.vmap(lambda xb, ib: xb[ib])(x, idx)
    hg = jnp.einsum('becd,edf->becf', xs, w_gate)
    hu = jnp.einsum('becd,edf->becf', xs, w_up)
    y = jnp.einsum('becf,efd->becd', jax.nn.silu(hg) * hu, w_down)
    y = y * g[..., None].astype(y.dtype)
    return jax.vmap(lambda yb, ib: jnp.zeros((s, d), yb.dtype).at[ib.reshape(-1)].add(yb.reshape(-1, d)))(y, idx)

def setup_inputs(seed: int = 0) -> dict:
    key = jax.random.key(seed)
    ks = jax.random.split(key, 24)
    L = DEPTH
    nrm = lambda k, shape: jax.random.normal(k, shape, jnp.float32)
    w = lambda k, shape, fan_in: nrm(k, shape) * (fan_in ** -0.5)
    gain = lambda k, shape: 1.0 + 0.05 * nrm(k, shape)
    return {
        'x': nrm(ks[0], (BATCH, SEQ, D_MODEL)),
        'mem': nrm(ks[1], (BATCH, N_MEM, D_MODEL)),
        'g_mix': gain(ks[2], (L, D_MODEL)),
        'w_in': w(ks[3], (L, D_MODEL, IN_COLS), D_MODEL),
        'na_rpb': 0.1 * nrm(ks[4], (L, NA_HEADS, 2 * NA_WIN_R - 1, 2 * NA_WIN_C - 1)),
        'mla_q_norm': gain(ks[5], (L, MLA_Q_RANK)),
        'w_mla_uq': w(ks[6], (L, MLA_Q_RANK, MLA_HEADS * (MLA_NOPE + MLA_ROPE)), MLA_Q_RANK),
        'mla_kv_norm': gain(ks[7], (L, MLA_KV_RANK)),
        'w_mla_ukv': w(ks[8], (L, MLA_KV_RANK, MLA_HEADS * (MLA_NOPE + MLA_V)), MLA_KV_RANK),
        'g_mem': gain(ks[9], (L, D_MODEL)),
        'w_mem_kv': w(ks[10], (L, D_MODEL, 2 * MEM_W), D_MODEL),
        'w_o_na': w(ks[11], (L, NA_W, D_MODEL), NA_W),
        'w_o_mla': w(ks[12], (L, MLA_W, D_MODEL), MLA_W),
        'w_o_mem': w(ks[13], (L, MEM_W, D_MODEL), MEM_W),
        'w_out': w(ks[14], (L, D_MODEL, D_MODEL), D_MODEL),
        'g_ffn': gain(ks[15], (L, D_MODEL)),
        'w_router': w(ks[16], (L, D_MODEL, N_EXPERTS), D_MODEL),
        'b_router': 0.01 * nrm(ks[17], (L, N_EXPERTS)),
        'w_gate': w(ks[18], (L, N_EXPERTS, D_MODEL, EXPERT_FF), D_MODEL),
        'w_up': w(ks[19], (L, N_EXPERTS, D_MODEL, EXPERT_FF), D_MODEL),
        'w_down': w(ks[20], (L, N_EXPERTS, EXPERT_FF, D_MODEL), EXPERT_FF),
        'g_final': gain(ks[21], (D_MODEL,)),
    }

def reference(x, mem, g_mix, w_in, na_rpb, mla_q_norm, w_mla_uq, mla_kv_norm, w_mla_ukv,
              g_mem, w_mem_kv, w_o_na, w_o_mla, w_o_mem, w_out, g_ffn, w_router, b_router,
              w_gate, w_up, w_down, g_final):
    b, s, d = x.shape
    t = jnp.arange(s)
    row, col = t // GRID_W, t % GRID_W
    h = x
    for l in range(DEPTH):
        n = rmsnorm(h, g_mix[l])
        z = n @ w_in[l]
        q_na, k_na, v_na, c_q, c_kv, k_rope, q_mem, gate_logits = jnp.split(z, IN_SPLITS, axis=-1)
        shp = (b, s, NA_HEADS, NA_HEAD_DIM)
        y_na = neighbourhood_attention(q_na.reshape(shp), k_na.reshape(shp), v_na.reshape(shp), na_rpb[l])
        y_mla = latent_attention(c_q, c_kv, k_rope, mla_q_norm[l], mla_kv_norm[l],
                                 w_mla_uq[l], w_mla_ukv[l], row, col)
        y_mem = memory_attention(q_mem, mem, g_mem[l], w_mem_kv[l])
        gates = jax.nn.sigmoid(gate_logits.reshape(b, s, N_BRANCH, d))
        merged = (gates[:, :, 0] * (y_na @ w_o_na[l])
                  + gates[:, :, 1] * (y_mla @ w_o_mla[l])
                  + gates[:, :, 2] * (y_mem @ w_o_mem[l]))
        h = h + merged @ w_out[l]
        h = h + expert_choice_ffn(rmsnorm(h, g_ffn[l]), w_router[l], b_router[l],
                                  w_gate[l], w_up[l], w_down[l])
    return rmsnorm(h, g_final)


_drawn_inputs = setup_inputs


def setup_inputs(seed=0):
    import zlib

    import numpy as np

    out = dict(_drawn_inputs(seed))
    spreads = {}
    factors = {'g_mix': 3.988,
     'na_rpb': 4.811,
     'mla_q_norm': 8.0,
     'mla_kv_norm': 8.0,
     'g_mem': 7.014,
     'b_router': 64.0,
     'g_ffn': 8.0}
    for name, (base, spread) in spreads.items():
        noise = np.random.default_rng([zlib.crc32(name.encode()), seed]).standard_normal(out[name].shape)
        drawn = base * np.exp(spread * noise) if base else spread * noise
        out[name] = __import__('jax').numpy.asarray(drawn.astype(out[name].dtype))
    for name, factor in factors.items():
        out[name] = (out[name] * factor).astype(out[name].dtype)
    return out
```

```python
from contextlib import ExitStack

import numpy as np

import concourse.bass as bass
from concourse import mybir

F32 = mybir.dt.float32
F32R = mybir.dt.float32r
U32 = mybir.dt.uint32
ACT = mybir.ActivationFunctionType
ALU = mybir.AluOpType
AX = mybir.AxisListType

P = 128
D = 1024
S = 512
GRID_W = 64
ROWS = S // GRID_W
N_MEM = 256
EPS = 1e-6
NA_HEADS, NA_DIM = 8, 64
WIN_R, WIN_C = 8, 16
MLA_HEADS, NOPE, ROPE, MLA_V = 8, 64, 32, 64
Q_RANK, KV_RANK = 384, 256
ROPE_BASE = 10000.0
MEM_HEADS, MEM_DIM = 4, 128
N_EXP, FF = 16, 1024
CAP = 2 * S // N_EXP
NA_W = NA_HEADS * NA_DIM
MEM_W = MEM_HEADS * MEM_DIM
MLA_QK = NOPE + ROPE
KB = D // P
TB = S // P
MB = N_MEM // P
PAIRS = N_EXP // 2
HALF = D // 2
C_Q, C_K, C_V = 0, NA_W, 2 * NA_W
C_CQ = 3 * NA_W
C_CKV = C_CQ + Q_RANK
C_KR = C_CKV + KV_RANK
C_QM = C_KR + ROPE
C_GATE = C_QM + MEM_W
MASKED = -1.0e30
LOWEST = -3.0e38

G_MIX, G_MEM, G_Q, G_KV, G_FFN = 0, KB, 2 * KB, 2 * KB + 3, 2 * KB + 5
GAIN_ROWS = 3 * KB + 5

COLS_PER_TILE = P // ROWS
RPB_R, RPB_C = 2 * WIN_R - 1, 2 * WIN_C - 1
TOEP_U = 3 * COLS_PER_TILE
RPB_PITCH, RPB_PAD = 64, 16
RPB_BUF = ROWS * NA_HEADS * ROWS * RPB_PITCH

SLOT_FIRST, SLOT_PREV, SLOT_MID, SLOT_NEXT, SLOT_LAST = range(5)
SLOTS = [(SLOT_FIRST, 0, True, False), (SLOT_PREV, -1, True, False), (SLOT_MID, 0, True, True),
         (SLOT_NEXT, 1, False, True), (SLOT_LAST, 0, False, True)]


def key_tiles(qb):
    return list(range(max(qb - 1, 0), min(qb + 1, TB - 1) + 1))


def table_slots(qb):
    if qb == 0:
        return SLOT_FIRST, SLOT_NEXT - SLOT_FIRST, 2
    if qb == TB - 1:
        return SLOT_PREV, SLOT_LAST - SLOT_PREV, 2
    return SLOT_PREV, 1, 3


def plan():
    jobs, steps = [], []

    def job(src, c0, n, kb):
        jobs.append((src, c0, n, kb))
        return len(jobs) - 1

    def tile(kind, args, j=None):
        steps.append(("tile", kind, args, j))

    for kb in range(KB):
        tile("memT", (kb,))
    for kb in range(KB):
        tile("nT", (kb,))
    for c in range(2):
        j = job("mem_kv", 256 * c, 256, KB)
        for i in range(2):
            tile("kmem", (2 * c + i, i), j)
        steps.append(("end", j))
    for c in range(2):
        j = job("mem_kv", MEM_W + 256 * c, 256, KB)
        for m in range(MB):
            tile("vmem", (m, c), j)
        steps.append(("end", j))
    for kind, c0 in (("qna", C_Q), ("kna", C_K)):
        for c in range(2):
            j = job("in", c0 + 256 * c, 256, KB)
            for i in range(2):
                tile(kind, (2 * c + i, i), j)
            steps.append(("end", j))
    for c in range(2):
        j = job("in", C_V + 256 * c, 256, KB)
        for t in range(TB):
            tile("vna", (t, c), j)
        steps.append(("end", j))
    for c0, n in ((0, 2), (2, 1)):
        j = job("in", C_CQ + P * c0, P * n, KB)
        for i in range(n):
            tile("cq", (c0 + i, i), j)
        steps.append(("end", j))
    tile("ssq", ("q",))
    j = job("in", C_CKV, 256, KB)
    for i in range(2):
        tile("ckv", (i, i), j)
    steps.append(("end", j))
    tile("ssq", ("kv",))
    j = job("in", C_KR - NOPE, MLA_QK, KB)
    tile("kpe", (), j)
    steps.append(("end", j))
    for c in range(2):
        j = job("in", C_QM + 256 * c, 256, KB)
        for i in range(2):
            tile("qmem", (2 * c + i, i), j)
        steps.append(("end", j))
    steps.append(("attn", "na"))
    steps.append(("attn", "mem"))
    steps.append(("latent",))
    for c in range(2):
        j = job("uq", 4 * MLA_QK * c, 4 * MLA_QK, Q_RANK // P)
        for i in range(4):
            tile("uq", (4 * c + i, i), j)
        steps.append(("end", j))
    j = job("ukv", 0, 1024, KV_RANK // P)
    for h in range(MLA_HEADS):
        tile("uk", (h,), j)
    for t in range(TB):
        tile("vmla", (t,), j)
    steps.append(("end", j))
    steps.append(("attn", "mla"))
    for n, (br, wo) in enumerate(((0, "o_na"), (2, "o_mem"), (1, "o_mla"))):
        for half in range(2):
            j = job(wo, 512 * half, 512, 4)
            for i in range(4):
                tile("o", (br, i), j)
            steps.append(("end", j))
            for c in range(2):
                j = job("in", C_GATE + br * D + 512 * half + 256 * c, 256, KB)
                for i in range(2):
                    tile("gate", (n, 4 * half + 2 * c + i, i), j)
                steps.append(("end", j))
    for c in range(4):
        j = job("out", 256 * c, 256, KB)
        for t in range(TB):
            tile("out", (t, c), j)
        steps.append(("end", j))
    return jobs, steps


def units_of(branch):
    if branch == "mem":
        return [(g, qb, None) for g in range(2) for qb in range(TB)]
    return [(g, qb, hp) for g in range(4) for qb in range(TB) for hp in range(2)]


def width_of(branch, qb):
    return P * len(key_tiles(qb)) if branch == "na" else S


def build(nc, ins, out):
    jobs, steps = plan()
    n_jobs = len(jobs)

    acc_of, unit_base, group_base = {}, {}, {}
    na_, nu_, ng_ = 0, 0, 0
    y_acc = {}
    for n, st in enumerate(steps):
        if st[0] == "tile":
            acc_of[n] = na_
            na_ += 1
        elif st[0] == "attn":
            br = st[1]
            unit_base[br], group_base[br] = nu_, ng_
            us = units_of(br)
            nu_ += len(us)
            groups = us[-1][0] + 1
            ng_ += groups
            for g in range(groups):
                y_acc[br, g] = na_
                na_ += 2 if br == "mem" else 1
    n_acc = na_
    acc_at = {}
    for n, st in enumerate(steps):
        if st[0] == "tile":
            acc_at[(st[1],) + st[2]] = acc_of[n]
    job_end = {st[3]: acc_of[n] + 1 for n, st in enumerate(steps) if st[0] == "tile" and st[3] is not None}
    last_gate = max(a for k, a in acc_at.items() if k[0] == "gate")
    last_acc_use = {"na": y_acc["na", 3] + 1, "mem": y_acc["mem", 1] + 2, "mla": y_acc["mla", 3] + 1}

    with ExitStack() as ctx:
        base = -(-nc.sbuf_base // 64) * 64

        def at(name, shape, off, dt=F32):
            return nc.alloc_sbuf_tensor_at(name, shape, dt, offset=base + off)

        K = 1024
        nt_hi = at("nt_hi", [P, KB, S], 0, F32R)
        nt_lo = at("nt_lo", [P, KB, S], 16 * K, F32R)
        w_raw = [at(f"w_raw{i}", [P, 2048], (32 + 8 * i) * K) for i in range(2)]
        w_hi = [at(f"w_hi{i}", [P, 2048], (48 + 16 * i) * K, F32R) for i in range(2)]
        w_lo = [at(f"w_lo{i}", [P, 2048], (56 + 16 * i) * K, F32R) for i in range(2)]
        q_na = at("q_na", [P, 4, S], 80 * K)
        k_na = at("k_na", [P, 4, S], 88 * K)
        q_mem = at("q_mem", [P, 4, S], 96 * K)
        toep = at("toep", [P, NA_HEADS, ROWS, TOEP_U], 80 * K)
        v_na = at("v_na", [P, TB, NA_W], 112 * K)
        table = at("table", [P, NA_HEADS, 5, P], 120 * K)
        k_mem = at("k_mem", [P, MEM_HEADS, N_MEM], 140 * K)
        v_mem = at("v_mem", [P, MB, MEM_W], 144 * K)
        memt_hi = at("memt_hi", [P, KB, N_MEM], 148 * K, F32R)
        memt_lo = at("memt_lo", [P, KB, N_MEM], 156 * K, F32R)
        c_q = at("c_q", [P, 3, S], 156 * K)
        c_kv = at("c_kv", [P, 2, S], 162 * K)
        k_pe = at("k_pe", [P, S], 166 * K)
        x_tok = at("x_tok", [P, TB, D], 168 * K)
        mem_tok = at("mem_tok", [P, MB, D], 184 * K)
        junk = at("junk", [P, D], 192 * K)
        rms_root = at("rms_root", [P, S], 192 * K)
        rms_inv = at("rms_inv", [P, S], 194 * K)
        probs_t = [at(f"probs_t{i}", [P, 2, TB, S], (168 + 16 * i) * K) for i in range(2)]
        cq_hi = at("cq_hi", [P, 3, S], 168 * K, F32R)
        cq_lo = at("cq_lo", [P, 3, S], 174 * K, F32R)
        ckv_hi = at("ckv_hi", [P, 2, S], 180 * K, F32R)
        ckv_lo = at("ckv_lo", [P, 2, S], 184 * K, F32R)
        q_mla = at("q_mla", [MLA_QK, MLA_HEADS, S], 120 * K)
        k_mla = at("k_mla", [MLA_QK, MLA_HEADS, S], 140 * K)
        v_mla = at("v_mla", [P, TB, MLA_HEADS * MLA_V], 112 * K)
        rope_cs = at("rope_cs", [MLA_QK, 2, S], 136 * K)
        probs = [at(f"probs{i}", [P, S], (200 + 2 * i) * K) for i in range(3)]
        square = [at(f"square{i}", [P, S], (200 + 2 * i) * K) for i in range(3)]
        rope_a = at("rope_a", [MLA_QK, S], 188 * K)
        rope_b = at("rope_b", [MLA_QK, S], 190 * K)
        y_hi, y_lo = {}, {}
        for g in range(4):
            y_hi[0, g] = at(f"y_na_hi{g}", [P, S], (80 + 2 * g) * K, F32R)
            y_lo[0, g] = at(f"y_na_lo{g}", [P, S], (88 + 2 * g) * K, F32R)
            y_hi[2, g] = at(f"y_mem_hi{g}", [P, S], (96 + 2 * g) * K, F32R)
            y_lo[2, g] = at(f"y_mem_lo{g}", [P, S], (104 + 2 * g) * K, F32R)
            y_hi[1, g] = at(f"y_mla_hi{g}", [P, S], (120 + 4 * g) * K, F32R)
            y_lo[1, g] = at(f"y_mla_lo{g}", [P, S], (140 + 4 * g) * K, F32R)
        merged = at("merged", [P, KB, S], 176 * K)
        branch_o = [at(f"branch_o{i}", [P, S], (192 + 2 * i) * K) for i in range(4)]
        gate_s = [at(f"gate_s{i}", [P, S], (200 + 2 * i) * K) for i in range(2)]
        m_hi = at("m_hi", [P, KB, S], 80 * K, F32R)
        m_lo = at("m_lo", [P, KB, S], 96 * K, F32R)
        h_tok = at("h_tok", [P, TB, D], 0)
        hr_tok = at("hr_tok", [P, TB, D], 16 * K)
        hn_t = at("hn_t", [P, KB, S], 32 * K)
        route_w = at("route_w", [P, KB, N_EXP], 204 * K)
        logit_t = at("logit_t", [N_EXP, S], 100 * K)
        aff_t = at("aff_t", [N_EXP, S], 102 * K)
        aff = at("aff", [P, TB, N_EXP], 104 * K)
        top_v = at("top_v", [N_EXP, P], 104 * K + 256)
        top_i = at("top_i", [N_EXP, CAP], 104 * K + 768, U32)
        top_f = at("top_f", [N_EXP, P], 105 * K)
        slot_gain = at("slot_gain", [P, N_EXP], 105 * K + 512)
        slot_row = at("slot_row", [P, N_EXP], 105 * K + 576, U32)
        slot_tok = at("slot_tok", [P, PAIRS], 105 * K + 640, U32)
        row_stat = at("row_stat", [P, 4, TB], 105 * K + 704)
        expert_w = [at(f"expert_w{c}", [P, 4, 1024], off * K) for c, off in enumerate((112, 128, 144, 160, 176, 84))]
        xs_all = at("xs_all", [P, PAIRS, D], 48 * K)
        xs_cur = at("xs_cur", [P, D], 0)
        xs_t = at("xs_t", [P, KB, P], 16 * K)
        silu_s = at("silu_s", [P, 512], 20 * K)
        hidden = at("hidden", [P, 512], 22 * K)
        hidden_t = at("hidden_t", [P, 4, P], 24 * K)
        y_sb = at("y_sb", [P, HALF], 26 * K)
        fin = at("fin", [P, TB, D], 0)
        fin_g = at("fin_g", [P, D], 192 * K)
        junk_b = at("junk_b", [P, D], 196 * K)
        SM = 206 * K
        ident = at("ident", [P, P], SM)
        ones = at("ones", [P, P], SM + 512)
        gain_t = at("gain_t", [P, 32], SM + 1024)
        stat = at("stat", [P, 64], SM + 1152)
        soft_m = at("soft_m", [P, 4, 2], SM + 1408)
        soft_s = at("soft_s", [P, 4, 2], SM + 1440)
        soft_r = at("soft_r", [P, 4, 2], SM + 1472)
        half_col = at("half_col", [P, 1], SM + 1504)
        mark = at("mark", [1, 1], SM + 1600)
        route_b = at("route_b", [N_EXP, 1], SM + 1536)
        eps_col = at("eps_col", [P, 1], SM + 1568)
        gain_rows = at("gain_rows", [GAIN_ROWS, P], 200 * K)

        bank = [ctx.enter_context(nc.psum_tensor(f"bank{i}", [P, 512], F32)) for i in range(8)]
        ACC, SC, TR = bank[0:3], bank[3:6], bank[6:8]

        rpb_rows = nc.dram_tensor("rpb_rows", (ROWS, NA_HEADS * ROWS, RPB_PITCH), F32, kind="Internal").ap()
        hn_rows = nc.dram_tensor("hn_rows", (S, D), F32, kind="Internal").ap()
        sum_rows = nc.dram_tensor("sum_rows", (2 * S, HALF), F32, kind="Internal").ap()

        def sem(name):
            return ctx.enter_context(nc.semaphore(name))

        gains_in, mem_in, rpb_zeroed, rpb_in, toep_in = (sem(x) for x in ("gains_in", "mem_in", "rpb_zeroed", "rpb_in", "toep_in"))
        x_in = sem("x_in")
        rope_in, half_in, resid_in, route_in = (sem(x) for x in ("rope_in", "half_in", "resid_in", "route_in"))
        raw_in = [sem(f"raw_in{i}") for i in range(2)]
        w_hi_ready, w_lo_ready = sem("w_hi_ready"), sem("w_lo_ready")
        const_ready, zeros_ready, ident_ready, table_ready, pool_seq = (sem(x) for x in ("const_ready", "zeros_ready", "ident_ready", "table_ready", "pool_seq"))
        gain_ps, gain_ready = sem("gain_ps"), sem("gain_ready")
        sumsq_done, root_in, root_done, xn_ready = sem("sumsq_done"), sem("root_in"), sem("root_done"), sem("xn_ready")
        acc_done = sem("acc_done")
        acc_free = [sem(f"acc_free{i}") for i in range(3)]
        hi_done = sem("hi_done")
        sq_ready, latent_hi = sem("sq_ready"), sem("latent_hi")
        latent_ready, rope_ready, kpe_spread = sem("latent_ready"), sem("rope_ready"), sem("kpe_spread")
        score_done, max_done, exp_done, p_ready, t_done = (sem(x) for x in ("score_done", "max_done", "exp_done", "p_ready", "t_done"))
        pt_done = [sem("pt_done_act"), sem("pt_done_dve")]
        silu_ready, gate_used, merged_hi, merged_lo = sem("silu_ready"), sem("gate_used"), sem("merged_hi"), sem("merged_lo")
        dve_seq = sem("dve_seq")
        hsq_done, hroot_done, hr_ready, hr_stored = (sem(x) for x in ("hsq_done", "hroot_done", "hr_ready", "hr_stored"))
        hnt_ps, hnt_ready = sem("hnt_ps"), sem("hnt_ready")
        logit_ps, logit_ready, logit_tok, soft_in, soft_exp, aff_ready, aff_ps, top_ready, top_ps, slots_ready = (
            sem(x) for x in ("logit_ps", "logit_ready", "logit_tok", "soft_in", "soft_exp", "aff_ready", "aff_ps", "top_ready", "top_ps", "slots_ready"))
        xs_in, xs_cur_ready, xs_tr, xs_t_ready = sem("xs_in"), sem("xs_cur_ready"), sem("xs_tr"), sem("xs_t_ready")
        chunk_in = [sem(f"chunk_in{c}") for c in range(6)]
        chunk_used = sem("chunk_used")
        gate_mm, up_mm, sig_ready, hid_ready, hid_tr, hid_t_ready, down_mm, y_ready, h_stored, rows_left, scattered = (
            sem(x) for x in ("gate_mm", "up_mm", "sig_ready", "hid_ready", "hid_tr", "hid_t_ready", "down_mm", "y_ready", "h_stored", "rows_left", "scattered"))
        sum_in, fin_g_in, fin_sq, fin_root, fin_ready, out_done = (sem(x) for x in ("sum_in", "fin_g_in", "fin_sq", "fin_root", "fin_ready", "out_done"))

        w_src = {"in": ins["w_in"][0], "mem_kv": ins["w_mem_kv"][0], "uq": ins["w_mla_uq"][0],
                 "ukv": ins["w_mla_ukv"][0], "o_na": ins["w_o_na"][0], "o_mla": ins["w_o_mla"][0],
                 "o_mem": ins["w_o_mem"][0], "out": ins["w_out"][0]}
        grid = "(r c) d -> c r d"
        x_dram = ins["x"][0].rearrange(grid, r=ROWS)
        out_dram = out[0].rearrange(grid, r=ROWS)
        wide = [("w_gate", 0), ("w_gate", 1), ("w_up", 0), ("w_up", 1), ("w_down", 0), ("w_down", 1)]

        def job_shape(j):
            return jobs[j][3], jobs[j][2]

        def w_view(t, j):
            kb, n = job_shape(j)
            return t[:, 0:kb * n].rearrange("p (k n) -> p k n", k=kb)

        def wait_read(eng, n):
            for b in range(3):
                eng.wait_ge(acc_free[b], (n - b + 2) // 3)

        def wait_acc_bank(eng, a):
            if a >= 3:
                eng.wait_ge(acc_free[a % 3], a // 3)

        def y_part(parts, br, g, hp):
            return parts[{"na": 0, "mla": 1, "mem": 2}[br], 2 * g + hp if br == "mem" else g]

        def probs_out(eng, ub, us, br, k, which):
            u = ub + k
            g, qb, hp = us[k]
            groups = us[-1][0] + 1
            ng = len(us) // groups
            gg = group_base[br] + g
            eng.wait_ge(t_done, u + 1)
            if k % ng < 2 and gg >= 2:
                pa = prev_group_acc[gg - 2]
                eng.wait_ge(acc_done, pa)
            buf = probs_t[gg % 2]
            cols = slice(P * qb, P * qb + P)
            if br == "mem":
                dst = buf[:, :, 0:2, cols]
                src = TR[u % 2][:].rearrange("p (a b n) -> p a b n", a=2, b=2)
            else:
                nk = width_of(br, qb) // P
                dst = buf[:, hp, 0:nk, cols]
                src = TR[u % 2][:, 0:nk * P].rearrange("p (b n) -> p b n", b=nk)
            if which == 0:
                eng.activation(dst, src, ACT.Copy).then_inc(pt_done[0], 1)
            else:
                eng.tensor_copy(dst, src).then_inc(pt_done[1], 1)

        prev_group_acc = []
        for br in ("na", "mem", "mla"):
            for g in range(2 if br == "mem" else 4):
                prev_group_acc.append(y_acc[br, g] + (2 if br == "mem" else 1))

        block = ctx.enter_context(nc.Block())

        @block.sync
        def _(sp):
            sp.dma_start(mem_tok[:], ins["mem"][0].rearrange("(m p) d -> p m d", p=P)).then_inc(mem_in, 16)
            for row, name, n in ((G_MIX, "g_mix", KB), (G_MEM, "g_mem", KB), (G_Q, "mla_q_norm", 3),
                                 (G_KV, "mla_kv_norm", 2), (G_FFN, "g_ffn", KB)):
                sp.dma_start(gain_rows[row:row + n, :], ins[name][0].rearrange("(k p) -> k p", p=P)).then_inc(gains_in, 16)
            for t in range(TB):
                sp.dma_start(x_tok[:, t, :], x_dram[COLS_PER_TILE * t:COLS_PER_TILE * (t + 1)]).then_inc(x_in, 16)
            sp.dma_start(half_col[:], ins["half_col"]).then_inc(half_in, 16)
            sp.dma_start(route_b[:], ins["b_router"].rearrange("a e -> e a")).then_inc(half_in, 16)

            def load_job(j):
                src, c0, n, kb = jobs[j]
                if j >= 2:
                    sp.wait_ge(w_lo_ready, j - 1)
                sp.dma_start(w_view(w_raw[j % 2], j),
                             w_src[src][:, c0:c0 + n].rearrange("(k p) n -> p k n", p=P)).then_inc(raw_in[j % 2], 16)

            load_job(0)
            load_job(1)
            sp.wait_ge(zeros_ready, 1)
            sp.dma_start(rpb_rows.rearrange("a b n -> (a b n)").rearrange("(p n) -> p n", p=P), junk[:, 0:RPB_BUF // P]).then_inc(rpb_zeroed, 16)
            sp.wait_ge(rpb_zeroed, 16)
            for r in range(ROWS):
                src = bass.AP(tensor=ins["na_rpb"].tensor, offset=(WIN_R - 1 - r) * RPB_C,
                              ap=[[RPB_R * RPB_C, NA_HEADS], [RPB_C, ROWS], [1, RPB_C]])
                sp.dma_start(rpb_rows[r, :, RPB_PAD:RPB_PAD + RPB_C].rearrange("(h k) n -> h k n", h=NA_HEADS), src).then_inc(rpb_in, 16)
            sp.wait_ge(rpb_in, 16 * ROWS)
            for c in range(COLS_PER_TILE):
                src = bass.AP(tensor=rpb_rows.tensor, offset=RPB_PAD - 1 - c,
                              ap=[[NA_HEADS * ROWS * RPB_PITCH, ROWS], [RPB_PITCH, NA_HEADS * ROWS], [1, TOEP_U]])
                sp.dma_start(toep[ROWS * c:ROWS * (c + 1)].rearrange("p h k u -> p (h k) u"), src).then_inc(toep_in, 16)
            out_job = next(j for j in range(n_jobs) if jobs[j][0] == "out")
            for j in range(2, n_jobs):
                if j == out_job + 2:
                    sp.wait_ge(acc_done, last_gate + 1)
                    for t in range(TB):
                        sp.dma_start(h_tok[:, t, :], x_dram[COLS_PER_TILE * t:COLS_PER_TILE * (t + 1)]).then_inc(resid_in, 16)
                    sp.dma_start(route_w[:], ins["w_router"][0].rearrange("(k p) e -> p k e", p=P)).then_inc(route_in, 16)
                load_job(j)

            def load_chunk(e, c):
                name, half = wide[c]
                src = ins[name][0, e, half * 512:(half + 1) * 512, :].rearrange("(k p) n -> p k n", p=P)
                sp.dma_start(expert_w[c][:], src).then_inc(chunk_in[c], 16)

            sp.wait_ge(acc_done, last_gate + 1)
            sp.wait_ge(merged_lo, KB)
            for c in range(5):
                load_chunk(0, c)
            sp.wait_ge(acc_done, n_acc)
            load_chunk(0, 5)
            wait_read(sp, n_acc)
            sp.dma_start(sum_rows.rearrange("(t p a) n -> p t (a n)", p=P, a=2), h_tok[:]).then_inc(h_stored, 16)
            sp.wait_ge(hr_ready, TB)
            sp.dma_start(hn_rows.rearrange("(t p) n -> p t n", p=P), hr_tok[:]).then_inc(hr_stored, 16)
            with sp.Fori(1, N_EXP) as e:
                for c in range(6):
                    if c % 2 == 0:
                        sp.wait_ge(chunk_used, 3 * (e - 1) + (c // 2 + 1))
                    else:
                        sp.wait_ge((gate_mm, up_mm, down_mm)[c // 2], e)
                    load_chunk(e, c)
            sp.dma_start(fin_g[:], ins["g_final"].partition_broadcast(P)).then_inc(fin_g_in, 16)
            sp.wait_ge(scattered, 16 * N_EXP)
            sp.dma_start(fin[:], sum_rows.rearrange("(t p a) n -> p t (a n)", p=P, a=2)).then_inc(sum_in, 16)
            for t in range(TB):
                sp.wait_ge(fin_ready, t + 1)
                sp.dma_start(out_dram[COLS_PER_TILE * t:COLS_PER_TILE * (t + 1)], fin[:, t, :]).then_inc(out_done, 16)
            sp.wait_ge(out_done, 16 * TB)

        @block.gpsimd
        def _(pool):
            pool.memset(junk[:, 0:RPB_BUF // P], 0.0).then_inc(zeros_ready, 1)
            pool.memset(ones[:], 1.0).then_inc(const_ready, 1)
            pool.memset(eps_col[:], EPS).then_inc(const_ready, 1)
            pool.memset(ident[:], 0.0).then_inc(pool_seq, 1)
            pool.wait_ge(pool_seq, 1)
            pool.affine_select(out=ident[:], in_=ident[:], compare_op=ALU.not_equal, fill=1.0, base=0,
                               pattern=[[-1, P]], channel_multiplier=1).then_inc(ident_ready, 1)
            pool.wait_ge(toep_in, 16 * COLS_PER_TILE)
            seq = 1
            for slot, dt, _, _ in SLOTS:
                u0 = COLS_PER_TILE * (dt + 1)
                pool.tensor_copy(table[:, :, slot, :].rearrange("p h (c r) -> p h c r", r=ROWS),
                                 toep[:, :, :, u0:u0 + COLS_PER_TILE].rearrange("p h r c -> p h c r")).then_inc(pool_seq, 1)
                seq += 1
            for slot, dt, lower, upper in SLOTS:
                part = table[:, :, slot, :].rearrange("p h (c r) -> p h c r", r=ROWS)
                for sign, on in ((1, lower), (-1, upper)):
                    if not on:
                        continue
                    pool.wait_ge(pool_seq, seq)
                    b = P * dt + ROWS * (WIN_C // 2) + ROWS - 1 if sign == 1 else -P * dt + ROWS * (WIN_C // 2 - 1)
                    pool.affine_select(out=part, in_=part, compare_op=ALU.is_ge, fill=MASKED, base=b,
                                       pattern=[[0, NA_HEADS], [sign * ROWS, COLS_PER_TILE], [0, ROWS]],
                                       channel_multiplier=-sign).then_inc(pool_seq, 1)
                    seq += 1
            pool.wait_ge(pool_seq, seq)
            pool.memset(stat[0:1, 60:61], 0.0).then_inc(table_ready, 1)
            pool.wait_ge(rope_ready, 1)
            pool.wait_ge(exp_done, unit_base["mla"])
            pool.wait_ge(acc_done, last_acc_use["mem"])
            for h in range(MLA_HEADS):
                pool.tensor_copy(k_mla[NOPE:MLA_QK, h, :], k_pe[NOPE:MLA_QK, :]).then_inc(kpe_spread, 1)
            pool.wait_ge(hr_stored, 16)
            pool.wait_ge(acc_done, n_acc)
            pool.wait_ge(slots_ready, 1)
            for j in range(PAIRS):
                pool.indirect_dma_start(out=xs_all[:, j, :], out_offset=None, in_=hn_rows[:, :],
                                        in_offset=bass.IndirectOffsetOnAxis(ap=slot_tok[:, j:j + 1], axis=0)).then_inc(xs_in, 16)
            pool.wait_ge(xs_in, 16 * PAIRS)
            pool.wait_ge(h_stored, 16)
            pool.tensor_copy(xs_cur[:], xs_all[:, 0, :]).then_inc(xs_cur_ready, 1)
            for j in range(PAIRS):
                pool.wait_ge(xs_tr, j + 1)
                pool.tensor_copy(xs_cur[:], xs_all[:, (j + 1) % PAIRS, :]).then_inc(xs_cur_ready, 1)
                for e in (2 * j, 2 * j + 1):
                    if e:
                        pool.wait_ge(scattered, 16 * e)
                    pool.memset(mark[:], 0.0).then_inc(rows_left, 1)
                    pool.wait_ge(y_ready, e + 1)
                    pool.indirect_dma_start(out=sum_rows[:, :], out_offset=bass.IndirectOffsetOnAxis(ap=slot_row[:, e:e + 1], axis=0),
                                            in_=y_sb[:], in_offset=None, compute_op=ALU.add).then_inc(scattered, 16)

        @block.scalar
        def _(act):
            def split_hi(j):
                act.wait_ge(raw_in[j % 2], 16 * (j // 2 + 1))
                if j >= 2:
                    act.wait_ge(acc_done, job_end[j - 2])
                kb, n = job_shape(j)
                act.activation(w_hi[j % 2][:, 0:kb * n], w_raw[j % 2][:, 0:kb * n], ACT.Copy).then_inc(w_hi_ready, 1)

            act.wait_ge(mem_in, 16)
            act.wait_ge(rpb_zeroed, 16)
            for m in range(MB):
                act.activation(junk[:], mem_tok[:, m, :], ACT.Square, accum_out=stat[:, m:m + 1]).then_inc(sumsq_done, 1)
                act.wait_ge(sumsq_done, m + 1)
            act.wait_ge(x_in, 16 * TB)
            for t in range(TB):
                act.activation(junk[:], x_tok[:, t, :], ACT.Square, accum_out=stat[:, MB + t:MB + t + 1]).then_inc(sumsq_done, 1)
                act.wait_ge(sumsq_done, MB + t + 1)
            act.wait_ge(const_ready, 2)
            act.activation(stat[:, 8:8 + MB + TB], stat[:, 0:MB + TB], ACT.Sqrt, scale=1.0 / D, bias=eps_col[:]).then_inc(root_done, 1)
            split_hi(0)
            split_hi(1)
            n_hi = n_copy = n_sq = n_gate = 0
            n_units = 0
            for n, st in enumerate(steps):
                if st[0] == "end":
                    if st[1] + 2 < n_jobs:
                        split_hi(st[1] + 2)
                    continue
                if st[0] == "latent":
                    act.wait_ge(max_done, unit_base["na"] + len(units_of("na")))
                    act.dma_start(rope_cs[NOPE:MLA_QK, 0, :], ins["rope_cos"]).then_inc(rope_in, 16)
                    act.dma_start(rope_cs[NOPE:MLA_QK, 1, :], ins["rope_sin"]).then_inc(rope_in, 16)
                    act.wait_ge(latent_ready, 5)
                    act.wait_ge(acc_done, last_acc_use["mem"])
                    for i in range(5):
                        dst, src = (cq_hi[:, i, :], c_q[:, i, :]) if i < 3 else (ckv_hi[:, i - 3, :], c_kv[:, i - 3, :])
                        act.activation(dst, src, ACT.Copy).then_inc(latent_hi, 1)
                    continue
                if st[0] == "attn":
                    br = st[1]
                    us, ub = units_of(br), unit_base[br]
                    groups = us[-1][0] + 1
                    ng = len(us) // groups
                    for i in range(len(us) + 3):
                        u = ub + i
                        if i < len(us):
                            act.wait_ge(max_done, u + 1)
                            if u >= 3:
                                act.wait_ge(t_done, u - 2)
                            w = width_of(br, us[i][1])
                            src = probs[u % 3] if br == "na" else SC[u % 3]
                            if br == "mem":
                                for hp in range(2):
                                    part = slice(256 * hp, 256 * hp + 256)
                                    last = act.activation(probs[u % 3][:, part], src[:, part], ACT.Exp, bias=soft_m[:, u % 4, hp:hp + 1],
                                                          accum_out=soft_s[:, u % 4, hp:hp + 1])
                                last.then_inc(exp_done, 1)
                            else:
                                act.activation(probs[u % 3][:, 0:w], src[:, 0:w], ACT.Exp, bias=soft_m[:, u % 4, 0:1],
                                               accum_out=soft_s[:, u % 4, 0:1]).then_inc(exp_done, 1)
                        k = i - 2
                        if 0 <= k < len(us) and (ub + k) % 2 == 0:
                            probs_out(act, ub, us, br, k, 0)
                        g, r = divmod(i - 2, ng)
                        if r == 0 and g >= 1:
                            for hp in range(2 if br == "mem" else 1):
                                a = y_acc[br, g - 1] + hp
                                act.wait_ge(acc_done, a + 1)
                                act.activation(y_part(y_hi, br, g - 1, hp)[:], ACC[a % 3][:], ACT.Copy).then_inc(hi_done, 1)
                                n_hi += 1
                    continue
                kind, args = st[1], st[2]
                a = acc_of[n]
                ps = ACC[a % 3]
                if kind in ("uk", "vmla") and args == (0,):
                    act.wait_ge(acc_done, last_acc_use["mem"])
                act.wait_ge(acc_done, a + 1)
                if kind in ("memT", "nT"):
                    kb, = args
                    act.wait_ge(gain_ready, 1)
                    if kind == "memT":
                        act.activation(memt_hi[:, kb, :], ps[:, 0:N_MEM], ACT.Copy, scale=gain_t[:, G_MEM + kb:G_MEM + kb + 1]).then_inc(hi_done, 1)
                    else:
                        act.activation(nt_hi[:, kb, :], ps[:], ACT.Copy, scale=gain_t[:, G_MIX + kb:G_MIX + kb + 1]).then_inc(hi_done, 1)
                    n_hi += 1
                elif kind == "kmem":
                    act.activation(k_mem[:, args[0], :], ps[:, 0:N_MEM], ACT.Copy).then_inc(acc_free[a % 3], 1)
                elif kind == "vmem":
                    m, c = args
                    act.activation(v_mem[:, m, 256 * c:256 * c + 256], ps[:, 0:256], ACT.Copy).then_inc(acc_free[a % 3], 1)
                elif kind == "qna":
                    act.wait_ge(table_ready, 1)
                    act.activation(q_na[:, args[0], :], ps[:], ACT.Copy, scale=NA_DIM ** -0.5).then_inc(acc_free[a % 3], 1)
                elif kind == "kna":
                    act.activation(k_na[:, args[0], :], ps[:], ACT.Copy).then_inc(acc_free[a % 3], 1)
                elif kind == "vna":
                    t, c = args
                    act.activation(v_na[:, t, 256 * c:256 * c + 256], ps[:, 0:256], ACT.Copy).then_inc(acc_free[a % 3], 1)
                elif kind == "qmem":
                    act.activation(q_mem[:, args[0], :], ps[:], ACT.Copy, scale=MEM_DIM ** -0.5).then_inc(acc_free[a % 3], 1)
                elif kind in ("cq", "ckv"):
                    i = args[0]
                    if kind == "ckv":
                        act.wait_ge(acc_done, acc_at["ssq", "q"] + 1)
                    act.activation(square[i][:], ps[:], ACT.Square).then_inc(sq_ready, 1)
                    dst = c_q if kind == "cq" else c_kv
                    act.activation(dst[:, i, :], ps[:], ACT.Copy).then_inc(acc_free[a % 3], 1)
                elif kind == "ssq":
                    width = Q_RANK if args[0] == "q" else KV_RANK
                    if args[0] == "kv":
                        act.wait_ge(latent_ready, 3)
                    act.activation(rms_root[:], ps[:], ACT.Sqrt, scale=1.0 / width, bias=eps_col[:]).then_inc(acc_free[a % 3], 1)
                elif kind == "kpe":
                    act.activation(k_pe[NOPE:MLA_QK, :], ps[NOPE:MLA_QK, :], ACT.Copy, scale=MLA_QK ** -0.5).then_inc(acc_free[a % 3], 1)
                elif kind == "uq":
                    act.activation(q_mla[0:NOPE, args[0], :], ps[0:NOPE, :], ACT.Copy).then_inc(hi_done, 1)
                    n_hi += 1
                elif kind == "uk":
                    act.activation(k_mla[0:NOPE, args[0], :], ps[0:NOPE, :], ACT.Copy, scale=MLA_QK ** -0.5).then_inc(acc_free[a % 3], 1)
                elif kind == "vmla":
                    act.activation(v_mla[:, args[0], :], ps[:], ACT.Copy).then_inc(acc_free[a % 3], 1)
                elif kind == "o":
                    i = args[1]
                    if n_copy >= 4:
                        act.wait_ge(gate_used, n_copy - 3)
                    act.activation(branch_o[i][:], ps[:], ACT.Copy).then_inc(acc_free[a % 3], 1)
                    n_copy += 1
                elif kind == "gate":
                    if n_gate >= 2:
                        act.wait_ge(gate_used, n_gate - 1)
                    act.activation(gate_s[n_gate % 2][:], ps[:], ACT.Sigmoid).then_inc(acc_free[a % 3], 1)
                    n_gate += 1
                    br_n, d, _ = args
                    if br_n == 2:
                        act.wait_ge(merged_lo, d)
                        act.wait_ge(gate_used, n_gate)
                        act.activation(m_hi[:, d, :], merged[:, d, :], ACT.Copy).then_inc(merged_hi, 1)
            wait_read(act, n_acc)
            for t in range(TB):
                act.activation(junk_b[:], h_tok[:, t, :], ACT.Square, accum_out=stat[:, 16 + t:17 + t]).then_inc(hsq_done, 1)
                act.wait_ge(hsq_done, t + 1)
            act.activation(stat[:, 20:20 + TB], stat[:, 16:16 + TB], ACT.Sqrt, scale=1.0 / D, bias=eps_col[:]).then_inc(hroot_done, 1)
            for kb in range(KB):
                act.wait_ge(hnt_ps, kb + 1)
                act.activation(hn_t[:, kb, :], TR[kb % 2][:], ACT.Copy, scale=gain_t[:, G_FFN + kb:G_FFN + kb + 1]).then_inc(hnt_ready, 1)
            act.wait_ge(soft_in, 1)
            act.activation(aff[:], aff[:], ACT.Exp).then_inc(soft_exp, 1)
            with act.Fori(0, N_EXP) as e:
                act.wait_ge(gate_mm, e + 1)
                act.activation(silu_s[:], bank[0][:], ACT.Sigmoid).then_inc(sig_ready, 1)
                act.wait_ge(hid_tr, e + 1)
                act.activation(hidden_t[:], bank[5][:].rearrange("p (c n) -> p c n", c=4), ACT.Copy).then_inc(hid_t_ready, 1)
            act.wait_ge(sum_in, 16)
            for t in range(TB):
                act.activation(junk_b[:], fin[:, t, :], ACT.Square, accum_out=stat[:, 32 + t:33 + t]).then_inc(fin_sq, 1)
                act.wait_ge(fin_sq, t + 1)
            act.activation(stat[:, 36:36 + TB], stat[:, 32:32 + TB], ACT.Sqrt, scale=1.0 / D, bias=eps_col[:]).then_inc(fin_root, 1)

        @block.tensor
        def _(pe):
            pe.wait_ge(gains_in, 80)
            pe.wait_ge(ident_ready, 1)
            pe.transpose(TR[0][:, 0:GAIN_ROWS], gain_rows[:], ident[0:GAIN_ROWS, 0:GAIN_ROWS]).then_inc(gain_ps, 1)

            def passes(n_k, ps, lhs, rhs, done=None):
                for k in range(n_k):
                    (l_hi, l_lo), (r_hi, r_lo) = lhs(k), rhs(k)
                    pe.matmul(ps, l_hi, r_hi, start=(k == 0), stop=False)
                    pe.matmul(ps, l_hi, r_lo, start=False, stop=False)
                    last = pe.matmul(ps, l_lo, r_hi, start=False, stop=(k == n_k - 1))
                last.then_inc(acc_done, 1)

            def attention(br):
                us, ub = units_of(br), unit_base[br]
                groups = us[-1][0] + 1
                ng = len(us) // groups

                def scores(i):
                    u = ub + i
                    g, qb, hp = us[i]
                    if u >= 3:
                        pe.wait_ge(exp_done, u - 2)
                    rows = slice(P * qb, P * qb + P)
                    if br == "na":
                        kts = key_tiles(qb)
                        part = slice(NA_DIM * hp, NA_DIM * hp + NA_DIM)
                        pe.matmul(SC[u % 3][:, 0:P * len(kts)], q_na[part, g, rows], k_na[part, g, P * kts[0]:P * (kts[-1] + 1)],
                                  start=True, stop=True).then_inc(score_done, 1)
                    elif br == "mem":
                        for h in range(2):
                            last = pe.matmul(SC[u % 3][:, 256 * h:256 * h + 256], q_mem[:, 2 * g + h, rows], k_mem[:, 2 * g + h, :],
                                             start=True, stop=True)
                        last.then_inc(score_done, 1)
                    else:
                        pe.matmul(SC[u % 3][:], q_mla[:, 2 * g + hp, rows], k_mla[:, 2 * g + hp, :],
                                  start=True, stop=True).then_inc(score_done, 1)

                def turn(i):
                    u = ub + i
                    pe.wait_ge(p_ready, u + 1)
                    if u >= 2:
                        pe.wait_ge(pt_done[u % 2], (u - 2) // 2 + 1)
                    nk = width_of(br, us[i][1]) // P
                    for j in range(nk):
                        last = pe.transpose(TR[u % 2][:, P * j:P * j + P], probs[u % 3][:, P * j:P * j + P], ident[:])
                    last.then_inc(t_done, 1)

                def values(g):
                    u_end = ub + ng * (g + 1)
                    pe.wait_ge(pt_done[0], (u_end + 1) // 2)
                    pe.wait_ge(pt_done[1], u_end // 2)
                    buf = probs_t[(group_base[br] + g) % 2]
                    a = y_acc[br, g]
                    if br == "mem":
                        for hp in range(2):
                            wait_acc_bank(pe, a + hp)
                            for m in range(MB):
                                last = pe.matmul(ACC[(a + hp) % 3][:], v_mem[:, m, P * (2 * g + hp):P * (2 * g + hp) + P], buf[:, hp, m, :],
                                                 start=(m == 0), stop=(m == MB - 1))
                            last.then_inc(acc_done, 1)
                        return
                    wait_acc_bank(pe, a)
                    ps = ACC[a % 3]
                    v = v_na if br == "na" else v_mla
                    for qb in (range(TB) if br == "na" else [None]):
                        kts = range(TB) if qb is None else key_tiles(qb)
                        cols = slice(0, S) if qb is None else slice(P * qb, P * qb + P)
                        for j, kt in enumerate(kts):
                            for hp in range(2):
                                c0 = P * g + 64 * hp
                                last = pe.matmul(ps[64 * hp:64 * hp + 64, cols], v[:, kt, c0:c0 + 64], buf[:, hp, j, cols],
                                                 start=(j == 0), stop=(j == len(kts) - 1))
                    last.then_inc(acc_done, 1)

                scores(0)
                scores(1)
                for i in range(len(us)):
                    if i + 2 < len(us):
                        scores(i + 2)
                    turn(i)
                    if i % ng == 0 and i > 0:
                        values(i // ng - 1)
                values(groups - 1)

            for n, st in enumerate(steps):
                if st[0] in ("end", "latent"):
                    continue
                if st[0] == "attn":
                    if st[1] == "na":
                        wait_read(pe, y_acc["na", 0])
                        pe.wait_ge(table_ready, 1)
                    if st[1] == "mla":
                        wait_read(pe, y_acc["mla", 0])
                        pe.wait_ge(kpe_spread, MLA_HEADS)
                    attention(st[1])
                    continue
                kind, args, j = st[1:]
                a = acc_of[n]
                ps = ACC[a % 3]
                wait_acc_bank(pe, a)
                if j is not None:
                    pe.wait_ge(w_lo_ready, j + 1)
                    wh, wl = w_view(w_hi[j % 2], j), w_view(w_lo[j % 2], j)

                def w_cols(c0, c):
                    return lambda k: (wh[:, k, c0:c0 + c], wl[:, k, c0:c0 + c])

                if kind in ("memT", "nT"):
                    kb, = args
                    tok, cnt = (mem_tok, MB) if kind == "memT" else (x_tok, TB)
                    pe.wait_ge(xn_ready, MB if kind == "memT" else MB + TB)
                    for t in range(cnt):
                        last = pe.transpose(ps[:, P * t:P * t + P], tok[:, t, P * kb:P * kb + P], ident[:])
                    last.then_inc(acc_done, 1)
                    continue
                if kind == "ssq":
                    cnt = 3 if args[0] == "q" else 2
                    pe.wait_ge(sq_ready, 3 if args[0] == "q" else 5)
                    for i in range(cnt):
                        last = pe.matmul(ps[:], ones[:], square[i][:], start=(i == 0), stop=(i == cnt - 1))
                    last.then_inc(acc_done, 1)
                    continue
                nt = lambda k: (nt_hi[:, k, :], nt_lo[:, k, :])
                if (kind, args) == ("kmem", (0, 0)):
                    wait_read(pe, 2 * KB)
                if kind == "kmem":
                    passes(KB, ps[:, 0:N_MEM], w_cols(P * args[1], P), lambda k: (memt_hi[:, k, :], memt_lo[:, k, :]))
                elif kind == "vmem":
                    m = args[0]
                    passes(KB, ps[:, 0:256], lambda k: (memt_hi[:, k, P * m:P * m + P], memt_lo[:, k, P * m:P * m + P]), w_cols(0, 256))
                elif kind in ("qna", "kna", "cq", "ckv", "qmem"):
                    passes(KB, ps[:], w_cols(P * args[1], P), nt)
                elif kind == "gate":
                    passes(KB, ps[:], w_cols(P * args[2], P), nt)
                elif kind == "kpe":
                    passes(KB, ps[0:MLA_QK, :], w_cols(0, MLA_QK), nt)
                elif kind == "vna":
                    t = args[0]
                    passes(KB, ps[:, 0:256], lambda k: (nt_hi[:, k, P * t:P * t + P], nt_lo[:, k, P * t:P * t + P]), w_cols(0, 256))
                elif kind == "uq":
                    pe.wait_ge(latent_ready, 10)
                    passes(3, ps[0:MLA_QK, :], w_cols(MLA_QK * args[1], MLA_QK), lambda k: (cq_hi[:, k, :], cq_lo[:, k, :]))
                elif kind == "uk":
                    passes(2, ps[0:NOPE, :], w_cols((NOPE + MLA_V) * args[0], NOPE), lambda k: (ckv_hi[:, k, :], ckv_lo[:, k, :]))
                elif kind == "vmla":
                    t = args[0]
                    vh = wh.rearrange("p k (h c) -> p k h c", h=MLA_HEADS)[:, :, :, NOPE:NOPE + MLA_V]
                    vl = wl.rearrange("p k (h c) -> p k h c", h=MLA_HEADS)[:, :, :, NOPE:NOPE + MLA_V]
                    passes(2, ps[:], lambda k: (ckv_hi[:, k, P * t:P * t + P], ckv_lo[:, k, P * t:P * t + P]),
                           lambda k: (vh[:, k], vl[:, k]))
                elif kind == "o":
                    br, i = args
                    passes(4, ps[:], w_cols(P * i, P), lambda k: (y_hi[br, k][:], y_lo[br, k][:]))
                elif kind == "out":
                    t = args[0]
                    pe.wait_ge(merged_lo, KB)
                    passes(KB, ps[:, 0:256], lambda k: (m_hi[:, k, P * t:P * t + P], m_lo[:, k, P * t:P * t + P]), w_cols(0, 256))
            pe.wait_ge(hr_ready, TB)
            for kb in range(KB):
                if kb >= 2:
                    pe.wait_ge(hnt_ready, kb - 1)
                for t in range(TB):
                    last = pe.transpose(TR[kb % 2][:, P * t:P * t + P], hr_tok[:, t, P * kb:P * kb + P], ident[:])
                last.then_inc(hnt_ps, 1)
            pe.wait_ge(hnt_ready, KB)
            pe.wait_ge(route_in, 16)
            for kb in range(KB):
                last = pe.matmul(bank[0][0:N_EXP, :], route_w[:, kb, :], hn_t[:, kb, :], start=(kb == 0), stop=(kb == KB - 1))
            last.then_inc(logit_ps, 1)
            pe.wait_ge(logit_ready, 1)
            for t in range(TB):
                last = pe.transpose(bank[1][:, N_EXP * t:N_EXP * t + N_EXP], logit_t[:, P * t:P * t + P], ident[0:N_EXP, 0:N_EXP])
            last.then_inc(logit_tok, 1)
            pe.wait_ge(aff_ready, 1)
            for t in range(TB):
                last = pe.transpose(bank[2][0:N_EXP, P * t:P * t + P], aff[:, t, :], ident[:])
            last.then_inc(aff_ps, 1)
            pe.wait_ge(top_ready, 2)
            pe.transpose(bank[3][:, 0:N_EXP], top_v[:], ident[0:N_EXP, 0:N_EXP])
            pe.transpose(bank[3][:, N_EXP:2 * N_EXP], top_f[:], ident[0:N_EXP, 0:N_EXP]).then_inc(top_ps, 1)

            def turn_rows():
                for kb in range(KB):
                    last = pe.transpose(bank[6 + kb // 4][:, P * (kb % 4):P * (kb % 4) + P], xs_cur[:, P * kb:P * kb + P], ident[:])
                last.then_inc(xs_tr, 1)

            pe.wait_ge(xs_cur_ready, 1)
            turn_rows()
            with pe.Fori(0, PAIRS) as j:
                pe.wait_ge(xs_t_ready, j + 1)
                for i in range(2):
                    e = 2 * j + i
                    rows = slice(CAP * i, CAP * i + CAP)
                    for m in range(2):
                        for c in range(2):
                            pe.wait_ge(chunk_in[2 * m + c], 16 * (e + 1))
                            for k in range(4):
                                for hf in range(2):
                                    last = pe.matmul(bank[m][CAP * hf:CAP * hf + CAP, :], xs_t[:, 4 * c + k, rows],
                                                     expert_w[2 * m + c][:, k, 512 * hf:512 * hf + 512],
                                                     start=(c == 0 and k == 0), stop=(c == 1 and k == 3))
                            if c == 0:
                                last.then_inc(chunk_used, 1)
                        last.then_inc((gate_mm, up_mm)[m], 1)
                    if i == 0:
                        pe.wait_ge(xs_cur_ready, j + 2)
                        turn_rows()
                    pe.wait_ge(hid_ready, e + 1)
                    for c in range(4):
                        last = pe.transpose(bank[5][:, P * c:P * c + P], hidden[:, P * c:P * c + P], ident[:])
                    last.then_inc(hid_tr, 1)
                    pe.wait_ge(hid_t_ready, e + 1)
                    for c in range(2):
                        pe.wait_ge(chunk_in[4 + c], 16 * (e + 1))
                        for k in range(4):
                            for hf in range(2):
                                last = pe.matmul(bank[4][CAP * hf:CAP * hf + CAP, :], hidden_t[:, k, CAP * c:CAP * c + CAP],
                                                 expert_w[4 + c][:, k, 512 * hf:512 * hf + 512],
                                                 start=(c == 0 and k == 0), stop=(c == 1 and k == 3))
                        if c == 0:
                            last.then_inc(chunk_used, 1)
                    last.then_inc(down_mm, 1)

        @block.vector
        def _(dve):
            chain = [0]

            def link(ins_):
                chain[0] += 1
                ins_.then_inc(dve_seq, 1)
                dve.wait_ge(dve_seq, chain[0])

            def split_lo(j):
                dve.wait_ge(w_hi_ready, j + 1)
                kb, n = job_shape(j)
                dve.tensor_tensor(w_lo[j % 2][:, 0:kb * n], w_raw[j % 2][:, 0:kb * n],
                                  w_hi[j % 2][:, 0:kb * n].bitcast(F32), ALU.subtract).then_inc(w_lo_ready, 1)

            def inverse(r):
                link(dve.reciprocal(r, r))

            dve.wait_ge(gain_ps, 1)
            dve.tensor_copy(gain_t[:, 0:GAIN_ROWS], TR[0][:, 0:GAIN_ROWS]).then_inc(gain_ready, 1)
            dve.wait_ge(root_done, 1)
            inverse(stat[:, 8:8 + MB + TB])
            for i in range(MB + TB):
                row = mem_tok[:, i, :] if i < MB else x_tok[:, i - MB, :]
                dve.tensor_scalar(row, row, stat[:, 8 + i:9 + i], None, ALU.mult).then_inc(xn_ready, 1)
            dve.wait_ge(gain_ready, 1)
            split_lo(0)
            split_lo(1)
            n_hi = n_gate = 0

            def minus_hi(dst, ps, hi):
                return dve.tensor_tensor(dst, ps, hi.bitcast(F32), ALU.subtract)

            def latents(c, n, g0):
                a = acc_at["ssq", "q" if c is c_q else "kv"]
                dve.wait_ge(acc_free[a % 3], a // 3 + 1)
                link(dve.reciprocal(rms_inv[:], rms_root[:]))
                for i in range(n):
                    dve.scalar_tensor_tensor(c[:, i, :], c[:, i, :], gain_t[:, g0 + i:g0 + i + 1], rms_inv[:],
                                             ALU.mult, ALU.mult).then_inc(latent_ready, 1)

            def rotate(dst, src, cos, sin):
                swap = [16 * (q // 16) + (q % 16 + 8) % 16 for q in range(32)]
                rows = slice(NOPE, MLA_QK)
                link(dve.stream_shuffle(rope_b[rows, :], src, swap))
                link(dve.tensor_tensor(rope_b[rows, :], rope_b[rows, :], sin, ALU.mult))
                link(dve.tensor_tensor(rope_a[rows, :], src, cos, ALU.mult))
                return dve.tensor_tensor(dst, rope_a[rows, :], rope_b[rows, :], ALU.add)

            for n, st in enumerate(steps):
                if st[0] == "end":
                    if st[1] + 2 < n_jobs:
                        split_lo(st[1] + 2)
                    continue
                if st[0] == "latent":
                    for i in range(5):
                        dve.wait_ge(latent_hi, i + 1)
                        dst, hi, src = ((cq_lo, cq_hi, c_q), (ckv_lo, ckv_hi, c_kv))[i // 3]
                        k = i % 3
                        dve.tensor_tensor(dst[:, k, :], src[:, k, :], hi[:, k, :].bitcast(F32), ALU.subtract).then_inc(latent_ready, 1)
                    dve.wait_ge(rope_in, 32)
                    dve.wait_ge(acc_free[acc_at["kpe",] % 3], acc_at["kpe",] // 3 + 1)
                    rotate(k_pe[NOPE:MLA_QK, :], k_pe[NOPE:MLA_QK, :], rope_cs[NOPE:MLA_QK, 0, :], rope_cs[NOPE:MLA_QK, 1, :]).then_inc(rope_ready, 1)
                    dve.wait_ge(rope_ready, 1)
                    continue
                if st[0] == "attn":
                    br = st[1]
                    us, ub = units_of(br), unit_base[br]
                    groups = us[-1][0] + 1
                    ng = len(us) // groups
                    for i in range(len(us) + 3):
                        u = ub + i
                        if i < len(us):
                            g, qb, hp = us[i]
                            dve.wait_ge(score_done, u + 1)
                            m = soft_m[:, u % 4, :]
                            if br == "na":
                                if u >= 3:
                                    dve.wait_ge(t_done, u - 2)
                                else:
                                    dve.wait_ge(acc_done, acc_at["ssq", "kv"] + 1)
                                s0, ds, ns = table_slots(qb)
                                w = P * ns
                                bias = table[:, 2 * g + hp, s0:s0 + ds * (ns - 1) + 1:ds, :]
                                link(dve.tensor_tensor(probs[u % 3][:, 0:w].rearrange("p (a b) -> p a b", a=ns),
                                                       SC[u % 3][:, 0:w].rearrange("p (a b) -> p a b", a=ns), bias, ALU.add))
                                dve.tensor_reduce(m[:, 0:1], probs[u % 3][:, 0:w], AX.X, ALU.max, negate=True).then_inc(max_done, 1)
                            elif br == "mem":
                                dve.tensor_reduce(m, SC[u % 3][:].rearrange("p (a b) -> p a b", a=2), AX.X, ALU.max, negate=True).then_inc(max_done, 1)
                            else:
                                dve.tensor_reduce(m[:, 0:1], SC[u % 3][:], AX.X, ALU.max, negate=True).then_inc(max_done, 1)
                        k = i - 1
                        if 0 <= k < len(us):
                            v = ub + k
                            dve.wait_ge(exp_done, v + 1)
                            w = width_of(br, us[k][1])
                            nh = 2 if br == "mem" else 1
                            link(dve.reciprocal(soft_r[:, v % 4, 0:nh], soft_s[:, v % 4, 0:nh]))
                            for hp in range(nh):
                                part = slice(256 * hp, 256 * hp + 256) if nh == 2 else slice(0, w)
                                last = dve.tensor_scalar(probs[v % 3][:, part], probs[v % 3][:, part], soft_r[:, v % 4, hp:hp + 1], None, ALU.mult)
                            last.then_inc(p_ready, 1)
                        k = i - 2
                        if 0 <= k < len(us) and (ub + k) % 2 == 1:
                            probs_out(dve, ub, us, br, k, 1)
                        g, r = divmod(i - 2, ng)
                        if r == 0 and g >= 1:
                            for hp in range(2 if br == "mem" else 1):
                                a = y_acc[br, g - 1] + hp
                                n_hi += 1
                                dve.wait_ge(hi_done, n_hi)
                                minus_hi(y_part(y_lo, br, g - 1, hp)[:], ACC[a % 3][:], y_part(y_hi, br, g - 1, hp)[:]).then_inc(acc_free[a % 3], 1)
                    continue
                kind, args = st[1], st[2]
                a = acc_of[n]
                ps = ACC[a % 3]
                if kind in ("memT", "nT"):
                    kb, = args
                    n_hi += 1
                    dve.wait_ge(hi_done, n_hi)
                    if kind == "memT":
                        dst, src, hi, g0 = memt_lo[:, kb, :], ps[:, 0:N_MEM], memt_hi[:, kb, :], G_MEM
                    else:
                        dst, src, hi, g0 = nt_lo[:, kb, :], ps[:], nt_hi[:, kb, :], G_MIX
                    dve.scalar_tensor_tensor(dst, src, gain_t[:, g0 + kb:g0 + kb + 1], hi.bitcast(F32),
                                             ALU.mult, ALU.subtract).then_inc(acc_free[a % 3], 1)
                elif kind == "ssq":
                    if args[0] == "q":
                        latents(c_q, 3, G_Q)
                    else:
                        latents(c_kv, 2, G_KV)
                elif kind == "uq":
                    n_hi += 1
                    dve.wait_ge(hi_done, n_hi)
                    rotate(q_mla[NOPE:MLA_QK, args[0], :], ps[NOPE:MLA_QK, :], rope_cs[NOPE:MLA_QK, 0, :],
                           rope_cs[NOPE:MLA_QK, 1, :]).then_inc(acc_free[a % 3], 1)
                    dve.wait_ge(acc_free[a % 3], a // 3 + 1)
                elif kind == "gate":
                    br_n, d, _ = args
                    i = n_gate % 4
                    dve.wait_ge(acc_free[a % 3], a // 3 + 1)
                    if br_n == 0:
                        dve.tensor_tensor(merged[:, d, :], branch_o[i][:], gate_s[n_gate % 2][:], ALU.mult).then_inc(gate_used, 1)
                    else:
                        link(dve.tensor_tensor(branch_o[i][:], branch_o[i][:], gate_s[n_gate % 2][:], ALU.mult))
                        dve.tensor_tensor(merged[:, d, :], merged[:, d, :], branch_o[i][:], ALU.add).then_inc(gate_used, 1)
                    n_gate += 1
                    dve.wait_ge(gate_used, n_gate)
                    if br_n == 2:
                        dve.wait_ge(merged_hi, d + 1)
                        dve.tensor_tensor(m_lo[:, d, :], merged[:, d, :], m_hi[:, d, :].bitcast(F32), ALU.subtract).then_inc(merged_lo, 1)
                elif kind == "out":
                    t, c = args
                    dve.wait_ge(acc_done, a + 1)
                    dve.wait_ge(resid_in, 16 * TB)
                    cols = slice(256 * c, 256 * c + 256)
                    dve.tensor_tensor(h_tok[:, t, cols], ps[:, 0:256], h_tok[:, t, cols], ALU.add).then_inc(acc_free[a % 3], 1)
            dve.wait_ge(hroot_done, 1)
            inverse(stat[:, 20:20 + TB])
            for t in range(TB):
                dve.tensor_scalar(hr_tok[:, t, :], h_tok[:, t, :], stat[:, 20 + t:21 + t], None, ALU.mult).then_inc(hr_ready, 1)
            dve.wait_ge(logit_ps, 1)
            dve.wait_ge(half_in, 32)
            dve.tensor_scalar(logit_t[:], bank[0][0:N_EXP, :], route_b[:, 0:1], None, ALU.add).then_inc(logit_ready, 1)
            dve.wait_ge(logit_tok, 1)
            rows = bank[1][:, 0:TB * N_EXP].rearrange("p (t e) -> p t e", e=N_EXP)
            link(dve.tensor_reduce(row_stat[:, 0, :], rows, AX.X, ALU.max))
            dve.tensor_tensor(aff[:], rows, row_stat[:, 0, :].unsqueeze(2).broadcast_to([P, TB, N_EXP]), ALU.subtract).then_inc(soft_in, 1)
            dve.wait_ge(soft_exp, 1)
            link(dve.tensor_reduce(row_stat[:, 1, :], aff[:], AX.X, ALU.add))
            link(dve.reciprocal(row_stat[:, 2, :], row_stat[:, 1, :]))
            dve.tensor_tensor(aff[:], aff[:], row_stat[:, 2, :].unsqueeze(2).broadcast_to([P, TB, N_EXP]), ALU.mult).then_inc(aff_ready, 1)
            dve.wait_ge(aff_ps, 1)
            link(dve.tensor_copy(aff_t[:], bank[2][0:N_EXP, :]))
            for r in range(CAP // 8):
                v8, i8 = top_v[:, 8 * r:8 * r + 8], top_i[:, 8 * r:8 * r + 8]
                link(dve.max(v8, aff_t[:]))
                link(dve.max_index(i8, v8, aff_t[:]))
                link(dve.match_replace(aff_t[:], v8, aff_t[:], -1.0))
            for r in range(2):
                last = dve.tensor_copy(top_f[:, CAP * r:CAP * r + CAP], top_i[:])
            last.then_inc(top_ready, 1)
            dve.tensor_copy(top_v[:, CAP:2 * CAP], top_v[:, 0:CAP]).then_inc(top_ready, 1)
            dve.wait_ge(top_ps, 1)
            dve.tensor_copy(slot_gain[:], bank[3][:, 0:N_EXP])
            dve.tensor_scalar(slot_row[:], bank[3][:, N_EXP:2 * N_EXP], 2.0, half_col[:], ALU.mult, ALU.add)
            for i in range(2):
                last = dve.tensor_copy(slot_tok[CAP * i:CAP * i + CAP, :], bank[3][CAP * i:CAP * i + CAP, N_EXP + i:2 * N_EXP:2])
            last.then_inc(slots_ready, 1)

            def gained_rows():
                for b in range(2):
                    g4 = gain_t[:, G_FFN + 4 * b:G_FFN + 4 * b + 4].unsqueeze(2).broadcast_to([P, 4, P])
                    last = dve.tensor_tensor(xs_t[:, 4 * b:4 * b + 4, :], bank[6 + b][:].rearrange("p (k n) -> p k n", k=4), g4, ALU.mult)
                last.then_inc(xs_t_ready, 1)

            dve.wait_ge(xs_tr, 1)
            gained_rows()
            with dve.Fori(0, PAIRS) as j:
                for i in range(2):
                    e = 2 * j + i
                    dve.wait_ge(sig_ready, e + 1)
                    dve.tensor_tensor(hidden[:], silu_s[:], bank[0][:], ALU.mult).then_inc(silu_ready, 1)
                    dve.wait_ge(silu_ready, e + 1)
                    dve.wait_ge(up_mm, e + 1)
                    dve.tensor_tensor(hidden[:], hidden[:], bank[1][:], ALU.mult).then_inc(hid_ready, 1)
                    if i == 1:
                        dve.wait_ge(xs_tr, j + 2)
                        gained_rows()
                    dve.wait_ge(down_mm, e + 1)
                    dve.wait_ge(rows_left, e + 1)
                    dve.tensor_scalar(y_sb[:], bank[4][:], slot_gain[:, bass.ds(e, 1)], None, ALU.mult).then_inc(y_ready, 1)
            dve.wait_ge(fin_root, 1)
            inverse(stat[:, 36:36 + TB])
            dve.wait_ge(fin_g_in, 16)
            for t in range(TB):
                dve.scalar_tensor_tensor(fin[:, t, :], fin[:, t, :], stat[:, 36 + t:37 + t], fin_g[:], ALU.mult, ALU.mult).then_inc(fin_ready, 1)


INPUTS = ["x", "mem", "g_mix", "w_in", "na_rpb", "mla_q_norm", "w_mla_uq", "mla_kv_norm", "w_mla_ukv", "g_mem",
          "w_mem_kv", "w_o_na", "w_o_mla", "w_o_mem", "w_out", "g_ffn", "w_router", "b_router", "w_gate", "w_up",
          "w_down", "g_final"]


def shape_constants():
    t = np.arange(S)
    col, row = t // ROWS, t % ROWS
    d = ROPE // 2
    inv = (ROPE_BASE ** (-np.arange(0, d, 2, dtype=np.float32) / d)).astype(np.float32)
    cos, sin = np.zeros((ROPE, S), np.float32), np.zeros((ROPE, S), np.float32)
    for part, pos in enumerate((row, col)):
        ang = (pos.astype(np.float32)[None, :] * inv[:, None]).astype(np.float32)
        r0 = d * part
        cos[r0:r0 + d // 2] = cos[r0 + d // 2:r0 + d] = np.cos(ang)
        sin[r0:r0 + d // 2] = -np.sin(ang)
        sin[r0 + d // 2:r0 + d] = np.sin(ang)
    half = (np.arange(P)[:, None] >= CAP).astype(np.float32)
    return {"rope_cos": cos, "rope_sin": sin, "half_col": half}


def kernel(**inputs):
    import concourse.bacc as bacc
    from concourse.bass_utils import run_bass_kernel_spmd

    nc = bacc.Bacc("TRN2", target_bir_lowering=False, num_devices=1)
    arrays, aps = {}, {}
    given = {name: np.ascontiguousarray(inputs[name]) for name in INPUTS}
    given.update(shape_constants())
    for name, a in given.items():
        arrays[f"in_{name}"] = a
        aps[name] = nc.dram_tensor(f"in_{name}", a.shape, mybir.dt.from_np(a.dtype), kind="ExternalInput").ap()
    out = nc.dram_tensor("out", (1, S, D), F32, kind="ExternalOutput").ap()
    build(nc, aps, out)
    return run_bass_kernel_spmd(nc, [arrays], core_ids=[0]).results[0]["out"]
```

```python
from contextlib import ExitStack

import numpy as np

import concourse.bass as bass
from concourse import mybir

F32 = mybir.dt.float32
F32R = mybir.dt.float32r
U32 = mybir.dt.uint32
ACT = mybir.ActivationFunctionType
ALU = mybir.AluOpType
AX = mybir.AxisListType

P = 128
D = 1024
S = 512
GRID_W = 64
ROWS = S // GRID_W
N_MEM = 256
EPS = 1e-6
NA_HEADS, NA_DIM = 8, 64
WIN_R, WIN_C = 8, 16
MLA_HEADS, NOPE, ROPE, MLA_V = 8, 64, 32, 64
Q_RANK, KV_RANK = 384, 256
ROPE_BASE = 10000.0
MEM_HEADS, MEM_DIM = 4, 128
N_EXP, FF = 16, 1024
CAP = 2 * S // N_EXP
NA_W = NA_HEADS * NA_DIM
MEM_W = MEM_HEADS * MEM_DIM
MLA_QK = NOPE + ROPE
KB = D // P
TB = S // P
MB = N_MEM // P
PAIRS = N_EXP // 2
HALF = D // 2
C_Q, C_K, C_V = 0, NA_W, 2 * NA_W
C_CQ = 3 * NA_W
C_CKV = C_CQ + Q_RANK
C_KR = C_CKV + KV_RANK
C_QM = C_KR + ROPE
C_GATE = C_QM + MEM_W
MASKED = -1.0e30
LOWEST = -3.0e38

G_MIX, G_MEM, G_Q, G_KV, G_FFN = 0, KB, 2 * KB, 2 * KB + 3, 2 * KB + 5
GAIN_ROWS = 3 * KB + 5

COLS_PER_TILE = P // ROWS
RPB_R, RPB_C = 2 * WIN_R - 1, 2 * WIN_C - 1
TOEP_U = 3 * COLS_PER_TILE
RPB_PITCH, RPB_PAD = 64, 16
RPB_BUF = ROWS * NA_HEADS * ROWS * RPB_PITCH

SLOT_FIRST, SLOT_PREV, SLOT_MID, SLOT_NEXT, SLOT_LAST = range(5)
SLOTS = [(SLOT_FIRST, 0, True, False), (SLOT_PREV, -1, True, False), (SLOT_MID, 0, True, True),
         (SLOT_NEXT, 1, False, True), (SLOT_LAST, 0, False, True)]


def key_tiles(qb):
    return list(range(max(qb - 1, 0), min(qb + 1, TB - 1) + 1))


def table_slots(qb):
    if qb == 0:
        return SLOT_FIRST, SLOT_NEXT - SLOT_FIRST, 2
    if qb == TB - 1:
        return SLOT_PREV, SLOT_LAST - SLOT_PREV, 2
    return SLOT_PREV, 1, 3


def plan():
    jobs, steps = [], []

    def job(src, c0, n, kb):
        jobs.append((src, c0, n, kb))
        return len(jobs) - 1

    def tile(kind, args, j=None):
        steps.append(("tile", kind, args, j))

    for kb in range(KB):
        tile("memT", (kb,))
    for kb in range(KB):
        tile("nT", (kb,))
    for c in range(2):
        j = job("mem_kv", 256 * c, 256, KB)
        for i in range(2):
            tile("kmem", (2 * c + i, i), j)
        steps.append(("end", j))
    for c in range(2):
        j = job("mem_kv", MEM_W + 256 * c, 256, KB)
        for m in range(MB):
            tile("vmem", (m, c), j)
        steps.append(("end", j))
    for kind, c0 in (("qna", C_Q), ("kna", C_K)):
        for c in range(2):
            j = job("in", c0 + 256 * c, 256, KB)
            for i in range(2):
                tile(kind, (2 * c + i, i), j)
            steps.append(("end", j))
    for c in range(2):
        j = job("in", C_V + 256 * c, 256, KB)
        for t in range(TB):
            tile("vna", (t, c), j)
        steps.append(("end", j))
    for c0, n in ((0, 2), (2, 1)):
        j = job("in", C_CQ + P * c0, P * n, KB)
        for i in range(n):
            tile("cq", (c0 + i, i), j)
        steps.append(("end", j))
    tile("ssq", ("q",))
    j = job("in", C_CKV, 256, KB)
    for i in range(2):
        tile("ckv", (i, i), j)
    steps.append(("end", j))
    tile("ssq", ("kv",))
    j = job("in", C_KR - NOPE, MLA_QK, KB)
    tile("kpe", (), j)
    steps.append(("end", j))
    for c in range(2):
        j = job("in", C_QM + 256 * c, 256, KB)
        for i in range(2):
            tile("qmem", (2 * c + i, i), j)
        steps.append(("end", j))
    steps.append(("attn", "na"))
    steps.append(("attn", "mem"))
    steps.append(("latent",))
    for c in range(2):
        j = job("uq", 4 * MLA_QK * c, 4 * MLA_QK, Q_RANK // P)
        for i in range(4):
            tile("uq", (4 * c + i, i), j)
        steps.append(("end", j))
    j = job("ukv", 0, 1024, KV_RANK // P)
    for h in range(MLA_HEADS):
        tile("uk", (h,), j)
    for t in range(TB):
        tile("vmla", (t,), j)
    steps.append(("end", j))
    steps.append(("attn", "mla"))
    for n, (br, wo) in enumerate(((0, "o_na"), (2, "o_mem"), (1, "o_mla"))):
        for half in range(2):
            j = job(wo, 512 * half, 512, 4)
            for i in range(4):
                tile("o", (br, i), j)
            steps.append(("end", j))
            for c in range(2):
                j = job("in", C_GATE + br * D + 512 * half + 256 * c, 256, KB)
                for i in range(2):
                    tile("gate", (n, 4 * half + 2 * c + i, i), j)
                steps.append(("end", j))
    for c in range(4):
        j = job("out", 256 * c, 256, KB)
        for t in range(TB):
            tile("out", (t, c), j)
        steps.append(("end", j))
        for kb in range(2 * c - 4, 2 * c - 2):
            if kb >= 0:
                steps.append(("route", kb))
        for kb in range(2 * c - 2, 2 * c):
            if kb >= 0:
                steps.append(("turn_h", kb))
    for kb in (4, 5):
        steps.append(("route", kb))
    for kb in (6, 7):
        steps.append(("turn_h", kb))
    for kb in (6, 7):
        steps.append(("route", kb))
    return jobs, steps


def units_of(branch):
    if branch == "mem":
        return [(g, qb, None) for g in range(2) for qb in range(TB)]
    return [(g, qb, hp) for g in range(4) for qb in range(TB) for hp in range(2)]


def width_of(branch, qb):
    return P * len(key_tiles(qb)) if branch == "na" else S


def build(nc, ins, out):
    jobs, steps = plan()
    n_jobs = len(jobs)

    acc_of, unit_base, group_base = {}, {}, {}
    na_, nu_, ng_ = 0, 0, 0
    y_acc = {}
    for n, st in enumerate(steps):
        if st[0] == "tile":
            acc_of[n] = na_
            na_ += 1
        elif st[0] == "attn":
            br = st[1]
            unit_base[br], group_base[br] = nu_, ng_
            us = units_of(br)
            nu_ += len(us)
            groups = us[-1][0] + 1
            ng_ += groups
            for g in range(groups):
                y_acc[br, g] = na_
                na_ += 2 if br == "mem" else 1
    n_acc = na_
    acc_at = {}
    for n, st in enumerate(steps):
        if st[0] == "tile":
            acc_at[(st[1],) + st[2]] = acc_of[n]
    job_end = {st[3]: acc_of[n] + 1 for n, st in enumerate(steps) if st[0] == "tile" and st[3] is not None}
    last_gate = max(a for k, a in acc_at.items() if k[0] == "gate")
    last_acc_use = {"na": y_acc["na", 3] + 1, "mem": y_acc["mem", 1] + 2, "mla": y_acc["mla", 3] + 1}

    with ExitStack() as ctx:
        base = -(-nc.sbuf_base // 64) * 64

        def at(name, shape, off, dt=F32):
            return nc.alloc_sbuf_tensor_at(name, shape, dt, offset=base + off)

        K = 1024
        nt_hi = at("nt_hi", [P, KB, S], 0, F32R)
        nt_lo = at("nt_lo", [P, KB, S], 16 * K, F32R)
        w_raw = [at(f"w_raw{i}", [P, 2048], (32 + 8 * i) * K) for i in range(2)]
        w_hi = [at(f"w_hi{i}", [P, 2048], (48 + 16 * i) * K, F32R) for i in range(2)]
        w_lo = [at(f"w_lo{i}", [P, 2048], (56 + 16 * i) * K, F32R) for i in range(2)]
        q_na = at("q_na", [P, 4, S], 80 * K)
        k_na = at("k_na", [P, 4, S], 88 * K)
        q_mem = at("q_mem", [P, 4, S], 96 * K)
        toep = at("toep", [P, NA_HEADS, ROWS, TOEP_U], 80 * K)
        v_na = at("v_na", [P, TB, NA_W], 112 * K)
        table = at("table", [P, NA_HEADS, 5, P], 120 * K)
        k_mem = at("k_mem", [P, MEM_HEADS, N_MEM], 140 * K)
        v_mem = at("v_mem", [P, MB, MEM_W], 144 * K)
        memt_hi = at("memt_hi", [P, KB, N_MEM], 148 * K, F32R)
        memt_lo = at("memt_lo", [P, KB, N_MEM], 156 * K, F32R)
        c_q = at("c_q", [P, 3, S], 156 * K)
        c_kv = at("c_kv", [P, 2, S], 162 * K)
        k_pe = at("k_pe", [P, S], 166 * K)
        x_tok = at("x_tok", [P, TB, D], 168 * K)
        mem_tok = at("mem_tok", [P, MB, D], 184 * K)
        junk = at("junk", [P, D], 192 * K)
        rms_root = at("rms_root", [P, S], 192 * K)
        rms_inv = at("rms_inv", [P, S], 194 * K)
        probs_t = [at(f"probs_t{i}", [P, 2, TB, S], (168 + 16 * i) * K) for i in range(2)]
        cq_hi = at("cq_hi", [P, 3, S], 168 * K, F32R)
        cq_lo = at("cq_lo", [P, 3, S], 174 * K, F32R)
        ckv_hi = at("ckv_hi", [P, 2, S], 180 * K, F32R)
        ckv_lo = at("ckv_lo", [P, 2, S], 184 * K, F32R)
        q_mla = at("q_mla", [MLA_QK, MLA_HEADS, S], 120 * K)
        k_mla = at("k_mla", [MLA_QK, MLA_HEADS, S], 140 * K)
        v_mla = at("v_mla", [P, TB, MLA_HEADS * MLA_V], 112 * K)
        rope_cs = at("rope_cs", [MLA_QK, 2, S], 136 * K)
        probs = [at(f"probs{i}", [P, S], (200 + 2 * i) * K) for i in range(3)]
        square = [at(f"square{i}", [P, S], (200 + 2 * i) * K) for i in range(3)]
        rope_a = at("rope_a", [MLA_QK, S], 188 * K)
        rope_b = at("rope_b", [MLA_QK, S], 190 * K)
        y_hi, y_lo = {}, {}
        for g in range(4):
            y_hi[0, g] = at(f"y_na_hi{g}", [P, S], (80 + 2 * g) * K, F32R)
            y_lo[0, g] = at(f"y_na_lo{g}", [P, S], (88 + 2 * g) * K, F32R)
            y_hi[2, g] = at(f"y_mem_hi{g}", [P, S], (96 + 2 * g) * K, F32R)
            y_lo[2, g] = at(f"y_mem_lo{g}", [P, S], (104 + 2 * g) * K, F32R)
            y_hi[1, g] = at(f"y_mla_hi{g}", [P, S], (120 + 4 * g) * K, F32R)
            y_lo[1, g] = at(f"y_mla_lo{g}", [P, S], (140 + 4 * g) * K, F32R)
        merged = at("merged", [P, KB, S], 176 * K)
        branch_o = [at(f"branch_o{i}", [P, S], (192 + 2 * i) * K) for i in range(4)]
        gate_s = [at(f"gate_s{i}", [P, S], (200 + 2 * i) * K) for i in range(2)]
        m_hi = at("m_hi", [P, KB, S], 80 * K, F32R)
        m_lo = at("m_lo", [P, KB, S], 96 * K, F32R)
        h_tok = at("h_tok", [P, TB, D], 0)
        hn_t = [at(f"hn_t{i}", [P, S], (192 + 2 * i) * K) for i in range(2)]
        route_w = at("route_w", [P, KB, N_EXP], 200 * K)
        junk_h = at("junk_h", [P, 256], 201 * K)
        hr_tok = at("hr_tok", [P, TB, D], 96 * K)
        logit_t = at("logit_t", [N_EXP, S], 196 * K)
        aff_t = at("aff_t", [N_EXP, S], 198 * K)
        R = 176 * K
        aff = at("aff", [P, TB, N_EXP], R)
        top_v = at("top_v", [N_EXP, P], R + 256)
        top_i = at("top_i", [N_EXP, CAP], R + 768, U32)
        top_f = at("top_f", [N_EXP, P], R + 1024)
        slot_gain = at("slot_gain", [P, N_EXP], R + 1536)
        slot_id = at("slot_id", [P, N_EXP], R + 1600)
        slot_tok = at("slot_tok", [P, PAIRS], R + 1664, U32)
        row_stat = at("row_stat", [P, 4, TB], R + 1728)
        gu_w = [[at(f"gu_w{i}{c}", [P, 4, FF], off * K) for c, off in enumerate(offs)]
                for i, offs in enumerate(((16, 112, 128, 144), (48, 64, 80, 96)))]
        down_w = [at(f"down_w{c}", [P, 4, D], off * K) for c, off in enumerate((160, 32))]
        xs_cur = at("xs_cur", [P, D], 178 * K)
        xs_t = at("xs_t", [P, KB, P], 182 * K)
        hidden_t = at("hidden_t", [P, 4, P], 186 * K)
        silu_s = at("silu_s", [P, 512], 188 * K)
        hidden = at("hidden", [P, 512], 190 * K)
        ye_hi = [at(f"ye_hi{i}", [P, HALF], (192 + 2 * i) * K, F32R) for i in range(2)]
        ye_lo = [at(f"ye_lo{i}", [P, HALF], (196 + 2 * i) * K, F32R) for i in range(2)]
        one_hot = [at(f"one_hot{i}", [P, S], (200 + 2 * i) * K, F32R) for i in range(2)]
        tok_row = at("tok_row", [P, S], 204 * K)
        tok_int = at("tok_int", [P, S], 202 * K, mybir.dt.int32)
        fin_g = at("fin_g", [P, D], 178 * K)
        junk_b = at("junk_b", [P, D], 186 * K)
        SM = 206 * K
        ident = at("ident", [P, P], SM)
        ones = at("ones", [P, P], SM + 512)
        gain_t = at("gain_t", [P, 32], SM + 1024)
        stat = at("stat", [P, 64], SM + 1152)
        soft_m = at("soft_m", [P, 4, 2], SM + 1408)
        soft_s = at("soft_s", [P, 4, 2], SM + 1440)
        soft_r = at("soft_r", [P, 4, 2], SM + 1472)
        h_part = at("h_part", [P, TB, 4], SM + 1152 + 96)
        eps_col = at("eps_col", [P, 1], SM + 1504)
        route_b = at("route_b", [P, N_EXP], SM + 1536)
        gain_rows = at("gain_rows", [GAIN_ROWS, P], 200 * K)

        bank = [ctx.enter_context(nc.psum_tensor(f"bank{i}", [P, 512], F32)) for i in range(8)]
        ACC, SC, TR = bank[0:3], bank[3:6], bank[6:8]

        rpb_rows = nc.dram_tensor("rpb_rows", (ROWS, NA_HEADS * ROWS, RPB_PITCH), F32, kind="Internal").ap()
        hn_rows = nc.dram_tensor("hn_rows", (S, D), F32, kind="Internal").ap()

        def sem(name):
            return ctx.enter_context(nc.semaphore(name))

        gains_in, mem_in, rpb_zeroed, rpb_in, toep_in = (sem(x) for x in ("gains_in", "mem_in", "rpb_zeroed", "rpb_in", "toep_in"))
        x_in = sem("x_in")
        rope_in, bias_in, resid_in, route_in = (sem(x) for x in ("rope_in", "bias_in", "resid_in", "route_in"))
        raw_in = [sem(f"raw_in{i}") for i in range(2)]
        w_hi_ready, w_lo_ready = sem("w_hi_ready"), sem("w_lo_ready")
        const_ready, zeros_ready, ident_ready, table_ready, pool_seq = (sem(x) for x in ("const_ready", "zeros_ready", "ident_ready", "table_ready", "pool_seq"))
        gain_ps, gain_ready = sem("gain_ps"), sem("gain_ready")
        sumsq_done, root_in, root_done, xn_ready = sem("sumsq_done"), sem("root_in"), sem("root_done"), sem("xn_ready")
        acc_done = sem("acc_done")
        acc_free = [sem(f"acc_free{i}") for i in range(3)]
        hi_done = sem("hi_done")
        sq_ready, latent_hi = sem("sq_ready"), sem("latent_hi")
        latent_ready, rope_ready, kpe_spread = sem("latent_ready"), sem("rope_ready"), sem("kpe_spread")
        score_done, max_done, exp_done, p_ready, t_done = (sem(x) for x in ("score_done", "max_done", "exp_done", "p_ready", "t_done"))
        pt_done = [sem("pt_done_act"), sem("pt_done_dve")]
        silu_ready, gate_used, merged_hi, merged_lo = sem("silu_ready"), sem("gate_used"), sem("merged_hi"), sem("merged_lo")
        dve_seq = sem("dve_seq")
        hsq_done, hsum_ready, hroot_done, hr_ready, hr_stored = (sem(x) for x in ("hsq_done", "hsum_ready", "hroot_done", "hr_ready", "hr_stored"))
        hnt_ps, hnt_ready, routed, tok_ready = sem("hnt_ps"), sem("hnt_ready"), sem("routed"), sem("tok_ready")
        logit_ready, logit_tok, soft_in, soft_exp, aff_ready, aff_ps, top_ready, top_ps, slots_ready = (
            sem(x) for x in ("logit_ready", "logit_tok", "soft_in", "soft_exp", "aff_ready", "aff_ps", "top_ready", "top_ps", "slots_ready"))
        xs_in, xs_tr, xs_t_ready = sem("xs_in"), sem("xs_tr"), sem("xs_t_ready")
        gu_in = [[sem(f"gu_in{i}{c}") for c in range(4)] for i in range(2)]
        down_in = [sem(f"down_in{c}") for c in range(2)]
        chunk_used = sem("chunk_used")
        gate_mm, up_mm, sig_ready, hid_ready, hid_tr, hid_t_ready, down_mm, y_hi_ready, y_ready, hot_ready, comb_ps, summed = (
            sem(x) for x in ("gate_mm", "up_mm", "sig_ready", "hid_ready", "hid_tr", "hid_t_ready", "down_mm", "y_hi_ready", "y_ready",
                             "hot_ready", "comb_ps", "summed"))
        fin_g_in, fin_sq, fin_root, fin_inv, fin_ready, out_done = (sem(x) for x in ("fin_g_in", "fin_sq", "fin_root", "fin_inv", "fin_ready", "out_done"))

        w_src = {"in": ins["w_in"][0], "mem_kv": ins["w_mem_kv"][0], "uq": ins["w_mla_uq"][0],
                 "ukv": ins["w_mla_ukv"][0], "o_na": ins["w_o_na"][0], "o_mla": ins["w_o_mla"][0],
                 "o_mem": ins["w_o_mem"][0], "out": ins["w_out"][0]}
        grid = "(r c) d -> c r d"
        x_dram = ins["x"][0].rearrange(grid, r=ROWS)
        out_dram = out[0].rearrange(grid, r=ROWS)
        def job_shape(j):
            return jobs[j][3], jobs[j][2]

        def w_view(t, j):
            kb, n = job_shape(j)
            return t[:, 0:kb * n].rearrange("p (k n) -> p k n", k=kb)

        def wait_read(eng, n):
            for b in range(3):
                eng.wait_ge(acc_free[b], (n - b + 2) // 3)

        def wait_acc_bank(eng, a):
            if a >= 3:
                eng.wait_ge(acc_free[a % 3], a // 3)

        def y_part(parts, br, g, hp):
            return parts[{"na": 0, "mla": 1, "mem": 2}[br], 2 * g + hp if br == "mem" else g]

        def probs_out(eng, ub, us, br, k, which):
            u = ub + k
            g, qb, hp = us[k]
            groups = us[-1][0] + 1
            ng = len(us) // groups
            gg = group_base[br] + g
            eng.wait_ge(t_done, u + 1)
            if k % ng < 2 and gg >= 2:
                pa = prev_group_acc[gg - 2]
                eng.wait_ge(acc_done, pa)
            buf = probs_t[gg % 2]
            cols = slice(P * qb, P * qb + P)
            if br == "mem":
                dst = buf[:, :, 0:2, cols]
                src = TR[u % 2][:].rearrange("p (a b n) -> p a b n", a=2, b=2)
            else:
                nk = width_of(br, qb) // P
                dst = buf[:, hp, 0:nk, cols]
                src = TR[u % 2][:, 0:nk * P].rearrange("p (b n) -> p b n", b=nk)
            if which == 0:
                eng.activation(dst, src, ACT.Copy).then_inc(pt_done[0], 1)
            else:
                eng.tensor_copy(dst, src).then_inc(pt_done[1], 1)

        def tok_banks(t):
            return (bank[2], bank[3]) if t % 2 == 0 else (bank[6], bank[7])

        prev_group_acc = []
        for br in ("na", "mem", "mla"):
            for g in range(2 if br == "mem" else 4):
                prev_group_acc.append(y_acc[br, g] + (2 if br == "mem" else 1))

        block = ctx.enter_context(nc.Block())

        @block.sync
        def _(sp):
            sp.dma_start(mem_tok[:], ins["mem"][0].rearrange("(m p) d -> p m d", p=P)).then_inc(mem_in, 16)
            for row, name, n in ((G_MIX, "g_mix", KB), (G_MEM, "g_mem", KB), (G_Q, "mla_q_norm", 3),
                                 (G_KV, "mla_kv_norm", 2), (G_FFN, "g_ffn", KB)):
                sp.dma_start(gain_rows[row:row + n, :], ins[name][0].rearrange("(k p) -> k p", p=P)).then_inc(gains_in, 16)
            for t in range(TB):
                sp.dma_start(x_tok[:, t, :], x_dram[COLS_PER_TILE * t:COLS_PER_TILE * (t + 1)]).then_inc(x_in, 16)
            sp.dma_start(route_b[:], ins["b_router"][0].partition_broadcast(P)).then_inc(bias_in, 16)

            def load_job(j):
                src, c0, n, kb = jobs[j]
                if j >= 2:
                    sp.wait_ge(w_lo_ready, j - 1)
                sp.dma_start(w_view(w_raw[j % 2], j),
                             w_src[src][:, c0:c0 + n].rearrange("(k p) n -> p k n", p=P)).then_inc(raw_in[j % 2], 16)

            load_job(0)
            load_job(1)
            sp.wait_ge(zeros_ready, 1)
            sp.dma_start(rpb_rows.rearrange("a b n -> (a b n)").rearrange("(p n) -> p n", p=P), junk[:, 0:RPB_BUF // P]).then_inc(rpb_zeroed, 16)
            sp.wait_ge(rpb_zeroed, 16)
            for r in range(ROWS):
                src = bass.AP(tensor=ins["na_rpb"].tensor, offset=(WIN_R - 1 - r) * RPB_C,
                              ap=[[RPB_R * RPB_C, NA_HEADS], [RPB_C, ROWS], [1, RPB_C]])
                sp.dma_start(rpb_rows[r, :, RPB_PAD:RPB_PAD + RPB_C].rearrange("(h k) n -> h k n", h=NA_HEADS), src).then_inc(rpb_in, 16)
            sp.wait_ge(rpb_in, 16 * ROWS)
            for c in range(COLS_PER_TILE):
                src = bass.AP(tensor=rpb_rows.tensor, offset=RPB_PAD - 1 - c,
                              ap=[[NA_HEADS * ROWS * RPB_PITCH, ROWS], [RPB_PITCH, NA_HEADS * ROWS], [1, TOEP_U]])
                sp.dma_start(toep[ROWS * c:ROWS * (c + 1)].rearrange("p h k u -> p (h k) u"), src).then_inc(toep_in, 16)
            out_job = next(j for j in range(n_jobs) if jobs[j][0] == "out")
            for j in range(2, n_jobs):
                if j == out_job + 2:
                    sp.wait_ge(acc_done, last_gate + 1)
                    sp.wait_ge(gate_used, 3 * KB)
                    for t in range(TB):
                        sp.dma_start(h_tok[:, t, :], x_dram[COLS_PER_TILE * t:COLS_PER_TILE * (t + 1)]).then_inc(resid_in, 16)
                    sp.dma_start(route_w[:], ins["w_router"][0].rearrange("(k p) e -> p k e", p=P)).then_inc(route_in, 16)
                load_job(j)

            def load_gate_up(e, i, c):
                src = ins[("w_gate", "w_up")[c // 2]][0, e, (c % 2) * 512:(c % 2 + 1) * 512, :]
                sp.dma_start(gu_w[i][c][:], src.rearrange("(k p) n -> p k n", p=P)).then_inc(gu_in[i][c], 16)

            def load_down(e, c):
                src = ins["w_down"][0, e, c * 512:(c + 1) * 512, :]
                sp.dma_start(down_w[c][:], src.rearrange("(k p) n -> p k n", p=P)).then_inc(down_in[c], 16)

            sp.wait_ge(merged_lo, KB)
            for c in range(4):
                load_gate_up(0, 0, c)
            load_down(0, 0)
            sp.wait_ge(acc_done, n_acc)
            load_down(0, 1)
            for c in range(3):
                load_gate_up(1, 1, c)
            for t in range(TB):
                sp.wait_ge(hr_ready, t + 1)
                sp.dma_start(hn_rows[P * t:P * t + P, :], hr_tok[:, t, :]).then_inc(hr_stored, 16)
            sp.wait_ge(hr_stored, 16 * TB)
            load_gate_up(1, 1, 3)
            def next_gate_up(j, i, m):
                sp.wait_ge(chunk_used, 6 * j + (3 * i - 5 + m))
                load_gate_up(2 * j + i, i, 2 * m)
                sp.wait_ge((gate_mm, up_mm)[m], 2 * j + (i - 1))
                load_gate_up(2 * j + i, i, 2 * m + 1)

            def next_down(j, i):
                sp.wait_ge(chunk_used, 6 * j + 3 * i)
                load_down(2 * j + i, 0)
                sp.wait_ge(down_mm, 2 * j + i)
                load_down(2 * j + i, 1)

            next_gate_up(1, 0, 0)
            next_gate_up(1, 0, 1)
            next_down(0, 1)
            next_gate_up(1, 1, 0)
            next_gate_up(1, 1, 1)
            next_down(1, 0)
            with sp.Fori(2, PAIRS) as j:
                next_gate_up(j, 0, 0)
                next_down(j - 1, 1)
                next_gate_up(j, 0, 1)
                next_gate_up(j, 1, 0)
                next_down(j, 0)
                next_gate_up(j, 1, 1)
            next_down(PAIRS - 1, 1)
            sp.wait_ge(xs_tr, PAIRS)
            sp.dma_start(fin_g[:], ins["g_final"].partition_broadcast(P)).then_inc(fin_g_in, 16)
            for t in range(TB):
                sp.wait_ge(fin_ready, t + 1)
                sp.dma_start(out_dram[COLS_PER_TILE * t:COLS_PER_TILE * (t + 1)], h_tok[:, t, :]).then_inc(out_done, 16)
            sp.wait_ge(out_done, 16 * TB)

        @block.gpsimd
        def _(pool):
            pool.memset(junk[:, 0:RPB_BUF // P], 0.0).then_inc(zeros_ready, 1)
            pool.memset(ones[:], 1.0).then_inc(const_ready, 1)
            pool.memset(eps_col[:], EPS).then_inc(const_ready, 1)
            pool.memset(ident[:], 0.0).then_inc(pool_seq, 1)
            pool.wait_ge(pool_seq, 1)
            pool.affine_select(out=ident[:], in_=ident[:], compare_op=ALU.not_equal, fill=1.0, base=0,
                               pattern=[[-1, P]], channel_multiplier=1).then_inc(ident_ready, 1)
            pool.wait_ge(toep_in, 16 * COLS_PER_TILE)
            seq = 1
            for slot, dt, _, _ in SLOTS:
                u0 = COLS_PER_TILE * (dt + 1)
                pool.tensor_copy(table[:, :, slot, :].rearrange("p h (c r) -> p h c r", r=ROWS),
                                 toep[:, :, :, u0:u0 + COLS_PER_TILE].rearrange("p h r c -> p h c r")).then_inc(pool_seq, 1)
                seq += 1
            for slot, dt, lower, upper in SLOTS:
                part = table[:, :, slot, :].rearrange("p h (c r) -> p h c r", r=ROWS)
                for sign, on in ((1, lower), (-1, upper)):
                    if not on:
                        continue
                    pool.wait_ge(pool_seq, seq)
                    b = P * dt + ROWS * (WIN_C // 2) + ROWS - 1 if sign == 1 else -P * dt + ROWS * (WIN_C // 2 - 1)
                    pool.affine_select(out=part, in_=part, compare_op=ALU.is_ge, fill=MASKED, base=b,
                                       pattern=[[0, NA_HEADS], [sign * ROWS, COLS_PER_TILE], [0, ROWS]],
                                       channel_multiplier=-sign).then_inc(pool_seq, 1)
                    seq += 1
            pool.wait_ge(pool_seq, seq)
            pool.memset(stat[0:1, 60:61], 0.0).then_inc(table_ready, 1)
            pool.wait_ge(rope_ready, 1)
            pool.wait_ge(exp_done, unit_base["mla"])
            pool.wait_ge(acc_done, last_acc_use["mem"])
            for h in range(MLA_HEADS):
                pool.tensor_copy(k_mla[NOPE:MLA_QK, h, :], k_pe[NOPE:MLA_QK, :]).then_inc(kpe_spread, 1)
            pool.wait_ge(gate_used, 3 * KB)
            pool.iota(tok_int[:], pattern=[[1, S]], base=0, channel_multiplier=0).then_inc(pool_seq, 1)
            pool.wait_ge(pool_seq, seq + 1)
            pool.tensor_copy(tok_row[:], tok_int[:]).then_inc(tok_ready, 1)
            pool.wait_ge(hr_stored, 16 * TB)
            pool.wait_ge(slots_ready, 1)
            for j in range(PAIRS):
                if j > 0:
                    pool.wait_ge(xs_tr, j)
                pool.indirect_dma_start(out=xs_cur[:], out_offset=None, in_=hn_rows[:, :],
                                        in_offset=bass.IndirectOffsetOnAxis(ap=slot_tok[:, j:j + 1], axis=0)).then_inc(xs_in, 16)

        @block.scalar
        def _(act):
            def split_hi(j):
                act.wait_ge(raw_in[j % 2], 16 * (j // 2 + 1))
                if j >= 2:
                    act.wait_ge(acc_done, job_end[j - 2])
                kb, n = job_shape(j)
                act.activation(w_hi[j % 2][:, 0:kb * n], w_raw[j % 2][:, 0:kb * n], ACT.Copy).then_inc(w_hi_ready, 1)

            act.wait_ge(mem_in, 16)
            act.wait_ge(rpb_zeroed, 16)
            for m in range(MB):
                act.activation(junk[:], mem_tok[:, m, :], ACT.Square, accum_out=stat[:, m:m + 1]).then_inc(sumsq_done, 1)
                act.wait_ge(sumsq_done, m + 1)
            act.wait_ge(x_in, 16 * TB)
            for t in range(TB):
                act.activation(junk[:], x_tok[:, t, :], ACT.Square, accum_out=stat[:, MB + t:MB + t + 1]).then_inc(sumsq_done, 1)
                act.wait_ge(sumsq_done, MB + t + 1)
            act.wait_ge(const_ready, 2)
            act.activation(stat[:, 8:8 + MB + TB], stat[:, 0:MB + TB], ACT.Sqrt, scale=1.0 / D, bias=eps_col[:]).then_inc(root_done, 1)
            split_hi(0)
            split_hi(1)
            n_hi = n_copy = n_out = n_gate = 0
            n_units = 0
            for n, st in enumerate(steps):
                if st[0] == "end":
                    if st[1] + 2 < n_jobs:
                        split_hi(st[1] + 2)
                    continue
                if st[0] == "latent":
                    act.wait_ge(max_done, unit_base["na"] + len(units_of("na")))
                    act.dma_start(rope_cs[NOPE:MLA_QK, 0, :], ins["rope_cos"]).then_inc(rope_in, 16)
                    act.dma_start(rope_cs[NOPE:MLA_QK, 1, :], ins["rope_sin"]).then_inc(rope_in, 16)
                    act.wait_ge(latent_ready, 5)
                    act.wait_ge(acc_done, last_acc_use["mem"])
                    for i in range(5):
                        dst, src = (cq_hi[:, i, :], c_q[:, i, :]) if i < 3 else (ckv_hi[:, i - 3, :], c_kv[:, i - 3, :])
                        act.activation(dst, src, ACT.Copy).then_inc(latent_hi, 1)
                    continue
                if st[0] == "route":
                    continue
                if st[0] == "turn_h":
                    kb = st[1]
                    act.wait_ge(hnt_ps, kb + 1)
                    if kb >= 2:
                        act.wait_ge(routed, kb - 1)
                    act.activation(hn_t[kb % 2][:], TR[kb % 2][:], ACT.Copy, scale=gain_t[:, G_FFN + kb:G_FFN + kb + 1]).then_inc(hnt_ready, 1)
                    continue
                if st[0] == "attn":
                    br = st[1]
                    us, ub = units_of(br), unit_base[br]
                    groups = us[-1][0] + 1
                    ng = len(us) // groups
                    for i in range(len(us) + 3):
                        u = ub + i
                        if i < len(us):
                            act.wait_ge(max_done, u + 1)
                            if u >= 3:
                                act.wait_ge(t_done, u - 2)
                            w = width_of(br, us[i][1])
                            src = probs[u % 3] if br == "na" else SC[u % 3]
                            if br == "mem":
                                for hp in range(2):
                                    part = slice(256 * hp, 256 * hp + 256)
                                    last = act.activation(probs[u % 3][:, part], src[:, part], ACT.Exp, bias=soft_m[:, u % 4, hp:hp + 1],
                                                          accum_out=soft_s[:, u % 4, hp:hp + 1])
                                last.then_inc(exp_done, 1)
                            else:
                                act.activation(probs[u % 3][:, 0:w], src[:, 0:w], ACT.Exp, bias=soft_m[:, u % 4, 0:1],
                                               accum_out=soft_s[:, u % 4, 0:1]).then_inc(exp_done, 1)
                        k = i - 2
                        if 0 <= k < len(us) and (ub + k) % 2 == 0:
                            probs_out(act, ub, us, br, k, 0)
                        g, r = divmod(i - 2, ng)
                        if r == 0 and g >= 1:
                            for hp in range(2 if br == "mem" else 1):
                                a = y_acc[br, g - 1] + hp
                                act.wait_ge(acc_done, a + 1)
                                act.activation(y_part(y_hi, br, g - 1, hp)[:], ACC[a % 3][:], ACT.Copy).then_inc(hi_done, 1)
                                n_hi += 1
                    continue
                kind, args = st[1], st[2]
                a = acc_of[n]
                ps = ACC[a % 3]
                if kind == "out":
                    t, c = args
                    act.wait_ge(acc_free[a % 3], a // 3 + 1)
                    if n_out > 0:
                        act.wait_ge(hsq_done, n_out)
                    n_out += 1
                    act.activation(junk_h[:], h_tok[:, t, 256 * c:256 * c + 256], ACT.Square,
                                   accum_out=h_part[:, t, c:c + 1]).then_inc(hsq_done, 1)
                    continue
                if kind in ("uk", "vmla") and args == (0,):
                    act.wait_ge(acc_done, last_acc_use["mem"])
                act.wait_ge(acc_done, a + 1)
                if kind in ("memT", "nT"):
                    kb, = args
                    act.wait_ge(gain_ready, 1)
                    if kind == "memT":
                        act.activation(memt_hi[:, kb, :], ps[:, 0:N_MEM], ACT.Copy, scale=gain_t[:, G_MEM + kb:G_MEM + kb + 1]).then_inc(hi_done, 1)
                    else:
                        act.activation(nt_hi[:, kb, :], ps[:], ACT.Copy, scale=gain_t[:, G_MIX + kb:G_MIX + kb + 1]).then_inc(hi_done, 1)
                    n_hi += 1
                elif kind == "kmem":
                    act.activation(k_mem[:, args[0], :], ps[:, 0:N_MEM], ACT.Copy).then_inc(acc_free[a % 3], 1)
                elif kind == "vmem":
                    m, c = args
                    act.activation(v_mem[:, m, 256 * c:256 * c + 256], ps[:, 0:256], ACT.Copy).then_inc(acc_free[a % 3], 1)
                elif kind == "qna":
                    act.wait_ge(table_ready, 1)
                    act.activation(q_na[:, args[0], :], ps[:], ACT.Copy, scale=NA_DIM ** -0.5).then_inc(acc_free[a % 3], 1)
                elif kind == "kna":
                    act.activation(k_na[:, args[0], :], ps[:], ACT.Copy).then_inc(acc_free[a % 3], 1)
                elif kind == "vna":
                    t, c = args
                    act.activation(v_na[:, t, 256 * c:256 * c + 256], ps[:, 0:256], ACT.Copy).then_inc(acc_free[a % 3], 1)
                elif kind == "qmem":
                    act.activation(q_mem[:, args[0], :], ps[:], ACT.Copy, scale=MEM_DIM ** -0.5).then_inc(acc_free[a % 3], 1)
                elif kind in ("cq", "ckv"):
                    i = args[0]
                    if kind == "ckv":
                        act.wait_ge(acc_done, acc_at["ssq", "q"] + 1)
                    act.activation(square[i][:], ps[:], ACT.Square).then_inc(sq_ready, 1)
                    dst = c_q if kind == "cq" else c_kv
                    act.activation(dst[:, i, :], ps[:], ACT.Copy).then_inc(acc_free[a % 3], 1)
                elif kind == "ssq":
                    width = Q_RANK if args[0] == "q" else KV_RANK
                    if args[0] == "kv":
                        act.wait_ge(latent_ready, 3)
                    act.activation(rms_root[:], ps[:], ACT.Sqrt, scale=1.0 / width, bias=eps_col[:]).then_inc(acc_free[a % 3], 1)
                elif kind == "kpe":
                    act.activation(k_pe[NOPE:MLA_QK, :], ps[NOPE:MLA_QK, :], ACT.Copy, scale=MLA_QK ** -0.5).then_inc(acc_free[a % 3], 1)
                elif kind == "uq":
                    act.activation(q_mla[0:NOPE, args[0], :], ps[0:NOPE, :], ACT.Copy).then_inc(hi_done, 1)
                    n_hi += 1
                elif kind == "uk":
                    act.activation(k_mla[0:NOPE, args[0], :], ps[0:NOPE, :], ACT.Copy, scale=MLA_QK ** -0.5).then_inc(acc_free[a % 3], 1)
                elif kind == "vmla":
                    act.activation(v_mla[:, args[0], :], ps[:], ACT.Copy).then_inc(acc_free[a % 3], 1)
                elif kind == "o":
                    i = args[1]
                    if n_copy >= 4:
                        act.wait_ge(gate_used, n_copy - 3)
                    act.activation(branch_o[i][:], ps[:], ACT.Copy).then_inc(acc_free[a % 3], 1)
                    n_copy += 1
                elif kind == "gate":
                    if n_gate >= 2:
                        act.wait_ge(gate_used, n_gate - 1)
                    act.activation(gate_s[n_gate % 2][:], ps[:], ACT.Sigmoid).then_inc(acc_free[a % 3], 1)
                    n_gate += 1
                    br_n, d, _ = args
                    if br_n == 2:
                        act.wait_ge(merged_lo, d)
                        act.wait_ge(gate_used, n_gate)
                        act.activation(m_hi[:, d, :], merged[:, d, :], ACT.Copy).then_inc(merged_hi, 1)
            act.wait_ge(hsum_ready, 1)
            act.activation(stat[:, 20:20 + TB], stat[:, 16:16 + TB], ACT.Sqrt, scale=1.0 / D, bias=eps_col[:]).then_inc(hroot_done, 1)
            act.wait_ge(routed, KB)
            act.activation(logit_t[:], bank[3][0:N_EXP, :], ACT.Copy).then_inc(logit_ready, 1)
            act.wait_ge(soft_in, 1)
            act.activation(aff[:], aff[:], ACT.Exp).then_inc(soft_exp, 1)
            with act.Fori(0, PAIRS) as j:
                for i in range(2):
                    e = 2 * j + i
                    act.wait_ge(gate_mm, e + 1)
                    act.activation(silu_s[:], bank[0][:], ACT.Sigmoid).then_inc(sig_ready, 1)
                    act.wait_ge(hid_tr, e + 1)
                    act.activation(hidden_t[:], bank[5][:].rearrange("p (c n) -> p c n", c=4), ACT.Copy).then_inc(hid_t_ready, 1)
                    act.wait_ge(down_mm, e + 1)
                    act.activation(ye_hi[i][:], bank[4][:], ACT.Copy, scale=slot_gain[:, bass.ds(e, 1)]).then_inc(y_hi_ready, 1)
            for t in range(TB):
                act.wait_ge(summed, 2 * TB * (PAIRS - 1) + 2 * (t + 1))
                act.activation(junk_b[:], h_tok[:, t, :], ACT.Square, accum_out=stat[:, 32 + t:33 + t]).then_inc(fin_sq, 1)
                act.wait_ge(fin_sq, t + 1)
                act.activation(stat[:, 36 + t:37 + t], stat[:, 32 + t:33 + t], ACT.Sqrt, scale=1.0 / D, bias=eps_col[:]).then_inc(fin_root, 1)

        @block.tensor
        def _(pe):
            pe.wait_ge(gains_in, 80)
            pe.wait_ge(ident_ready, 1)
            pe.transpose(TR[0][:, 0:GAIN_ROWS], gain_rows[:], ident[0:GAIN_ROWS, 0:GAIN_ROWS]).then_inc(gain_ps, 1)

            def passes(n_k, ps, lhs, rhs, done=None):
                for k in range(n_k):
                    (l_hi, l_lo), (r_hi, r_lo) = lhs(k), rhs(k)
                    pe.matmul(ps, l_hi, r_hi, start=(k == 0), stop=False)
                    pe.matmul(ps, l_hi, r_lo, start=False, stop=False)
                    last = pe.matmul(ps, l_lo, r_hi, start=False, stop=(k == n_k - 1))
                last.then_inc(acc_done, 1)

            def attention(br):
                us, ub = units_of(br), unit_base[br]
                groups = us[-1][0] + 1
                ng = len(us) // groups

                def scores(i):
                    u = ub + i
                    g, qb, hp = us[i]
                    if u >= 3:
                        pe.wait_ge(exp_done, u - 2)
                    rows = slice(P * qb, P * qb + P)
                    if br == "na":
                        kts = key_tiles(qb)
                        part = slice(NA_DIM * hp, NA_DIM * hp + NA_DIM)
                        pe.matmul(SC[u % 3][:, 0:P * len(kts)], q_na[part, g, rows], k_na[part, g, P * kts[0]:P * (kts[-1] + 1)],
                                  start=True, stop=True).then_inc(score_done, 1)
                    elif br == "mem":
                        for h in range(2):
                            last = pe.matmul(SC[u % 3][:, 256 * h:256 * h + 256], q_mem[:, 2 * g + h, rows], k_mem[:, 2 * g + h, :],
                                             start=True, stop=True)
                        last.then_inc(score_done, 1)
                    else:
                        pe.matmul(SC[u % 3][:], q_mla[:, 2 * g + hp, rows], k_mla[:, 2 * g + hp, :],
                                  start=True, stop=True).then_inc(score_done, 1)

                def turn(i):
                    u = ub + i
                    pe.wait_ge(p_ready, u + 1)
                    if u >= 2:
                        pe.wait_ge(pt_done[u % 2], (u - 2) // 2 + 1)
                    nk = width_of(br, us[i][1]) // P
                    for j in range(nk):
                        last = pe.transpose(TR[u % 2][:, P * j:P * j + P], probs[u % 3][:, P * j:P * j + P], ident[:])
                    last.then_inc(t_done, 1)

                def values(g):
                    u_end = ub + ng * (g + 1)
                    pe.wait_ge(pt_done[0], (u_end + 1) // 2)
                    pe.wait_ge(pt_done[1], u_end // 2)
                    buf = probs_t[(group_base[br] + g) % 2]
                    a = y_acc[br, g]
                    if br == "mem":
                        for hp in range(2):
                            wait_acc_bank(pe, a + hp)
                            for m in range(MB):
                                last = pe.matmul(ACC[(a + hp) % 3][:], v_mem[:, m, P * (2 * g + hp):P * (2 * g + hp) + P], buf[:, hp, m, :],
                                                 start=(m == 0), stop=(m == MB - 1))
                            last.then_inc(acc_done, 1)
                        return
                    wait_acc_bank(pe, a)
                    ps = ACC[a % 3]
                    v = v_na if br == "na" else v_mla
                    for qb in (range(TB) if br == "na" else [None]):
                        kts = range(TB) if qb is None else key_tiles(qb)
                        cols = slice(0, S) if qb is None else slice(P * qb, P * qb + P)
                        for j, kt in enumerate(kts):
                            for hp in range(2):
                                c0 = P * g + 64 * hp
                                last = pe.matmul(ps[64 * hp:64 * hp + 64, cols], v[:, kt, c0:c0 + 64], buf[:, hp, j, cols],
                                                 start=(j == 0), stop=(j == len(kts) - 1))
                    last.then_inc(acc_done, 1)

                scores(0)
                scores(1)
                for i in range(len(us)):
                    if i + 2 < len(us):
                        scores(i + 2)
                    turn(i)
                    if i % ng == 0 and i > 0:
                        values(i // ng - 1)
                values(groups - 1)

            for n, st in enumerate(steps):
                if st[0] in ("end", "latent"):
                    continue
                if st[0] == "turn_h":
                    kb = st[1]
                    wait_read(pe, acc_at["out", TB - 1, kb // 2] + 1)
                    if kb >= 2:
                        pe.wait_ge(hnt_ready, kb - 1)
                    for t in range(TB):
                        last = pe.transpose(TR[kb % 2][:, P * t:P * t + P], h_tok[:, t, P * kb:P * kb + P], ident[:])
                    last.then_inc(hnt_ps, 1)
                    continue
                if st[0] == "route":
                    kb = st[1]
                    pe.wait_ge(route_in, 16)
                    pe.wait_ge(hnt_ready, kb + 1)
                    pe.matmul(bank[3][0:N_EXP, :], route_w[:, kb, :], hn_t[kb % 2][:], start=(kb == 0), stop=(kb == KB - 1)).then_inc(routed, 1)
                    continue
                if st[0] == "attn":
                    if st[1] == "na":
                        wait_read(pe, y_acc["na", 0])
                        pe.wait_ge(table_ready, 1)
                    if st[1] == "mla":
                        wait_read(pe, y_acc["mla", 0])
                        pe.wait_ge(kpe_spread, MLA_HEADS)
                    attention(st[1])
                    continue
                kind, args, j = st[1:]
                a = acc_of[n]
                ps = ACC[a % 3]
                wait_acc_bank(pe, a)
                if j is not None:
                    pe.wait_ge(w_lo_ready, j + 1)
                    wh, wl = w_view(w_hi[j % 2], j), w_view(w_lo[j % 2], j)

                def w_cols(c0, c):
                    return lambda k: (wh[:, k, c0:c0 + c], wl[:, k, c0:c0 + c])

                if kind in ("memT", "nT"):
                    kb, = args
                    tok, cnt = (mem_tok, MB) if kind == "memT" else (x_tok, TB)
                    pe.wait_ge(xn_ready, MB if kind == "memT" else MB + TB)
                    for t in range(cnt):
                        last = pe.transpose(ps[:, P * t:P * t + P], tok[:, t, P * kb:P * kb + P], ident[:])
                    last.then_inc(acc_done, 1)
                    continue
                if kind == "ssq":
                    cnt = 3 if args[0] == "q" else 2
                    pe.wait_ge(sq_ready, 3 if args[0] == "q" else 5)
                    for i in range(cnt):
                        last = pe.matmul(ps[:], ones[:], square[i][:], start=(i == 0), stop=(i == cnt - 1))
                    last.then_inc(acc_done, 1)
                    continue
                nt = lambda k: (nt_hi[:, k, :], nt_lo[:, k, :])
                if (kind, args) == ("kmem", (0, 0)):
                    wait_read(pe, 2 * KB)
                if kind == "kmem":
                    passes(KB, ps[:, 0:N_MEM], w_cols(P * args[1], P), lambda k: (memt_hi[:, k, :], memt_lo[:, k, :]))
                elif kind == "vmem":
                    m = args[0]
                    passes(KB, ps[:, 0:256], lambda k: (memt_hi[:, k, P * m:P * m + P], memt_lo[:, k, P * m:P * m + P]), w_cols(0, 256))
                elif kind in ("qna", "kna", "cq", "ckv", "qmem"):
                    passes(KB, ps[:], w_cols(P * args[1], P), nt)
                elif kind == "gate":
                    passes(KB, ps[:], w_cols(P * args[2], P), nt)
                elif kind == "kpe":
                    passes(KB, ps[0:MLA_QK, :], w_cols(0, MLA_QK), nt)
                elif kind == "vna":
                    t = args[0]
                    passes(KB, ps[:, 0:256], lambda k: (nt_hi[:, k, P * t:P * t + P], nt_lo[:, k, P * t:P * t + P]), w_cols(0, 256))
                elif kind == "uq":
                    pe.wait_ge(latent_ready, 10)
                    passes(3, ps[0:MLA_QK, :], w_cols(MLA_QK * args[1], MLA_QK), lambda k: (cq_hi[:, k, :], cq_lo[:, k, :]))
                elif kind == "uk":
                    passes(2, ps[0:NOPE, :], w_cols((NOPE + MLA_V) * args[0], NOPE), lambda k: (ckv_hi[:, k, :], ckv_lo[:, k, :]))
                elif kind == "vmla":
                    t = args[0]
                    vh = wh.rearrange("p k (h c) -> p k h c", h=MLA_HEADS)[:, :, :, NOPE:NOPE + MLA_V]
                    vl = wl.rearrange("p k (h c) -> p k h c", h=MLA_HEADS)[:, :, :, NOPE:NOPE + MLA_V]
                    passes(2, ps[:], lambda k: (ckv_hi[:, k, P * t:P * t + P], ckv_lo[:, k, P * t:P * t + P]),
                           lambda k: (vh[:, k], vl[:, k]))
                elif kind == "o":
                    br, i = args
                    passes(4, ps[:], w_cols(P * i, P), lambda k: (y_hi[br, k][:], y_lo[br, k][:]))
                elif kind == "out":
                    t = args[0]
                    pe.wait_ge(merged_lo, KB)
                    passes(KB, ps[:, 0:256], lambda k: (m_hi[:, k, P * t:P * t + P], m_lo[:, k, P * t:P * t + P]), w_cols(0, 256))
            wait_read(pe, n_acc)
            pe.wait_ge(logit_ready, 1)
            for t in range(TB):
                last = pe.transpose(bank[1][:, N_EXP * t:N_EXP * t + N_EXP], logit_t[:, P * t:P * t + P], ident[0:N_EXP, 0:N_EXP])
            last.then_inc(logit_tok, 1)
            pe.wait_ge(aff_ready, 1)
            for t in range(TB):
                last = pe.transpose(bank[2][0:N_EXP, P * t:P * t + P], aff[:, t, :], ident[:])
            last.then_inc(aff_ps, 1)
            pe.wait_ge(top_ready, 2)
            pe.transpose(bank[3][:, 0:N_EXP], top_v[:], ident[0:N_EXP, 0:N_EXP])
            pe.transpose(bank[3][:, N_EXP:2 * N_EXP], top_f[:], ident[0:N_EXP, 0:N_EXP]).then_inc(top_ps, 1)

            def turn_rows():
                for kb in range(KB):
                    last = pe.transpose(bank[6 + kb // 4][:, P * (kb % 4):P * (kb % 4) + P], xs_cur[:, P * kb:P * kb + P], ident[:])
                last.then_inc(xs_tr, 1)

            def pair(j, more):
                pe.wait_ge(xs_t_ready, j + 1)
                for i in range(2):
                    e = 2 * j + i
                    rows = slice(CAP * i, CAP * i + CAP)
                    for m in range(2):
                        for c in range(2):
                            pe.wait_ge(gu_in[i][2 * m + c], 16 * (j + 1))
                            for k in range(4):
                                for hf in range(2):
                                    last = pe.matmul(bank[m][CAP * hf:CAP * hf + CAP, :], xs_t[:, 4 * c + k, rows],
                                                     gu_w[i][2 * m + c][:, k, HALF * hf:HALF * hf + HALF],
                                                     start=(c == 0 and k == 0), stop=(c == 1 and k == 3))
                            if c == 0:
                                last.then_inc(chunk_used, 1)
                        last.then_inc((gate_mm, up_mm)[m], 1)
                    pe.wait_ge(hid_ready, e + 1)
                    for c in range(4):
                        last = pe.transpose(bank[5][:, P * c:P * c + P], hidden[:, P * c:P * c + P], ident[:])
                    last.then_inc(hid_tr, 1)
                    if i == 0 and more:
                        pe.wait_ge(xs_in, 16 * (j + 2))
                        turn_rows()
                    pe.wait_ge(hid_t_ready, e + 1)
                    for c in range(2):
                        pe.wait_ge(down_in[c], 16 * (e + 1))
                        for k in range(4):
                            for hf in range(2):
                                last = pe.matmul(bank[4][CAP * hf:CAP * hf + CAP, :], hidden_t[:, k, CAP * c:CAP * c + CAP],
                                                 down_w[c][:, k, HALF * hf:HALF * hf + HALF],
                                                 start=(c == 0 and k == 0), stop=(c == 1 and k == 3))
                        if c == 0:
                            last.then_inc(chunk_used, 1)
                    last.then_inc(down_mm, 1)
                pe.wait_ge(y_ready, 2 * (j + 1))
                for t in range(TB):
                    if t >= 2:
                        pe.wait_ge(summed, 2 * TB * j + 2 * (t - 1))
                    for hf in range(2):
                        rows = slice(CAP * hf, CAP * hf + CAP)
                        for i in range(2):
                            for part, y in enumerate((ye_hi[i], ye_lo[i])):
                                last = pe.matmul(tok_banks(t)[hf][:], one_hot[i][rows, P * t:P * t + P], y[rows, :],
                                                 start=(i == 0 and part == 0), stop=(i == 1 and part == 1))
                    last.then_inc(comb_ps, 1)

            pe.wait_ge(xs_in, 16)
            turn_rows()
            with pe.Fori(0, PAIRS - 1) as j:
                pair(j, True)
            pair(PAIRS - 1, False)

        @block.vector
        def _(dve):
            chain = [0]

            def link(ins_):
                chain[0] += 1
                ins_.then_inc(dve_seq, 1)
                dve.wait_ge(dve_seq, chain[0])

            def split_lo(j):
                dve.wait_ge(w_hi_ready, j + 1)
                kb, n = job_shape(j)
                dve.tensor_tensor(w_lo[j % 2][:, 0:kb * n], w_raw[j % 2][:, 0:kb * n],
                                  w_hi[j % 2][:, 0:kb * n].bitcast(F32), ALU.subtract).then_inc(w_lo_ready, 1)

            def inverse(r):
                link(dve.reciprocal(r, r))

            dve.wait_ge(gain_ps, 1)
            dve.tensor_copy(gain_t[:, 0:GAIN_ROWS], TR[0][:, 0:GAIN_ROWS]).then_inc(gain_ready, 1)
            dve.wait_ge(root_done, 1)
            inverse(stat[:, 8:8 + MB + TB])
            for i in range(MB + TB):
                row = mem_tok[:, i, :] if i < MB else x_tok[:, i - MB, :]
                dve.tensor_scalar(row, row, stat[:, 8 + i:9 + i], None, ALU.mult).then_inc(xn_ready, 1)
            dve.wait_ge(gain_ready, 1)
            split_lo(0)
            split_lo(1)
            n_hi = n_gate = 0

            def minus_hi(dst, ps, hi):
                return dve.tensor_tensor(dst, ps, hi.bitcast(F32), ALU.subtract)

            def latents(c, n, g0):
                a = acc_at["ssq", "q" if c is c_q else "kv"]
                dve.wait_ge(acc_free[a % 3], a // 3 + 1)
                link(dve.reciprocal(rms_inv[:], rms_root[:]))
                for i in range(n):
                    dve.scalar_tensor_tensor(c[:, i, :], c[:, i, :], gain_t[:, g0 + i:g0 + i + 1], rms_inv[:],
                                             ALU.mult, ALU.mult).then_inc(latent_ready, 1)

            def rotate(dst, src, cos, sin):
                swap = [16 * (q // 16) + (q % 16 + 8) % 16 for q in range(32)]
                rows = slice(NOPE, MLA_QK)
                link(dve.stream_shuffle(rope_b[rows, :], src, swap))
                link(dve.tensor_tensor(rope_b[rows, :], rope_b[rows, :], sin, ALU.mult))
                link(dve.tensor_tensor(rope_a[rows, :], src, cos, ALU.mult))
                return dve.tensor_tensor(dst, rope_a[rows, :], rope_b[rows, :], ALU.add)

            for n, st in enumerate(steps):
                if st[0] in ("route", "turn_h"):
                    continue
                if st[0] == "end":
                    if st[1] + 2 < n_jobs:
                        split_lo(st[1] + 2)
                    continue
                if st[0] == "latent":
                    for i in range(5):
                        dve.wait_ge(latent_hi, i + 1)
                        dst, hi, src = ((cq_lo, cq_hi, c_q), (ckv_lo, ckv_hi, c_kv))[i // 3]
                        k = i % 3
                        dve.tensor_tensor(dst[:, k, :], src[:, k, :], hi[:, k, :].bitcast(F32), ALU.subtract).then_inc(latent_ready, 1)
                    dve.wait_ge(rope_in, 32)
                    dve.wait_ge(acc_free[acc_at["kpe",] % 3], acc_at["kpe",] // 3 + 1)
                    rotate(k_pe[NOPE:MLA_QK, :], k_pe[NOPE:MLA_QK, :], rope_cs[NOPE:MLA_QK, 0, :], rope_cs[NOPE:MLA_QK, 1, :]).then_inc(rope_ready, 1)
                    dve.wait_ge(rope_ready, 1)
                    continue
                if st[0] == "attn":
                    br = st[1]
                    us, ub = units_of(br), unit_base[br]
                    groups = us[-1][0] + 1
                    ng = len(us) // groups
                    for i in range(len(us) + 3):
                        u = ub + i
                        if i < len(us):
                            g, qb, hp = us[i]
                            dve.wait_ge(score_done, u + 1)
                            m = soft_m[:, u % 4, :]
                            if br == "na":
                                if u >= 3:
                                    dve.wait_ge(t_done, u - 2)
                                else:
                                    dve.wait_ge(acc_done, acc_at["ssq", "kv"] + 1)
                                s0, ds, ns = table_slots(qb)
                                w = P * ns
                                bias = table[:, 2 * g + hp, s0:s0 + ds * (ns - 1) + 1:ds, :]
                                link(dve.tensor_tensor(probs[u % 3][:, 0:w].rearrange("p (a b) -> p a b", a=ns),
                                                       SC[u % 3][:, 0:w].rearrange("p (a b) -> p a b", a=ns), bias, ALU.add))
                                dve.tensor_reduce(m[:, 0:1], probs[u % 3][:, 0:w], AX.X, ALU.max, negate=True).then_inc(max_done, 1)
                            elif br == "mem":
                                dve.tensor_reduce(m, SC[u % 3][:].rearrange("p (a b) -> p a b", a=2), AX.X, ALU.max, negate=True).then_inc(max_done, 1)
                            else:
                                dve.tensor_reduce(m[:, 0:1], SC[u % 3][:], AX.X, ALU.max, negate=True).then_inc(max_done, 1)
                        k = i - 1
                        if 0 <= k < len(us):
                            v = ub + k
                            dve.wait_ge(exp_done, v + 1)
                            w = width_of(br, us[k][1])
                            nh = 2 if br == "mem" else 1
                            link(dve.reciprocal(soft_r[:, v % 4, 0:nh], soft_s[:, v % 4, 0:nh]))
                            for hp in range(nh):
                                part = slice(256 * hp, 256 * hp + 256) if nh == 2 else slice(0, w)
                                last = dve.tensor_scalar(probs[v % 3][:, part], probs[v % 3][:, part], soft_r[:, v % 4, hp:hp + 1], None, ALU.mult)
                            last.then_inc(p_ready, 1)
                        k = i - 2
                        if 0 <= k < len(us) and (ub + k) % 2 == 1:
                            probs_out(dve, ub, us, br, k, 1)
                        g, r = divmod(i - 2, ng)
                        if r == 0 and g >= 1:
                            for hp in range(2 if br == "mem" else 1):
                                a = y_acc[br, g - 1] + hp
                                n_hi += 1
                                dve.wait_ge(hi_done, n_hi)
                                minus_hi(y_part(y_lo, br, g - 1, hp)[:], ACC[a % 3][:], y_part(y_hi, br, g - 1, hp)[:]).then_inc(acc_free[a % 3], 1)
                    continue
                kind, args = st[1], st[2]
                a = acc_of[n]
                ps = ACC[a % 3]
                if kind in ("memT", "nT"):
                    kb, = args
                    n_hi += 1
                    dve.wait_ge(hi_done, n_hi)
                    if kind == "memT":
                        dst, src, hi, g0 = memt_lo[:, kb, :], ps[:, 0:N_MEM], memt_hi[:, kb, :], G_MEM
                    else:
                        dst, src, hi, g0 = nt_lo[:, kb, :], ps[:], nt_hi[:, kb, :], G_MIX
                    dve.scalar_tensor_tensor(dst, src, gain_t[:, g0 + kb:g0 + kb + 1], hi.bitcast(F32),
                                             ALU.mult, ALU.subtract).then_inc(acc_free[a % 3], 1)
                elif kind == "ssq":
                    if args[0] == "q":
                        latents(c_q, 3, G_Q)
                    else:
                        latents(c_kv, 2, G_KV)
                elif kind == "uq":
                    n_hi += 1
                    dve.wait_ge(hi_done, n_hi)
                    rotate(q_mla[NOPE:MLA_QK, args[0], :], ps[NOPE:MLA_QK, :], rope_cs[NOPE:MLA_QK, 0, :],
                           rope_cs[NOPE:MLA_QK, 1, :]).then_inc(acc_free[a % 3], 1)
                    dve.wait_ge(acc_free[a % 3], a // 3 + 1)
                elif kind == "gate":
                    br_n, d, _ = args
                    i = n_gate % 4
                    dve.wait_ge(acc_free[a % 3], a // 3 + 1)
                    if br_n == 0:
                        dve.tensor_tensor(merged[:, d, :], branch_o[i][:], gate_s[n_gate % 2][:], ALU.mult).then_inc(gate_used, 1)
                    else:
                        link(dve.tensor_tensor(branch_o[i][:], branch_o[i][:], gate_s[n_gate % 2][:], ALU.mult))
                        dve.tensor_tensor(merged[:, d, :], merged[:, d, :], branch_o[i][:], ALU.add).then_inc(gate_used, 1)
                    n_gate += 1
                    dve.wait_ge(gate_used, n_gate)
                    if br_n == 2:
                        dve.wait_ge(merged_hi, d + 1)
                        dve.tensor_tensor(m_lo[:, d, :], merged[:, d, :], m_hi[:, d, :].bitcast(F32), ALU.subtract).then_inc(merged_lo, 1)
                elif kind == "out":
                    t, c = args
                    dve.wait_ge(acc_done, a + 1)
                    dve.wait_ge(resid_in, 16 * TB)
                    cols = slice(256 * c, 256 * c + 256)
                    dve.tensor_tensor(h_tok[:, t, cols], ps[:, 0:256], h_tok[:, t, cols], ALU.add).then_inc(acc_free[a % 3], 1)
            dve.wait_ge(hsq_done, 4 * TB)
            dve.tensor_reduce(stat[:, 16:16 + TB], h_part[:], AX.X, ALU.add).then_inc(hsum_ready, 1)
            dve.wait_ge(hroot_done, 1)
            inverse(stat[:, 20:20 + TB])
            for t in range(TB):
                dve.tensor_scalar(hr_tok[:, t, :], h_tok[:, t, :], stat[:, 20 + t:21 + t], None, ALU.mult).then_inc(hr_ready, 1)
            dve.wait_ge(bias_in, 16)
            dve.wait_ge(logit_tok, 1)
            for t in range(TB):
                last = dve.scalar_tensor_tensor(aff[:, t, :], bank[1][:, N_EXP * t:N_EXP * t + N_EXP], stat[:, 20 + t:21 + t], route_b[:],
                                                ALU.mult, ALU.add)
            link(last)
            link(dve.tensor_reduce(row_stat[:, 0, :], aff[:], AX.X, ALU.max))
            dve.tensor_tensor(aff[:], aff[:], row_stat[:, 0, :].unsqueeze(2).broadcast_to([P, TB, N_EXP]), ALU.subtract).then_inc(soft_in, 1)
            dve.wait_ge(soft_exp, 1)
            link(dve.tensor_reduce(row_stat[:, 1, :], aff[:], AX.X, ALU.add))
            link(dve.reciprocal(row_stat[:, 2, :], row_stat[:, 1, :]))
            dve.tensor_tensor(aff[:], aff[:], row_stat[:, 2, :].unsqueeze(2).broadcast_to([P, TB, N_EXP]), ALU.mult).then_inc(aff_ready, 1)
            dve.wait_ge(aff_ps, 1)
            link(dve.tensor_copy(aff_t[:], bank[2][0:N_EXP, :]))
            for r in range(CAP // 8):
                v8, i8 = top_v[:, 8 * r:8 * r + 8], top_i[:, 8 * r:8 * r + 8]
                link(dve.max(v8, aff_t[:]))
                link(dve.max_index(i8, v8, aff_t[:]))
                link(dve.match_replace(aff_t[:], v8, aff_t[:], -1.0))
            for r in range(2):
                last = dve.tensor_copy(top_f[:, CAP * r:CAP * r + CAP], top_i[:])
            last.then_inc(top_ready, 1)
            dve.tensor_copy(top_v[:, CAP:2 * CAP], top_v[:, 0:CAP]).then_inc(top_ready, 1)
            dve.wait_ge(top_ps, 1)
            dve.tensor_copy(slot_gain[:], bank[3][:, 0:N_EXP])
            dve.tensor_copy(slot_id[:], bank[3][:, N_EXP:2 * N_EXP])
            for i in range(2):
                last = dve.tensor_copy(slot_tok[CAP * i:CAP * i + CAP, :], bank[3][CAP * i:CAP * i + CAP, N_EXP + i:2 * N_EXP:2])
            last.then_inc(slots_ready, 1)

            def gained_rows():
                for b in range(2):
                    g4 = gain_t[:, G_FFN + 4 * b:G_FFN + 4 * b + 4].unsqueeze(2).broadcast_to([P, 4, P])
                    last = dve.tensor_tensor(xs_t[:, 4 * b:4 * b + 4, :], bank[6 + b][:].rearrange("p (k n) -> p k n", k=4), g4, ALU.mult)
                last.then_inc(xs_t_ready, 1)

            def pair(j, more):
                for i in range(2):
                    e = 2 * j + i
                    dve.wait_ge(sig_ready, e + 1)
                    dve.tensor_tensor(hidden[:], silu_s[:], bank[0][:], ALU.mult).then_inc(silu_ready, 1)
                    dve.wait_ge(silu_ready, e + 1)
                    dve.wait_ge(up_mm, e + 1)
                    dve.tensor_tensor(hidden[:], hidden[:], bank[1][:], ALU.mult).then_inc(hid_ready, 1)
                    dve.tensor_scalar(one_hot[i][:], tok_row[:], slot_id[:, bass.ds(e, 1)], None, ALU.is_equal).then_inc(hot_ready, 1)
                    if i == 1 and more:
                        dve.wait_ge(xs_tr, j + 2)
                        gained_rows()
                    dve.wait_ge(y_hi_ready, e + 1)
                    dve.scalar_tensor_tensor(ye_lo[i][:], bank[4][:], slot_gain[:, bass.ds(e, 1)], ye_hi[i][:].bitcast(F32),
                                             ALU.mult, ALU.subtract).then_inc(y_ready, 1)
                for t in range(TB):
                    dve.wait_ge(comb_ps, TB * j + (t + 1))
                    for hf in range(2):
                        cols = slice(HALF * hf, HALF * hf + HALF)
                        dve.tensor_tensor(h_tok[:, t, cols], tok_banks(t)[hf][:], h_tok[:, t, cols], ALU.add).then_inc(summed, 1)

            dve.wait_ge(tok_ready, 1)
            dve.wait_ge(xs_tr, 1)
            gained_rows()
            with dve.Fori(0, PAIRS - 1) as j:
                pair(j, True)
            pair(PAIRS - 1, False)
            dve.wait_ge(fin_g_in, 16)
            for t in range(TB):
                dve.wait_ge(fin_root, t + 1)
                link(dve.reciprocal(stat[:, 40 + t:41 + t], stat[:, 36 + t:37 + t]))
                dve.scalar_tensor_tensor(h_tok[:, t, :], h_tok[:, t, :], stat[:, 40 + t:41 + t], fin_g[:], ALU.mult, ALU.mult).then_inc(fin_ready, 1)


INPUTS = ["x", "mem", "g_mix", "w_in", "na_rpb", "mla_q_norm", "w_mla_uq", "mla_kv_norm", "w_mla_ukv", "g_mem",
          "w_mem_kv", "w_o_na", "w_o_mla", "w_o_mem", "w_out", "g_ffn", "w_router", "b_router", "w_gate", "w_up",
          "w_down", "g_final"]


def shape_constants():
    t = np.arange(S)
    col, row = t // ROWS, t % ROWS
    d = ROPE // 2
    inv = (ROPE_BASE ** (-np.arange(0, d, 2, dtype=np.float32) / d)).astype(np.float32)
    cos, sin = np.zeros((ROPE, S), np.float32), np.zeros((ROPE, S), np.float32)
    for part, pos in enumerate((row, col)):
        ang = (pos.astype(np.float32)[None, :] * inv[:, None]).astype(np.float32)
        r0 = d * part
        cos[r0:r0 + d // 2] = cos[r0 + d // 2:r0 + d] = np.cos(ang)
        sin[r0:r0 + d // 2] = -np.sin(ang)
        sin[r0 + d // 2:r0 + d] = np.sin(ang)
    return {"rope_cos": cos, "rope_sin": sin}


def kernel(**inputs):
    import concourse.bacc as bacc
    from concourse.bass_utils import run_bass_kernel_spmd

    nc = bacc.Bacc("TRN2", target_bir_lowering=False, num_devices=1)
    arrays, aps = {}, {}
    given = {name: np.ascontiguousarray(inputs[name]) for name in INPUTS}
    given.update(shape_constants())
    for name, a in given.items():
        arrays[f"in_{name}"] = a
        aps[name] = nc.dram_tensor(f"in_{name}", a.shape, mybir.dt.from_np(a.dtype), kind="ExternalInput").ap()
    out = nc.dram_tensor("out", (1, S, D), F32, kind="ExternalOutput").ap()
    build(nc, aps, out)
    return run_bass_kernel_spmd(nc, [arrays], core_ids=[0]).results[0]["out"]
```

```python
from contextlib import ExitStack

import numpy as np

import concourse.bass as bass
from concourse import mybir

F32 = mybir.dt.float32
F32R = mybir.dt.float32r
U32 = mybir.dt.uint32
ACT = mybir.ActivationFunctionType
ALU = mybir.AluOpType
AX = mybir.AxisListType

P = 128
D = 1024
S = 512
GRID_W = 64
ROWS = S // GRID_W
N_MEM = 256
EPS = 1e-6
NA_HEADS, NA_DIM = 8, 64
WIN_R, WIN_C = 8, 16
MLA_HEADS, NOPE, ROPE, MLA_V = 8, 64, 32, 64
Q_RANK, KV_RANK = 384, 256
ROPE_BASE = 10000.0
MEM_HEADS, MEM_DIM = 4, 128
N_EXP, FF = 16, 1024
CAP = 2 * S // N_EXP
NA_W = NA_HEADS * NA_DIM
MEM_W = MEM_HEADS * MEM_DIM
MLA_QK = NOPE + ROPE
KB = D // P
TB = S // P
MB = N_MEM // P
PAIRS = N_EXP // 2
HALF = D // 2
C_Q, C_K, C_V = 0, NA_W, 2 * NA_W
C_CQ = 3 * NA_W
C_CKV = C_CQ + Q_RANK
C_KR = C_CKV + KV_RANK
C_QM = C_KR + ROPE
C_GATE = C_QM + MEM_W
MASKED = -1.0e30
QUARTERS = 4
NORM_PARTS = 4

G_MIX, G_MEM, G_Q, G_KV, G_FFN = 0, KB, 2 * KB, 2 * KB + 3, 2 * KB + 5
GAIN_ROWS = 3 * KB + 5

COLS_PER_TILE = P // ROWS
RPB_R, RPB_C = 2 * WIN_R - 1, 2 * WIN_C - 1
TOEP_U = 3 * COLS_PER_TILE
RPB_PITCH, RPB_PAD = 64, 16
RPB_BUF = ROWS * NA_HEADS * ROWS * RPB_PITCH

SLOT_FIRST, SLOT_PREV, SLOT_MID, SLOT_NEXT, SLOT_LAST = range(5)
SLOTS = [(SLOT_FIRST, 0, True, False), (SLOT_PREV, -1, True, False), (SLOT_MID, 0, True, True),
         (SLOT_NEXT, 1, False, True), (SLOT_LAST, 0, False, True)]


def key_tiles(qb):
    return list(range(max(qb - 1, 0), min(qb + 1, TB - 1) + 1))


def table_slots(qb):
    if qb == 0:
        return SLOT_FIRST, SLOT_NEXT - SLOT_FIRST, 2
    if qb == TB - 1:
        return SLOT_PREV, SLOT_LAST - SLOT_PREV, 2
    return SLOT_PREV, 1, 3


def plan():
    jobs, steps = [], []

    def job(src, c0, n, kb):
        jobs.append((src, c0, n, kb))
        return len(jobs) - 1

    def tile(kind, args, j=None):
        steps.append(("tile", kind, args, j, 0))

    def pieces(kind, args, j, n_k, n):
        cuts = list(range(0, n_k, n))
        return ([[("part", kind, args, j, k, k + n)] for k in cuts[:-1]]
                + [[("tile", kind, args, j, cuts[-1])]])

    def weave(phase, numbers, fillers):
        n = 0
        for i, u in enumerate(numbers):
            steps.append(("unit", u, phase))
            end = len(fillers) * (i + 1) // len(numbers)
            for f in fillers[n:end]:
                steps.extend(f)
            n = end
            steps.append(("turn", u, phase))

    steps += [("rms", "mem"), ("split", 0, 0, QUARTERS)]
    for kb in range(KB):
        tile("memT", (kb,))
    steps += [("split", 1, 0, QUARTERS), ("rms", "x")]
    for c in range(2):
        j = job("mem_kv", 256 * c, 256, KB)
        for i in range(2):
            tile("kmem", (2 * c + i, i), j)
        steps.append(("end", j))
    for c in range(2):
        j = job("mem_kv", MEM_W + 256 * c, 256, KB)
        for m in range(MB):
            tile("vmem", (m, c), j)
            for kb in range(2):
                tile("nT", (2 * (MB * c + m) + kb,))
        steps.append(("end", j))
    for kind, c0 in (("qna", C_Q), ("kna", C_K)):
        for c in range(2):
            j = job("in", c0 + 256 * c, 256, KB)
            for i in range(2):
                tile(kind, (2 * c + i, i), j)
            steps.append(("end", j))
    j = job("in", C_V, 256, KB)
    for t in range(TB):
        tile("vna", (t, 0), j)
    steps.append(("end", j))
    j = job("in", C_V + 256, 256, KB)
    beside = [[("tile", "vna", (t, 1), j, 0)] for t in range(TB)]
    beside[-1].append(("end", j))
    na, mem, mla = (FIRST_UNIT[b] for b in ("na", "mem", "mla"))
    woven = []
    for c0, n in ((0, 1), (1, 2)):
        j = job("in", C_CQ + P * c0, P * n, KB)
        for i in range(n):
            woven += pieces("cq", (c0 + i, i), j, KB, 2)
        woven[-1].append(("end", j))
    for c in range(2):
        j = job("in", C_QM + 256 * c, 256, KB)
        for i in range(2):
            woven += pieces("qmem", (2 * c + i, i), j, KB, 2)
        woven[-1].append(("end", j))
    behind = 4 * 4
    woven.insert(behind, [("tile", "ssq", ("q",), None, 0)])
    for n, place in enumerate((17, 18, 19, 20, 25, 26, 27)):
        woven[place].append(("norm", "q", n))
    weave(0, range(na, mem), beside + woven)
    woven = []
    j = job("in", C_CKV, 256, KB)
    for i in range(2):
        woven += pieces("ckv", (i, i), j, KB, 2)
    woven[-1].append(("end", j))
    woven.insert(2, [("rope_load",)])
    norms = [("norm", "kv", n) for n in range(NORM_PARTS + 2)]
    j = job("in", C_KR - NOPE, MLA_QK, KB)
    key = pieces("kpe", (), j, KB, 2)
    woven += [[("tile", "ssq", ("kv",), None, 0)], norms[:1] + key[0], norms[1:3] + key[1], norms[3:] + [("latent", 0, 3)] + key[2],
              key[3] + [("end", j)]]
    weave(0, range(mem, mla + DRAIN), woven)
    steps.append(("latent", 3, 5))
    j = job("uq", 0, 4 * MLA_QK, Q_RANK // P)
    j_kv = job("ukv", 0, 1024, KV_RANK // P)
    j_q = [j, job("uq", 4 * MLA_QK, 4 * MLA_QK, Q_RANK // P)]
    for step in ("q0", "q1", "k0", "k1", "q2", "rotate", "k2", "q3", "end", "k3", "k4", "k5",
                 "q4", "q5", "k6", "q6", "q7", "k7"):
        if step == "rotate":
            steps.append(("rotate_key",))
        elif step == "end":
            steps.append(("end", j_q[0]))
        elif step[0] == "q":
            h = int(step[1])
            tile("uq", (h, h % 4), j_q[h // 4])
        else:
            tile("uk", (int(step[1]),), j_kv)
    woven = [[("tile", "vmla", (t,), j_kv, 0)] for t in range(TB)]
    woven[-1] += [("end", j_kv), ("end", j_q[1])]
    weave(1, range(mla, mla + COPY_LAG), woven)
    weave(1, range(mla + COPY_LAG, len(UNITS) + DRAIN), [])
    for n, (br, wo) in enumerate(((0, "o_na"), (2, "o_mem"), (1, "o_mla"))):
        for half in range(2):
            j = job(wo, 512 * half, 512, 4)
            for i in range(4):
                tile("o", (br, i), j)
            steps.append(("end", j))
            for c in range(2):
                j = job("in", C_GATE + br * D + 512 * half + 256 * c, 256, KB)
                for i in range(2):
                    tile("gate", (n, 4 * half + 2 * c + i, i), j)
                steps.append(("end", j))
    for c in range(4):
        j = job("out", 256 * c, 256, KB)
        for t in range(TB):
            tile("out", (t, c), j)
        steps.append(("end", j))
        for kb in range(2 * c - 4, 2 * c - 2):
            if kb >= 0:
                steps.append(("route", kb))
        for kb in range(2 * c - 2, 2 * c):
            if kb >= 0:
                steps.append(("turn_h", kb))
    for kb in (4, 5):
        steps.append(("route", kb))
    for kb in (6, 7):
        steps.append(("turn_h", kb))
    for kb in (6, 7):
        steps.append(("route", kb))
    ordered, queued = [], []
    for n, st in enumerate(steps):
        if st[0] == "end":
            ordered += queued
            queued = []
            if st[1] + 2 < len(jobs):
                if any(later[0] == "unit" for later in steps[n + 1:n + 6]):
                    queued = [("split", st[1] + 2, q, q + 1) for q in range(QUARTERS)]
                else:
                    ordered.append(("split", st[1] + 2, 0, QUARTERS))
            continue
        if queued and (st[0] == "latent" or st[0] in ("tile", "part") and st[3] == queued[0][1]):
            ordered += queued
            queued = []
        ordered.append(st)
        if queued and st[0] == "unit":
            ordered.append(queued.pop(0))
    steps = ordered
    return jobs, steps


def units_of(branch):
    if branch == "mem":
        return [(branch, g, qb, None) for g in range(2) for qb in range(TB)]
    return [(branch, g, qb, hp) for g in range(4) for qb in range(TB) for hp in range(2)]


UNITS, FIRST_UNIT, GROUPS = [], {}, []
for _br in ("na", "mem", "mla"):
    FIRST_UNIT[_br] = len(UNITS)
    UNITS += units_of(_br)
    _n = 4 if _br == "mem" else 8
    GROUPS += [(_br, g, u, u + _n) for g, u in enumerate(range(FIRST_UNIT[_br], len(UNITS), _n))]
NORM_LAG, TURN_LAG, COPY_LAG, VALUE_LAG, OUT_LAG = 1, 2, 3, 4, 5
DRAIN = OUT_LAG


PHASES = [(0, FIRST_UNIT["mla"]), (FIRST_UNIT["mla"], len(UNITS))]


def unit_at(step, lag=0):
    _, i, phase = step
    first, end = PHASES[phase]
    return i - lag if first <= i - lag < end else None


def group_ending(step, lag):
    u = unit_at(step, lag)
    return next((n for n, g in enumerate(GROUPS) if u is not None and g[3] - 1 == u), None)


def copier(u):
    return int(u % 8 == 7)


def copies_until(u, which):
    return sum(copier(v) == which for v in range(u))


def group_of(u):
    return next(n for n, g in enumerate(GROUPS) if g[2] <= u < g[3])


def width_of(branch, qb):
    return P * len(key_tiles(qb)) if branch == "na" else S


def build(nc, ins, out):
    jobs, steps = plan()
    n_jobs = len(jobs)

    acc_of, part_acc, y_acc, bank_of = {}, {}, {}, {}
    n_acc = 0
    banks = [0, 1, 2]
    open_tile, open_y = None, None
    for n, st in enumerate(steps):
        if st[0] in ("tile", "part"):
            if st[4] == 0:
                open_tile = (banks.pop(0), [])
            open_tile[1].append(n)
            if st[0] == "tile":
                acc_of[n] = n_acc
                part_acc.update((m, n_acc) for m in open_tile[1])
                bank_of[n_acc] = open_tile[0]
                banks.append(open_tile[0])
                n_acc += 1
        elif st[0] == "turn" and unit_at(st, VALUE_LAG) is not None:
            u = unit_at(st, VALUE_LAG)
            br, _, qb, hp = UNITS[u]
            if br == "mem":
                if qb == TB - 1:
                    y_acc[group_of(u)] = n_acc
                    for _ in range(2):
                        bank_of[n_acc] = banks.pop(0)
                        banks.append(bank_of[n_acc])
                        n_acc += 1
            elif hp == 1:
                if qb == 0:
                    open_y = banks.pop(0)
                if qb == TB - 1:
                    y_acc[group_of(u)] = n_acc
                    bank_of[n_acc] = open_y
                    banks.append(open_y)
                    n_acc += 1
    use_of = {a: sum(bank_of[b] == bank_of[a] for b in range(a)) for a in range(n_acc)}

    def uses_until(b, n):
        return sum(bank_of[a] == b for a in range(n))

    acc_at = {}
    for n, st in enumerate(steps):
        if st[0] == "tile":
            acc_at[(st[1],) + st[2]] = acc_of[n]
    job_end = {st[3]: acc_of[n] + 1 for n, st in enumerate(steps) if st[0] == "tile" and st[3] is not None}
    last_gate = max(a for k, a in acc_at.items() if k[0] == "gate")
    n_phase = [y_acc[5] + 2, y_acc[9] + 1]

    with ExitStack() as ctx:
        base = -(-nc.sbuf_base // 64) * 64

        def at(name, shape, off, dt=F32):
            return nc.alloc_sbuf_tensor_at(name, shape, dt, offset=base + off)

        K = 1024
        nt_hi = at("nt_hi", [P, KB, S], 0, F32R)
        nt_lo = at("nt_lo", [P, KB, S], 16 * K, F32R)
        w_raw = [at(f"w_raw{i}", [P, 2048], (32 + 8 * i) * K) for i in range(2)]
        w_hi = [at(f"w_hi{i}", [P, 2048], (48 + 16 * i) * K, F32R) for i in range(2)]
        w_lo = [at(f"w_lo{i}", [P, 2048], (56 + 16 * i) * K, F32R) for i in range(2)]
        q_na = at("q_na", [P, 4, S], 80 * K)
        k_na = at("k_na", [P, 4, S], 88 * K)
        q_mem = at("q_mem", [P, 4, S], 96 * K)
        toep = at("toep", [P, NA_HEADS, ROWS, TOEP_U], 96 * K)
        v_na = at("v_na", [P, TB, NA_W], 112 * K)
        table = at("table", [P, NA_HEADS, 5, P], 120 * K)
        k_mem = at("k_mem", [P, MEM_HEADS, N_MEM], 140 * K)
        v_mem = at("v_mem", [P, MB, MEM_W], 144 * K)
        memt_hi = at("memt_hi", [P, KB, N_MEM], 148 * K, F32R)
        memt_lo = at("memt_lo", [P, KB, N_MEM], 156 * K, F32R)
        c_q = at("c_q", [P, 3, S], 156 * K)
        c_kv = at("c_kv", [P, 2, S], 162 * K)
        k_pe = at("k_pe", [P, S], 166 * K)
        x_tok = at("x_tok", [P, TB, D], 168 * K)
        mem_tok = at("mem_tok", [P, MB, D], 184 * K)
        junk = at("junk", [P, D], 192 * K)
        rpb_zeros = at("rpb_zeros", [P, RPB_BUF // P], 204 * K)
        rms_root = at("rms_root", [P, S], 154 * K)
        probs_t = [at(f"probs_t{i}", [P, 2, TB, S], (168 + 16 * i) * K) for i in range(2)]
        cq_hi = at("cq_hi", [P, 3, S], 168 * K, F32R)
        cq_lo = at("cq_lo", [P, 3, S], 174 * K, F32R)
        ckv_hi = at("ckv_hi", [P, 2, S], 180 * K, F32R)
        ckv_lo = at("ckv_lo", [P, 2, S], 184 * K, F32R)
        q_mla = at("q_mla", [MLA_QK, MLA_HEADS, S], 120 * K)
        k_mla = at("k_mla", [MLA_QK, MLA_HEADS, S], 140 * K)
        v_mla = at("v_mla", [P, TB, MLA_HEADS * MLA_V], 112 * K)
        rope_cs = at("rope_cs", [MLA_QK, 2, S], 136 * K)
        probs = [at(f"probs{i}", [P, S], (200 + 2 * i) * K) for i in range(3)]
        square = [at(f"square{i}", [P, S], (148 + 2 * i) * K) for i in range(3)]
        rope_a = at("rope_a", [MLA_QK, S], 112 * K)
        rope_b = at("rope_b", [MLA_QK, S], 114 * K)
        y_hi, y_lo = {}, {}
        for g in range(4):
            y_hi[0, g] = at(f"y_na_hi{g}", [P, S], (80 + 2 * g) * K, F32R)
            y_lo[0, g] = at(f"y_na_lo{g}", [P, S], (88 + 2 * g) * K, F32R)
            y_hi[2, g] = at(f"y_mem_hi{g}", [P, S], (96 + 2 * g) * K, F32R)
            y_lo[2, g] = at(f"y_mem_lo{g}", [P, S], (104 + 2 * g) * K, F32R)
            y_hi[1, g] = at(f"y_mla_hi{g}", [P, S], (120 + 4 * g) * K, F32R)
            y_lo[1, g] = at(f"y_mla_lo{g}", [P, S], (140 + 4 * g) * K, F32R)
        merged = at("merged", [P, KB, S], 176 * K)
        branch_o = [at(f"branch_o{i}", [P, S], (192 + 2 * i) * K) for i in range(4)]
        gate_s = [at(f"gate_s{i}", [P, S], (200 + 2 * i) * K) for i in range(2)]
        m_hi = at("m_hi", [P, KB, S], 80 * K, F32R)
        m_lo = at("m_lo", [P, KB, S], 176 * K, F32R)
        h_tok = at("h_tok", [P, TB, D], 0)
        hn_t = [at(f"hn_t{i}", [P, S], (192 + 2 * i) * K) for i in range(2)]
        route_w = at("route_w", [P, KB, N_EXP], 200 * K)
        junk_h = at("junk_h", [P, 256], 201 * K)
        hr_tok = at("hr_tok", [P, TB, D], 80 * K)
        logit_t = at("logit_t", [N_EXP, S], 196 * K)
        aff_t = at("aff_t", [N_EXP, S], 198 * K)
        R = 176 * K
        aff = at("aff", [P, TB, N_EXP], R)
        top_v = at("top_v", [N_EXP, P], R + 256)
        top_i = at("top_i", [N_EXP, CAP], R + 768, U32)
        top_f = at("top_f", [N_EXP, P], R + 1024)
        slot_gain = at("slot_gain", [P, N_EXP], R + 1536)
        slot_id = at("slot_id", [P, N_EXP], R + 1600)
        slot_tok = at("slot_tok", [P, PAIRS], R + 1664, U32)
        row_stat = at("row_stat", [P, 4, TB], R + 1728)
        gu_w = [[at(f"gu_w{i}{c}", [P, 4, FF], off * K) for c, off in enumerate(offs)]
                for i, offs in enumerate(((16, 112, 128, 144), (96, 48, 64, 80)))]
        down_w = [at(f"down_w{c}", [P, 4, D], off * K) for c, off in enumerate((160, 32))]
        xs_cur = at("xs_cur", [P, D], 178 * K)
        xs_t = at("xs_t", [P, KB, P], 182 * K)
        hidden_t = at("hidden_t", [P, 4, P], 186 * K)
        silu_s = at("silu_s", [P, 512], 188 * K)
        hidden = at("hidden", [P, 512], 190 * K)
        ye_hi = at("ye_hi", [P, HALF], 192 * K, F32R)
        ye_lo = at("ye_lo", [P, HALF], 194 * K, F32R)
        one_hot = at("one_hot", [P, S], 196 * K, F32R)
        tok_row = at("tok_row", [P, S], 204 * K)
        tok_int = at("tok_int", [P, S], 202 * K, mybir.dt.int32)
        fin_g = at("fin_g", [P, D], 178 * K)
        junk_b = at("junk_b", [P, D], 186 * K)
        SM = 206 * K
        ident = at("ident", [P, P], SM)
        ones = at("ones", [P, P], SM + 512)
        gain_t = at("gain_t", [P, 32], SM + 1024)
        stat = at("stat", [P, 64], SM + 1152)
        soft_m = at("soft_m", [P, 4, 2], SM + 1408)
        soft_s = at("soft_s", [P, 4, 2], SM + 1440)
        soft_r = at("soft_r", [P, 4, 2], SM + 1472)
        h_part = at("h_part", [P, TB, 4], SM + 1152 + 96)
        eps_col = at("eps_col", [P, 1], SM + 1504)
        route_b = at("route_b", [P, N_EXP], SM + 1536)
        gain_rows = at("gain_rows", [GAIN_ROWS, P], 200 * K)

        bank = [ctx.enter_context(nc.psum_tensor(f"bank{i}", [P, 512], F32)) for i in range(8)]
        ACC, SC, TR = bank[0:3], bank[3:6], bank[6:8]

        rpb_rows = nc.dram_tensor("rpb_rows", (ROWS, NA_HEADS * ROWS, RPB_PITCH), F32, kind="Internal").ap()
        hn_rows = nc.dram_tensor("hn_rows", (S, D), F32, kind="Internal").ap()

        def sem(name):
            return ctx.enter_context(nc.semaphore(name))

        gains_in, rpb_zeroed, rpb_in, toep_in = (sem(x) for x in ("gains_in", "rpb_zeroed", "rpb_in", "toep_in"))
        mem_in = [sem(f"mem_in{m}") for m in range(MB)]
        x_in = [sem(f"x_in{t}") for t in range(TB)]
        rope_in, bias_in, resid_in, route_in = (sem(x) for x in ("rope_in", "bias_in", "resid_in", "route_in"))
        raw_in = [sem(f"raw_in{i}") for i in range(2)]
        w_hi_ready, w_lo_ready = sem("w_hi_ready"), sem("w_lo_ready")
        const_ready, zeros_ready, ident_ready, table_ready, pool_seq = (sem(x) for x in ("const_ready", "zeros_ready", "ident_ready", "table_ready", "pool_seq"))
        gain_ps, gain_ready = sem("gain_ps"), sem("gain_ready")
        sumsq_done, root_done, xn_ready = sem("sumsq_done"), sem("root_done"), sem("xn_ready")
        acc_done = sem("acc_done")
        acc_free = [sem(f"acc_free{i}") for i in range(3)]
        hi_done = sem("hi_done")
        sq_ready, latent_hi = sem("sq_ready"), sem("latent_hi")
        latent_ready, rope_ready, kpe_spread = sem("latent_ready"), sem("rope_ready"), sem("kpe_spread")
        score_done, max_done, exp_done, p_ready, t_done = (sem(x) for x in ("score_done", "max_done", "exp_done", "p_ready", "t_done"))
        pt_done = [sem("pt_done_act"), sem("pt_done_dve")]
        silu_ready, gate_used, merged_hi, merged_lo = sem("silu_ready"), sem("gate_used"), sem("merged_hi"), sem("merged_lo")
        dve_seq = sem("dve_seq")
        hsq_done, hsum_ready, hroot_done, hr_ready, hr_stored = (sem(x) for x in ("hsq_done", "hsum_ready", "hroot_done", "hr_ready", "hr_stored"))
        hnt_ps, hnt_ready, routed, tok_ready = sem("hnt_ps"), sem("hnt_ready"), sem("routed"), sem("tok_ready")
        logit_ready, logit_tok, soft_in, soft_exp, aff_ready, aff_ps, top_ready, top_ps, slots_ready = (
            sem(x) for x in ("logit_ready", "logit_tok", "soft_in", "soft_exp", "aff_ready", "aff_ps", "top_ready", "top_ps", "slots_ready"))
        xs_in, xs_tr, xs_t_ready = sem("xs_in"), sem("xs_tr"), sem("xs_t_ready")
        gu_in = [[sem(f"gu_in{i}{c}") for c in range(4)] for i in range(2)]
        down_in = [sem(f"down_in{c}") for c in range(2)]
        last_half_in, chunk_used = sem("last_half_in"), sem("chunk_used")
        gate_mm, up_mm, sig_ready, hid_ready, hid_tr, hid_t_ready, down_mm, y_hi_ready, y_ready, hot_ready, comb_ps, summed = (
            sem(x) for x in ("gate_mm", "up_mm", "sig_ready", "hid_ready", "hid_tr", "hid_t_ready", "down_mm", "y_hi_ready", "y_ready",
                             "hot_ready", "comb_ps", "summed"))
        fin_g_in, fin_sq, fin_root, fin_ready, out_done = (sem(x) for x in ("fin_g_in", "fin_sq", "fin_root", "fin_ready", "out_done"))

        w_src = {"in": ins["w_in"][0], "mem_kv": ins["w_mem_kv"][0], "uq": ins["w_mla_uq"][0],
                 "ukv": ins["w_mla_ukv"][0], "o_na": ins["w_o_na"][0], "o_mla": ins["w_o_mla"][0],
                 "o_mem": ins["w_o_mem"][0], "out": ins["w_out"][0]}
        grid = "(r c) d -> c r d"
        x_dram = ins["x"][0].rearrange(grid, r=ROWS)
        out_dram = out[0].rearrange(grid, r=ROWS)
        def job_shape(j):
            return jobs[j][3], jobs[j][2]

        def w_view(t, j):
            kb, n = job_shape(j)
            return t[:, 0:kb * n].rearrange("p (k n) -> p k n", k=kb)

        def wait_read(eng, n):
            for b in range(3):
                if uses_until(b, n) > 0:
                    eng.wait_ge(acc_free[b], uses_until(b, n))

        def wait_tile_read(eng, a):
            eng.wait_ge(acc_free[bank_of[a]], use_of[a] + 1)

        def wait_acc_bank(eng, a):
            if use_of[a] > 0:
                eng.wait_ge(acc_free[bank_of[a]], use_of[a])

        def quarters(j, q, end):
            n = jobs[j][2] * jobs[j][3] // QUARTERS
            return slice(n * q, n * end)

        def y_part(parts, br, g, hp):
            return parts[{"na": 0, "mla": 1, "mem": 2}[br], 2 * g + hp if br == "mem" else g]

        def probs_out(eng, u, which):
            br, _, qb, hp = UNITS[u]
            g = group_of(u)
            eng.wait_ge(t_done, u + 1)
            first = next(v for v in range(GROUPS[g][2], GROUPS[g][3]) if copier(v) == which)
            if u == first and GROUPS[g][:2] == ("mla", 0):
                eng.wait_ge(acc_done, acc_at["vmla", TB - 1] + 1)
            elif u == first and g >= 2:
                eng.wait_ge(acc_done, y_acc[g - 2] + (2 if GROUPS[g - 2][0] == "mem" else 1))
            buf = probs_t[g % 2]
            cols = slice(P * qb, P * qb + P)
            if br == "mem":
                dst = buf[:, :, 0:2, cols]
                src = TR[u % 2][:].rearrange("p (a b n) -> p a b n", a=2, b=2)
            else:
                nk = width_of(br, qb) // P
                dst = buf[:, hp, 0:nk, cols]
                src = TR[u % 2][:, 0:nk * P].rearrange("p (b n) -> p b n", b=nk)
            if which == 0:
                eng.activation(dst, src, ACT.Copy).then_inc(pt_done[0], 1)
            else:
                eng.tensor_copy(dst, src).then_inc(pt_done[1], 1)

        def tok_banks(e, t):
            if isinstance(e, int) and e == N_EXP - 1 and t >= 2:
                return (bank[0], bank[1]) if t == 2 else (bank[5], bank[4])
            return (bank[2], bank[3]) if t % 2 == 0 else (bank[6], bank[7])

        block = ctx.enter_context(nc.Block())

        @block.sync
        def _(sp):
            def load_job(j):
                src, c0, n, kb = jobs[j]
                if j >= 2:
                    sp.wait_ge(w_lo_ready, QUARTERS * (j - 1))
                sp.dma_start(w_view(w_raw[j % 2], j),
                             w_src[src][:, c0:c0 + n].rearrange("(k p) n -> p k n", p=P)).then_inc(raw_in[j % 2], 16)

            for m in range(MB):
                sp.dma_start(mem_tok[:, m, :], ins["mem"][0, P * m:P * m + P, :]).then_inc(mem_in[m], 16)
            load_job(0)
            for row, name, n in ((G_MIX, "g_mix", KB), (G_MEM, "g_mem", KB), (G_Q, "mla_q_norm", 3),
                                 (G_KV, "mla_kv_norm", 2), (G_FFN, "g_ffn", KB)):
                sp.dma_start(gain_rows[row:row + n, :], ins[name][0].rearrange("(k p) -> k p", p=P)).then_inc(gains_in, 16)
            for t in range(TB):
                sp.dma_start(x_tok[:, t, :], x_dram[COLS_PER_TILE * t:COLS_PER_TILE * (t + 1)]).then_inc(x_in[t], 16)
            load_job(1)
            sp.wait_ge(rpb_zeroed, 16)
            for r in range(ROWS):
                src = bass.AP(tensor=ins["na_rpb"].tensor, offset=(WIN_R - 1 - r) * RPB_C,
                              ap=[[RPB_R * RPB_C, NA_HEADS], [RPB_C, ROWS], [1, RPB_C]])
                sp.dma_start(rpb_rows[r, :, RPB_PAD:RPB_PAD + RPB_C].rearrange("(h k) n -> h k n", h=NA_HEADS), src).then_inc(rpb_in, 16)
            load_job(2)
            sp.wait_ge(rpb_in, 16 * ROWS)
            for c in range(COLS_PER_TILE):
                src = bass.AP(tensor=rpb_rows.tensor, offset=RPB_PAD - 1 - c,
                              ap=[[NA_HEADS * ROWS * RPB_PITCH, ROWS], [RPB_PITCH, NA_HEADS * ROWS], [1, TOEP_U]])
                sp.dma_start(toep[ROWS * c:ROWS * (c + 1)].rearrange("p h k u -> p (h k) u"), src).then_inc(toep_in, 16)
                if c == COLS_PER_TILE // 2 - 1:
                    load_job(3)
            sp.dma_start(route_b[:], ins["b_router"][0].partition_broadcast(P)).then_inc(bias_in, 16)
            def load_gate_up(e, i, c):
                src = ins[("w_gate", "w_up")[c // 2]][0, e, (c % 2) * 512:(c % 2 + 1) * 512, :]
                sp.dma_start(gu_w[i][c][:], src.rearrange("(k p) n -> p k n", p=P)).then_inc(gu_in[i][c], 16)

            def load_down(e, c):
                src = ins["w_down"][0, e, c * 512:(c + 1) * 512, :]
                sp.dma_start(down_w[c][:], src.rearrange("(k p) n -> p k n", p=P)).then_inc(down_in[c], 16)

            out_job = next(j for j in range(n_jobs) if jobs[j][0] == "out")
            for j in range(4, n_jobs):
                if j == out_job + 2:
                    sp.wait_ge(acc_done, last_gate + 1)
                    sp.wait_ge(gate_used, 3 * KB)
                    for t in range(TB):
                        sp.dma_start(h_tok[:, t, :], x_dram[COLS_PER_TILE * t:COLS_PER_TILE * (t + 1)]).then_inc(resid_in, 16)
                    sp.dma_start(route_w[:], ins["w_router"][0].rearrange("(k p) e -> p k e", p=P)).then_inc(route_in, 16)
                load_job(j)

            sp.wait_ge(merged_lo, KB)
            for c in range(4):
                load_gate_up(0, 0, c)
            load_down(0, 0)
            load_gate_up(1, 1, 0)
            sp.wait_ge(w_lo_ready, QUARTERS * n_jobs)
            load_down(0, 1)
            sp.wait_ge(acc_done, job_end[n_jobs - 2])
            load_gate_up(1, 1, 1 + n_jobs % 2)
            for t in range(TB):
                sp.wait_ge(hr_ready, t + 1)
                sp.dma_start(hn_rows[P * t:P * t + P, :], hr_tok[:, t, :]).then_inc(hr_stored, 16)
            load_gate_up(1, 1, 2 - n_jobs % 2)
            sp.wait_ge(hr_stored, 16 * TB)
            load_gate_up(1, 1, 3)
            def next_gate_up(j, i, m):
                sp.wait_ge(chunk_used, 6 * j + (3 * i - 5 + m))
                load_gate_up(2 * j + i, i, 2 * m)
                sp.wait_ge((gate_mm, up_mm)[m], 2 * j + (i - 1))
                load_gate_up(2 * j + i, i, 2 * m + 1)

            def next_down(j, i):
                sp.wait_ge(chunk_used, 6 * j + 3 * i)
                load_down(2 * j + i, 0)
                sp.wait_ge(down_mm, 2 * j + i)
                load_down(2 * j + i, 1)

            next_gate_up(1, 0, 0)
            next_gate_up(1, 0, 1)
            next_down(0, 1)
            next_gate_up(1, 1, 0)
            next_gate_up(1, 1, 1)
            next_down(1, 0)
            with sp.Fori(2, PAIRS) as j:
                next_gate_up(j, 0, 0)
                next_down(j - 1, 1)
                next_gate_up(j, 0, 1)
                next_down(j, 0)
                next_gate_up(j, 1, 0)
                next_gate_up(j, 1, 1)
            sp.wait_ge(chunk_used, 3 * (N_EXP - 1))
            load_down(N_EXP - 1, 0)
            sp.wait_ge(down_mm, N_EXP - 1)
            src = ins["w_down"][0, N_EXP - 1, 512:1024, :].rearrange("(k p) n -> p k n", p=P)
            sp.dma_start(down_w[1][:, 0:2], src[:, 0:2]).then_inc(down_in[1], 16)
            sp.dma_start(down_w[1][:, 2:4], src[:, 2:4]).then_inc(last_half_in, 16)
            sp.wait_ge(xs_tr, 2 * PAIRS)
            sp.dma_start(fin_g[:], ins["g_final"].partition_broadcast(P)).then_inc(fin_g_in, 16)
            for t in range(TB):
                sp.wait_ge(fin_ready, t + 1)
                sp.dma_start(out_dram[COLS_PER_TILE * t:COLS_PER_TILE * (t + 1)], h_tok[:, t, :]).then_inc(out_done, 16)
            sp.wait_ge(out_done, 16 * TB)

        @block.gpsimd
        def _(pool):
            pool.memset(rpb_zeros[:], 0.0).then_inc(zeros_ready, 1)
            pool.memset(ones[:], 1.0).then_inc(const_ready, 1)
            pool.memset(eps_col[:], EPS).then_inc(const_ready, 1)
            pool.memset(ident[:], 0.0).then_inc(pool_seq, 1)
            pool.wait_ge(pool_seq, 1)
            pool.affine_select(out=ident[:], in_=ident[:], compare_op=ALU.not_equal, fill=1.0, base=0,
                               pattern=[[-1, P]], channel_multiplier=1).then_inc(ident_ready, 1)
            pool.wait_ge(toep_in, 16 * COLS_PER_TILE)
            seq = 1
            for slot, dt, _, _ in SLOTS:
                u0 = COLS_PER_TILE * (dt + 1)
                pool.tensor_copy(table[:, :, slot, :].rearrange("p h (c r) -> p h c r", r=ROWS),
                                 toep[:, :, :, u0:u0 + COLS_PER_TILE].rearrange("p h r c -> p h c r")).then_inc(pool_seq, 1)
                seq += 1
            for slot, dt, lower, upper in SLOTS:
                part = table[:, :, slot, :].rearrange("p h (c r) -> p h c r", r=ROWS)
                for sign, on in ((1, lower), (-1, upper)):
                    if not on:
                        continue
                    pool.wait_ge(pool_seq, seq)
                    b = P * dt + ROWS * (WIN_C // 2) + ROWS - 1 if sign == 1 else -P * dt + ROWS * (WIN_C // 2 - 1)
                    pool.affine_select(out=part, in_=part, compare_op=ALU.is_ge, fill=MASKED, base=b,
                                       pattern=[[0, NA_HEADS], [sign * ROWS, COLS_PER_TILE], [0, ROWS]],
                                       channel_multiplier=-sign).then_inc(pool_seq, 1)
                    seq += 1
            pool.wait_ge(pool_seq, seq)
            pool.memset(stat[0:1, 60:61], 0.0).then_inc(table_ready, 1)
            pool.wait_ge(rope_ready, 1)
            pool.wait_ge(exp_done, FIRST_UNIT["mla"])
            pool.wait_ge(acc_done, n_phase[0])
            for h in range(MLA_HEADS):
                pool.tensor_copy(k_mla[NOPE:MLA_QK, h, :], k_pe[NOPE:MLA_QK, :]).then_inc(kpe_spread, 1)
            pool.wait_ge(gate_used, 3 * KB)
            pool.iota(tok_int[:], pattern=[[1, S]], base=0, channel_multiplier=0).then_inc(pool_seq, 1)
            pool.wait_ge(pool_seq, seq + 1)
            pool.tensor_copy(tok_row[:], tok_int[:]).then_inc(tok_ready, 1)
            pool.wait_ge(hr_stored, 16 * TB)
            pool.wait_ge(slots_ready, 1)
            for j in range(PAIRS):
                if j > 0:
                    pool.wait_ge(xs_tr, 2 * j)
                pool.indirect_dma_start(out=xs_cur[:], out_offset=None, in_=hn_rows[:, :],
                                        in_offset=bass.IndirectOffsetOnAxis(ap=slot_tok[:, j:j + 1], axis=0)).then_inc(xs_in, 16)

        @block.scalar
        def _(act):
            def split_hi(j, q, end):
                if q == 0:
                    act.wait_ge(raw_in[j % 2], 16 * (j // 2 + 1))
                    if j >= 2:
                        act.wait_ge(acc_done, job_end[j - 2])
                part = quarters(j, q, end)
                act.activation(w_hi[j % 2][:, part], w_raw[j % 2][:, part], ACT.Copy).then_inc(w_hi_ready, end - q)

            def root_table(n):
                act.activation(stat[:, 61 + n:62 + n], eps_col[:], ACT.Sqrt)

            def rms(which):
                tok, loaded, s0, cnt = (mem_tok, mem_in, 0, MB) if which == "mem" else (x_tok, x_in, MB, TB)
                for t in range(cnt):
                    act.wait_ge(loaded[t], 16)
                    if s0 + t > 0:
                        act.wait_ge(sumsq_done, s0 + t)
                    act.activation(junk[:], tok[:, t, :], ACT.Square, accum_out=stat[:, s0 + t:s0 + t + 1]).then_inc(sumsq_done, 1)
                act.wait_ge(sumsq_done, s0 + cnt)
                act.activation(stat[:, 8 + s0:8 + s0 + cnt], stat[:, s0:s0 + cnt], ACT.Sqrt, scale=1.0 / D, bias=eps_col[:]).then_inc(root_done, 1)

            act.wait_ge(const_ready, 2)
            root_table(0)
            act.wait_ge(zeros_ready, 1)
            act.dma_start(rpb_rows.rearrange("a b n -> (a b n)").rearrange("(p n) -> p n", p=P), rpb_zeros[:]).then_inc(rpb_zeroed, 16)
            n_hi = n_copy = n_out = n_gate = 0
            for n, st in enumerate(steps):
                if st[0] == "split":
                    split_hi(*st[1:])
                    continue
                if st[0] == "rms":
                    rms(st[1])
                    continue
                if st[0] == "rope_load":
                    act.wait_ge(max_done, FIRST_UNIT["mem"])
                    act.dma_start(rope_cs[NOPE:MLA_QK, 0, :], ins["rope_cos"]).then_inc(rope_in, 16)
                    act.dma_start(rope_cs[NOPE:MLA_QK, 1, :], ins["rope_sin"]).then_inc(rope_in, 16)
                    continue
                if st[0] == "latent":
                    act.wait_ge(latent_ready, 5)
                    act.wait_ge(acc_done, n_phase[0] if st[2] == 5 else y_acc[4] + 2)
                    for i in range(st[1], st[2]):
                        dst, src = (cq_hi[:, i, :], c_q[:, i, :]) if i < 3 else (ckv_hi[:, i - 3, :], c_kv[:, i - 3, :])
                        act.activation(dst, src, ACT.Copy).then_inc(latent_hi, 1)
                    continue
                if st[0] in ("turn", "route", "part", "rotate_key", "norm"):
                    continue
                if st[0] == "turn_h":
                    kb = st[1]
                    act.wait_ge(hnt_ps, kb + 1)
                    if kb >= 2:
                        act.wait_ge(routed, kb - 1)
                    act.activation(hn_t[kb % 2][:], TR[kb % 2][:], ACT.Copy, scale=gain_t[:, G_FFN + kb:G_FFN + kb + 1]).then_inc(hnt_ready, 1)
                    continue
                if st[0] == "unit":
                    u = unit_at(st, COPY_LAG)
                    if u is not None and copier(u) == 0:
                        probs_out(act, u, 0)
                    u = unit_at(st)
                    if u is not None:
                        br, _, qb, _ = UNITS[u]
                        act.wait_ge(max_done, u + 1)
                        if u >= 3:
                            act.wait_ge(t_done, u - 2)
                        w = width_of(br, qb)
                        src = probs[u % 3] if br == "na" else SC[u % 3]
                        if br == "mem":
                            for hp in range(2):
                                part = slice(256 * hp, 256 * hp + 256)
                                last = act.activation(probs[u % 3][:, part], src[:, part], ACT.Exp, bias=soft_m[:, u % 4, hp:hp + 1],
                                                      accum_out=soft_s[:, u % 4, hp:hp + 1])
                            last.then_inc(exp_done, 1)
                        else:
                            act.activation(probs[u % 3][:, 0:w], src[:, 0:w], ACT.Exp, bias=soft_m[:, u % 4, 0:1],
                                           accum_out=soft_s[:, u % 4, 0:1]).then_inc(exp_done, 1)
                    g = group_ending(st, OUT_LAG)
                    if g is not None:
                        br = GROUPS[g][0]
                        for hp in range(2 if br == "mem" else 1):
                            a = y_acc[g] + hp
                            act.wait_ge(acc_done, a + 1)
                            act.activation(y_part(y_hi, br, GROUPS[g][1], hp)[:], ACC[bank_of[a]][:], ACT.Copy).then_inc(hi_done, 1)
                            n_hi += 1
                    continue
                kind, args = st[1], st[2]
                a = acc_of[n]
                ps = ACC[bank_of[a]]
                if kind == "out":
                    t, c = args
                    act.wait_ge(acc_free[bank_of[a]], use_of[a] + 1)
                    if n_out > 0:
                        act.wait_ge(hsq_done, n_out)
                    n_out += 1
                    act.activation(junk_h[:], h_tok[:, t, 256 * c:256 * c + 256], ACT.Square,
                                   accum_out=h_part[:, t, c:c + 1]).then_inc(hsq_done, 1)
                    continue
                if (kind, args) == ("uk", (0,)):
                    act.wait_ge(acc_done, n_phase[0])
                if (kind, args) == ("vmla", (0,)):
                    wait_read(act, acc_at["uq", MLA_HEADS - 1, 3] + 1)
                act.wait_ge(acc_done, a + 1)
                if kind in ("memT", "nT"):
                    kb, = args
                    act.wait_ge(gain_ready, 1)
                    if kind == "memT":
                        act.activation(memt_hi[:, kb, :], ps[:, 0:N_MEM], ACT.Copy, scale=gain_t[:, G_MEM + kb:G_MEM + kb + 1]).then_inc(hi_done, 1)
                    else:
                        act.activation(nt_hi[:, kb, :], ps[:], ACT.Copy, scale=gain_t[:, G_MIX + kb:G_MIX + kb + 1]).then_inc(hi_done, 1)
                    n_hi += 1
                elif kind == "kmem":
                    act.activation(k_mem[:, args[0], :], ps[:, 0:N_MEM], ACT.Copy).then_inc(acc_free[bank_of[a]], 1)
                elif kind == "vmem":
                    m, c = args
                    act.activation(v_mem[:, m, 256 * c:256 * c + 256], ps[:, 0:256], ACT.Copy).then_inc(acc_free[bank_of[a]], 1)
                elif kind == "qna":
                    act.activation(q_na[:, args[0], :], ps[:], ACT.Copy, scale=NA_DIM ** -0.5).then_inc(acc_free[bank_of[a]], 1)
                elif kind == "kna":
                    act.activation(k_na[:, args[0], :], ps[:], ACT.Copy).then_inc(acc_free[bank_of[a]], 1)
                elif kind == "vna":
                    t, c = args
                    act.wait_ge(table_ready, 1)
                    act.activation(v_na[:, t, 256 * c:256 * c + 256], ps[:, 0:256], ACT.Copy).then_inc(acc_free[bank_of[a]], 1)
                elif kind == "qmem":
                    act.activation(q_mem[:, args[0], :], ps[:], ACT.Copy, scale=MEM_DIM ** -0.5).then_inc(acc_free[bank_of[a]], 1)
                elif kind in ("cq", "ckv"):
                    i = args[0]
                    if kind == "ckv":
                        act.wait_ge(acc_done, acc_at["ssq", "q"] + 1)
                    act.activation(square[i][:], ps[:], ACT.Square).then_inc(sq_ready, 1)
                    dst = c_q if kind == "cq" else c_kv
                    act.activation(dst[:, i, :], ps[:], ACT.Copy).then_inc(acc_free[bank_of[a]], 1)
                elif kind == "ssq":
                    width = Q_RANK if args[0] == "q" else KV_RANK
                    if args[0] == "kv":
                        act.wait_ge(latent_ready, 3)
                    act.activation(rms_root[:], ps[:], ACT.Sqrt, scale=1.0 / width, bias=eps_col[:]).then_inc(acc_free[bank_of[a]], 1)
                elif kind == "kpe":
                    act.activation(k_pe[NOPE:MLA_QK, :], ps[NOPE:MLA_QK, :], ACT.Copy, scale=MLA_QK ** -0.5).then_inc(acc_free[bank_of[a]], 1)
                elif kind == "uq":
                    act.activation(q_mla[0:NOPE, args[0], :], ps[0:NOPE, :], ACT.Copy).then_inc(hi_done, 1)
                    n_hi += 1
                elif kind == "uk":
                    act.activation(k_mla[0:NOPE, args[0], :], ps[0:NOPE, :], ACT.Copy, scale=MLA_QK ** -0.5).then_inc(acc_free[bank_of[a]], 1)
                elif kind == "vmla":
                    act.activation(v_mla[:, args[0], :], ps[:], ACT.Copy).then_inc(acc_free[bank_of[a]], 1)
                elif kind == "o":
                    i = args[1]
                    if n_copy >= 4:
                        act.wait_ge(gate_used, n_copy - 3)
                    act.activation(branch_o[i][:], ps[:], ACT.Copy).then_inc(acc_free[bank_of[a]], 1)
                    n_copy += 1
                elif kind == "gate":
                    if n_gate >= 2:
                        act.wait_ge(gate_used, n_gate - 1)
                    act.activation(gate_s[n_gate % 2][:], ps[:], ACT.Sigmoid).then_inc(acc_free[bank_of[a]], 1)
                    n_gate += 1
                    if n_gate == 3 * KB:
                        root_table(1)
                    br_n, d, _ = args
                    if br_n == 2:
                        act.wait_ge(merged_lo, d)
                        act.wait_ge(gate_used, n_gate)
                        act.activation(m_hi[:, d, :], merged[:, d, :], ACT.Copy).then_inc(merged_hi, 1)
            act.wait_ge(hsum_ready, 1)
            act.activation(stat[:, 20:20 + TB], stat[:, 16:16 + TB], ACT.Sqrt, scale=1.0 / D, bias=eps_col[:]).then_inc(hroot_done, 1)
            act.wait_ge(routed, KB)
            act.activation(logit_t[:], bank[3][0:N_EXP, :], ACT.Copy).then_inc(logit_ready, 1)
            act.wait_ge(soft_in, 1)
            act.activation(aff[:], aff[:], ACT.Exp).then_inc(soft_exp, 1)
            with act.Fori(0, PAIRS) as j:
                for i in range(2):
                    e = 2 * j + i
                    act.wait_ge(gate_mm, e + 1)
                    act.activation(silu_s[:], bank[0][:], ACT.Sigmoid).then_inc(sig_ready, 1)
                    act.wait_ge(hid_tr, e + 1)
                    act.activation(hidden_t[:], bank[5][:].rearrange("p (c n) -> p c n", c=4), ACT.Copy).then_inc(hid_t_ready, 1)
                    act.wait_ge(down_mm, e + 1)
                    act.activation(ye_hi[:], bank[4][:], ACT.Copy, scale=slot_gain[:, bass.ds(e, 1)]).then_inc(y_hi_ready, 1)
            root_table(2)
            for t in range(TB):
                act.wait_ge(summed, 2 * TB * (N_EXP - 1) + 2 * (t + 1))
                act.activation(junk_b[:], h_tok[:, t, :], ACT.Square, accum_out=stat[:, 32 + t:33 + t]).then_inc(fin_sq, 1)
                act.wait_ge(fin_sq, t + 1)
                act.activation(stat[:, 36 + t:37 + t], stat[:, 32 + t:33 + t], ACT.Sqrt, scale=1.0 / D, bias=eps_col[:]).then_inc(fin_root, 1)

        @block.tensor
        def _(pe):
            pe.wait_ge(gains_in, 80)
            pe.wait_ge(ident_ready, 1)
            pe.transpose(TR[0][:, 0:GAIN_ROWS], gain_rows[:], ident[0:GAIN_ROWS, 0:GAIN_ROWS]).then_inc(gain_ps, 1)

            def passes(n_k, ps, lhs, rhs, k0=0, end=None):
                for k in range(k0, n_k if end is None else end):
                    (l_hi, l_lo), (r_hi, r_lo) = lhs(k), rhs(k)
                    pe.matmul(ps, l_hi, r_hi, start=(k == 0), stop=False)
                    pe.matmul(ps, l_hi, r_lo, start=False, stop=False)
                    last = pe.matmul(ps, l_lo, r_hi, start=False, stop=(k == n_k - 1))
                if end is None:
                    last.then_inc(acc_done, 1)

            def scores(u):
                br, g, qb, hp = UNITS[u]
                if u >= 3:
                    pe.wait_ge(exp_done, u - 2)
                rows = slice(P * qb, P * qb + P)
                if br == "na":
                    kts = key_tiles(qb)
                    part = slice(NA_DIM * hp, NA_DIM * hp + NA_DIM)
                    pe.matmul(SC[u % 3][:, 0:P * len(kts)], q_na[part, g, rows], k_na[part, g, P * kts[0]:P * (kts[-1] + 1)],
                              start=True, stop=True).then_inc(score_done, 1)
                elif br == "mem":
                    for h in range(2):
                        last = pe.matmul(SC[u % 3][:, 256 * h:256 * h + 256], q_mem[:, 2 * g + h, rows], k_mem[:, 2 * g + h, :],
                                         start=True, stop=True)
                    last.then_inc(score_done, 1)
                else:
                    pe.matmul(SC[u % 3][:], q_mla[:, 2 * g + hp, rows], k_mla[:, 2 * g + hp, :],
                              start=True, stop=True).then_inc(score_done, 1)

            def turn(u):
                pe.wait_ge(p_ready, u + 1)
                if u >= 2:
                    pe.wait_ge(pt_done[copier(u - 2)], copies_until(u - 1, copier(u - 2)))
                for j in range(width_of(UNITS[u][0], UNITS[u][2]) // P):
                    last = pe.transpose(TR[u % 2][:, P * j:P * j + P], probs[u % 3][:, P * j:P * j + P], ident[:])
                last.then_inc(t_done, 1)

            def values(u):
                br, g, qb, hp = UNITS[u]
                n = group_of(u)
                if br == "mem" and qb < TB - 1 or hp == 0:
                    return
                if u == 1:
                    wait_tile_read(pe, acc_at["vna", TB - 1, 1])
                for which in range(2):
                    pe.wait_ge(pt_done[which], copies_until(u + 1, which))
                buf = probs_t[n % 2]
                a = y_acc[n]
                if br == "mem":
                    for hp in range(2):
                        wait_acc_bank(pe, a + hp)
                        for m in range(MB):
                            last = pe.matmul(ACC[bank_of[a + hp]][:], v_mem[:, m, P * (2 * g + hp):P * (2 * g + hp) + P], buf[:, hp, m, :],
                                             start=(m == 0), stop=(m == MB - 1))
                        last.then_inc(acc_done, 1)
                    return
                if qb == 0:
                    wait_acc_bank(pe, a)
                ps = ACC[bank_of[a]]
                v = v_na if br == "na" else v_mla
                kts = key_tiles(qb) if br == "na" else range(TB)
                cols = slice(P * qb, P * qb + P)
                for j, kt in enumerate(kts):
                    for hp in range(2):
                        c0 = P * g + 64 * hp
                        last = pe.matmul(ps[64 * hp:64 * hp + 64, cols], v[:, kt, c0:c0 + 64], buf[:, hp, j, cols],
                                         start=(j == 0), stop=(j == len(kts) - 1))
                if qb == TB - 1:
                    last.then_inc(acc_done, 1)

            for n, st in enumerate(steps):
                if st[0] in ("split", "rms", "latent", "rotate_key", "norm", "rope_load"):
                    continue
                if st[0] == "turn_h":
                    kb = st[1]
                    wait_read(pe, acc_at["out", TB - 1, kb // 2] + 1)
                    if kb >= 2:
                        pe.wait_ge(hnt_ready, kb - 1)
                    for t in range(TB):
                        last = pe.transpose(TR[kb % 2][:, P * t:P * t + P], h_tok[:, t, P * kb:P * kb + P], ident[:])
                    last.then_inc(hnt_ps, 1)
                    continue
                if st[0] == "route":
                    kb = st[1]
                    pe.wait_ge(route_in, 16)
                    pe.wait_ge(hnt_ready, kb + 1)
                    pe.matmul(bank[3][0:N_EXP, :], route_w[:, kb, :], hn_t[kb % 2][:], start=(kb == 0), stop=(kb == KB - 1)).then_inc(routed, 1)
                    continue
                if st[0] == "unit":
                    u = unit_at(st)
                    if u is not None:
                        if u == FIRST_UNIT["na"]:
                            wait_tile_read(pe, acc_at["kna", 3, 1])
                            pe.wait_ge(table_ready, 1)
                        if u == FIRST_UNIT["mem"]:
                            wait_tile_read(pe, acc_at["qmem", 3, 1])
                        if u == FIRST_UNIT["mla"]:
                            pe.wait_ge(kpe_spread, MLA_HEADS)
                        if u >= FIRST_UNIT["mla"] and u == GROUPS[group_of(u)][2]:
                            h = 2 * UNITS[u][1] + 1
                            wait_read(pe, max(acc_at["uq", h, h % 4], acc_at["uk", h]) + 1)
                        if UNITS[u][0] != "na":
                            scores(u)
                        elif UNITS[u][3] == 0:
                            scores(u)
                            scores(u + 1)
                    continue
                if st[0] == "turn":
                    u = unit_at(st, TURN_LAG)
                    if u is not None:
                        turn(u)
                    u = unit_at(st, VALUE_LAG)
                    if u is not None:
                        values(u)
                    continue
                kind, args, j, k0 = st[1:5]
                end = st[5] if st[0] == "part" else None
                a = part_acc[n] if st[0] == "part" else acc_of[n]
                ps = ACC[bank_of[a]]
                if k0 == 0:
                    wait_acc_bank(pe, a)
                if j is not None:
                    pe.wait_ge(w_lo_ready, QUARTERS * (j + 1))
                    wh, wl = w_view(w_hi[j % 2], j), w_view(w_lo[j % 2], j)

                def w_cols(c0, c):
                    return lambda k: (wh[:, k, c0:c0 + c], wl[:, k, c0:c0 + c])

                if kind in ("memT", "nT"):
                    kb, = args
                    tok, cnt = (mem_tok, MB) if kind == "memT" else (x_tok, TB)
                    pe.wait_ge(xn_ready, MB if kind == "memT" else MB + TB)
                    for t in range(cnt):
                        last = pe.transpose(ps[:, P * t:P * t + P], tok[:, t, P * kb:P * kb + P], ident[:])
                    last.then_inc(acc_done, 1)
                    continue
                if kind == "ssq":
                    cnt = 3 if args[0] == "q" else 2
                    pe.wait_ge(sq_ready, 3 if args[0] == "q" else 5)
                    for i in range(cnt):
                        last = pe.matmul(ps[:], ones[:], square[i][:], start=(i == 0), stop=(i == cnt - 1))
                    last.then_inc(acc_done, 1)
                    continue
                nt = lambda k: (nt_hi[:, k, :], nt_lo[:, k, :])
                if (kind, args) == ("kmem", (0, 0)):
                    wait_read(pe, acc_at["memT", KB - 1] + 1)
                if (kind, args) == ("qna", (0, 0)):
                    wait_read(pe, acc_at["nT", KB - 1] + 1)
                if kind == "kmem":
                    passes(KB, ps[:, 0:N_MEM], w_cols(P * args[1], P), lambda k: (memt_hi[:, k, :], memt_lo[:, k, :]))
                elif kind == "vmem":
                    m = args[0]
                    passes(KB, ps[:, 0:256], lambda k: (memt_hi[:, k, P * m:P * m + P], memt_lo[:, k, P * m:P * m + P]), w_cols(0, 256))
                elif kind in ("qna", "kna", "cq", "ckv", "qmem"):
                    passes(KB, ps[:], w_cols(P * args[1], P), nt, k0, end)
                elif kind == "gate":
                    passes(KB, ps[:], w_cols(P * args[2], P), nt)
                elif kind == "kpe":
                    passes(KB, ps[0:MLA_QK, :], w_cols(0, MLA_QK), nt, k0, end)
                elif kind == "vna":
                    t = args[0]
                    passes(KB, ps[:, 0:256], lambda k: (nt_hi[:, k, P * t:P * t + P], nt_lo[:, k, P * t:P * t + P]), w_cols(0, 256))
                elif kind == "uq":
                    pe.wait_ge(latent_ready, 8)
                    passes(3, ps[0:MLA_QK, :], w_cols(MLA_QK * args[1], MLA_QK), lambda k: (cq_hi[:, k, :], cq_lo[:, k, :]))
                elif kind == "uk":
                    pe.wait_ge(latent_ready, 10)
                    passes(2, ps[0:NOPE, :], w_cols((NOPE + MLA_V) * args[0], NOPE), lambda k: (ckv_hi[:, k, :], ckv_lo[:, k, :]))
                elif kind == "vmla":
                    t = args[0]
                    vh = wh.rearrange("p k (h c) -> p k h c", h=MLA_HEADS)[:, :, :, NOPE:NOPE + MLA_V]
                    vl = wl.rearrange("p k (h c) -> p k h c", h=MLA_HEADS)[:, :, :, NOPE:NOPE + MLA_V]
                    passes(2, ps[:], lambda k: (ckv_hi[:, k, P * t:P * t + P], ckv_lo[:, k, P * t:P * t + P]),
                           lambda k: (vh[:, k], vl[:, k]))
                elif kind == "o":
                    br, i = args
                    passes(4, ps[:], w_cols(P * i, P), lambda k: (y_hi[br, k][:], y_lo[br, k][:]))
                elif kind == "out":
                    t = args[0]
                    if args == (0, 0):
                        for k in range(KB):
                            pe.wait_ge(merged_lo, k + 1)
                            passes(KB, ps[:, 0:256], lambda k: (m_hi[:, k, 0:P], m_lo[:, k, 0:P]), w_cols(0, 256), k,
                                   k + 1 if k < KB - 1 else None)
                        continue
                    passes(KB, ps[:, 0:256], lambda k: (m_hi[:, k, P * t:P * t + P], m_lo[:, k, P * t:P * t + P]), w_cols(0, 256))
            wait_read(pe, n_acc)
            pe.wait_ge(logit_ready, 1)
            for t in range(TB):
                last = pe.transpose(bank[1][:, N_EXP * t:N_EXP * t + N_EXP], logit_t[:, P * t:P * t + P], ident[0:N_EXP, 0:N_EXP])
            last.then_inc(logit_tok, 1)
            pe.wait_ge(aff_ready, 1)
            for t in range(TB):
                last = pe.transpose(bank[2][0:N_EXP, P * t:P * t + P], aff[:, t, :], ident[:])
            last.then_inc(aff_ps, 1)
            pe.wait_ge(top_ready, 2)
            pe.transpose(bank[3][:, 0:N_EXP], top_v[:], ident[0:N_EXP, 0:N_EXP])
            pe.transpose(bank[3][:, N_EXP:2 * N_EXP], top_f[:], ident[0:N_EXP, 0:N_EXP]).then_inc(top_ps, 1)

            def turn_rows():
                for kb in range(KB):
                    last = pe.transpose(bank[6 + kb // 4][:, P * (kb % 4):P * (kb % 4) + P], xs_cur[:, P * kb:P * kb + P], ident[:])
                    if kb % 4 == 3:
                        last.then_inc(xs_tr, 1)

            def send(e, tiles):
                for t in tiles:
                    if t == 0:
                        pe.wait_ge(y_ready, e + 1)
                    if t >= 2 and tok_banks(e, t) == tok_banks(e, t - 2):
                        pe.wait_ge(summed, 2 * TB * e + 2 * (t - 1))
                    for part, y in enumerate((ye_hi, ye_lo)):
                        for hf in range(2):
                            rows = slice(CAP * hf, CAP * hf + CAP)
                            last = pe.matmul(tok_banks(e, t)[hf][:], one_hot[rows, P * t:P * t + P], y[rows, :],
                                             start=(part == 0), stop=(part == 1))
                    last.then_inc(comb_ps, 1)

            def pair(j, first=False, more=True):
                pe.wait_ge(xs_t_ready, 2 * j + 1)
                for i in range(2):
                    e = 2 * j + i
                    rows = slice(CAP * i, CAP * i + CAP)
                    before = not (first and i == 0)
                    for m in range(2):
                        for c in range(2):
                            pe.wait_ge(gu_in[i][2 * m + c], 16 * (j + 1))
                            if (i, m, c) == (0, 0, 1):
                                pe.wait_ge(xs_t_ready, 2 * j + 2)
                            for k in range(4):
                                for hf in range(2):
                                    last = pe.matmul(bank[m][CAP * hf:CAP * hf + CAP, :], xs_t[:, 4 * c + k, rows],
                                                     gu_w[i][2 * m + c][:, k, HALF * hf:HALF * hf + HALF],
                                                     start=(c == 0 and k == 0), stop=(c == 1 and k == 3))
                            if c == 0:
                                last.then_inc(chunk_used, 1)
                            if before and m == 1 and c == 0:
                                send(e - 1, (2, 3))
                        last.then_inc((gate_mm, up_mm)[m], 1)
                        if before and m == 0:
                            send(e - 1, (0, 1))
                    pe.wait_ge(hid_ready, e + 1)
                    for c in range(4):
                        last = pe.transpose(bank[5][:, P * c:P * c + P], hidden[:, P * c:P * c + P], ident[:])
                    last.then_inc(hid_tr, 1)
                    if i == 1 and more:
                        pe.wait_ge(xs_in, 16 * (j + 2))
                        turn_rows()
                    pe.wait_ge(hid_t_ready, e + 1)
                    for c in range(2):
                        pe.wait_ge(down_in[c], 16 * (e + 1))
                        for k in range(4):
                            if not more and (i, c, k) == (1, 1, 2):
                                pe.wait_ge(last_half_in, 16)
                            for hf in range(2):
                                last = pe.matmul(bank[4][CAP * hf:CAP * hf + CAP, :], hidden_t[:, k, CAP * c:CAP * c + CAP],
                                                 down_w[c][:, k, HALF * hf:HALF * hf + HALF],
                                                 start=(c == 0 and k == 0), stop=(c == 1 and k == 3))
                        if c == 0:
                            last.then_inc(chunk_used, 1)
                    last.then_inc(down_mm, 1)

            pe.wait_ge(xs_in, 16)
            turn_rows()
            pair(0, first=True)
            with pe.Fori(1, PAIRS - 1) as j:
                pair(j)
            pair(PAIRS - 1, more=False)
            send(N_EXP - 1, range(TB))

        @block.vector
        def _(dve):
            chain = [0]

            def link(ins_):
                chain[0] += 1
                ins_.then_inc(dve_seq, 1)
                dve.wait_ge(dve_seq, chain[0])

            def split_lo(j, q, end):
                dve.wait_ge(w_hi_ready, QUARTERS * j + end)
                part = quarters(j, q, end)
                dve.tensor_tensor(w_lo[j % 2][:, part], w_raw[j % 2][:, part],
                                  w_hi[j % 2][:, part].bitcast(F32), ALU.subtract).then_inc(w_lo_ready, end - q)

            def inverse(r):
                link(dve.reciprocal(r, r))

            dve.wait_ge(gain_ps, 1)
            dve.tensor_copy(gain_t[:, 0:GAIN_ROWS], TR[0][:, 0:GAIN_ROWS]).then_inc(gain_ready, 1)
            dve.wait_ge(gain_ready, 1)

            def scale_rows(which):
                tok, s0, cnt = (mem_tok, 0, MB) if which == "mem" else (x_tok, MB, TB)
                dve.wait_ge(root_done, 1 if which == "mem" else 2)
                inverse(stat[:, 8 + s0:8 + s0 + cnt])
                for t in range(cnt):
                    dve.tensor_scalar(tok[:, t, :], tok[:, t, :], stat[:, 8 + s0 + t:9 + s0 + t], None, ALU.mult).then_inc(xn_ready, 1)

            n_hi = n_gate = 0

            def minus_hi(dst, ps, hi):
                return dve.tensor_tensor(dst, ps, hi.bitcast(F32), ALU.subtract)

            def norm(which, n):
                a = acc_at["ssq", which]
                dve.wait_ge(acc_free[bank_of[a]], use_of[a] + 1)
                if n < NORM_PARTS:
                    w = S // NORM_PARTS
                    cols = slice(w * n, w * n + w)
                    link(dve.reciprocal(rms_root[:, cols], rms_root[:, cols]))
                    return
                c, g0 = (c_q, G_Q) if which == "q" else (c_kv, G_KV)
                i = n - NORM_PARTS
                dve.scalar_tensor_tensor(c[:, i, :], c[:, i, :], gain_t[:, g0 + i:g0 + i + 1], rms_root[:],
                                         ALU.mult, ALU.mult).then_inc(latent_ready, 1)

            def rotate(dst, src, cos, sin):
                swap = [16 * (q // 16) + (q % 16 + 8) % 16 for q in range(32)]
                rows = slice(NOPE, MLA_QK)
                link(dve.stream_shuffle(rope_b[rows, :], src, swap))
                link(dve.tensor_tensor(rope_b[rows, :], rope_b[rows, :], sin, ALU.mult))
                link(dve.tensor_tensor(rope_a[rows, :], src, cos, ALU.mult))
                return dve.tensor_tensor(dst, rope_a[rows, :], rope_b[rows, :], ALU.add)

            for n, st in enumerate(steps):
                if st[0] in ("turn", "route", "turn_h", "part", "rope_load"):
                    continue
                if st[0] == "split":
                    split_lo(*st[1:])
                    continue
                if st[0] == "rms":
                    scale_rows(st[1])
                    continue
                if st[0] == "latent":
                    for i in range(st[1], st[2]):
                        dve.wait_ge(latent_hi, i + 1)
                        dst, hi, src = ((cq_lo, cq_hi, c_q), (ckv_lo, ckv_hi, c_kv))[i // 3]
                        k = i % 3
                        dve.tensor_tensor(dst[:, k, :], src[:, k, :], hi[:, k, :].bitcast(F32), ALU.subtract).then_inc(latent_ready, 1)
                    continue
                if st[0] == "norm":
                    norm(*st[1:])
                    continue
                if st[0] == "rotate_key":
                    dve.wait_ge(acc_free[bank_of[acc_at["kpe",]]], use_of[acc_at["kpe",]] + 1)
                    rotate(k_pe[NOPE:MLA_QK, :], k_pe[NOPE:MLA_QK, :], rope_cs[NOPE:MLA_QK, 0, :], rope_cs[NOPE:MLA_QK, 1, :]).then_inc(rope_ready, 1)
                    dve.wait_ge(rope_ready, 1)
                    continue
                if st[0] == "unit":
                    u = unit_at(st, COPY_LAG)
                    if u is not None and copier(u) == 1:
                        probs_out(dve, u, 1)
                    u = unit_at(st)
                    if u is not None:
                        br, g, qb, hp = UNITS[u]
                        dve.wait_ge(score_done, u + 1)
                        m = soft_m[:, u % 4, :]
                        if br == "na":
                            if u >= 3:
                                dve.wait_ge(t_done, u - 2)
                            s0, ds, ns = table_slots(qb)
                            w = P * ns
                            bias = table[:, 2 * g + hp, s0:s0 + ds * (ns - 1) + 1:ds, :]
                            link(dve.tensor_tensor(probs[u % 3][:, 0:w].rearrange("p (a b) -> p a b", a=ns),
                                                   SC[u % 3][:, 0:w].rearrange("p (a b) -> p a b", a=ns), bias, ALU.add))
                            dve.tensor_reduce(m[:, 0:1], probs[u % 3][:, 0:w], AX.X, ALU.max, negate=True).then_inc(max_done, 1)
                        elif br == "mem":
                            dve.tensor_reduce(m, SC[u % 3][:].rearrange("p (a b) -> p a b", a=2), AX.X, ALU.max, negate=True).then_inc(max_done, 1)
                        else:
                            dve.tensor_reduce(m[:, 0:1], SC[u % 3][:], AX.X, ALU.max, negate=True).then_inc(max_done, 1)
                    u = unit_at(st, NORM_LAG)
                    if u is not None:
                        br, _, qb, _ = UNITS[u]
                        dve.wait_ge(exp_done, u + 1)
                        nh = 2 if br == "mem" else 1
                        link(dve.reciprocal(soft_r[:, u % 4, 0:nh], soft_s[:, u % 4, 0:nh]))
                        for hp in range(nh):
                            part = slice(256 * hp, 256 * hp + 256) if nh == 2 else slice(0, width_of(br, qb))
                            last = dve.tensor_scalar(probs[u % 3][:, part], probs[u % 3][:, part], soft_r[:, u % 4, hp:hp + 1], None, ALU.mult)
                        last.then_inc(p_ready, 1)
                    g = group_ending(st, OUT_LAG)
                    if g is not None:
                        br = GROUPS[g][0]
                        for hp in range(2 if br == "mem" else 1):
                            a = y_acc[g] + hp
                            n_hi += 1
                            dve.wait_ge(hi_done, n_hi)
                            minus_hi(y_part(y_lo, br, GROUPS[g][1], hp)[:], ACC[bank_of[a]][:], y_part(y_hi, br, GROUPS[g][1], hp)[:]).then_inc(acc_free[bank_of[a]], 1)
                    continue
                kind, args = st[1], st[2]
                a = acc_of[n]
                ps = ACC[bank_of[a]]
                if kind in ("memT", "nT"):
                    kb, = args
                    n_hi += 1
                    dve.wait_ge(hi_done, n_hi)
                    if kind == "memT":
                        dst, src, hi, g0 = memt_lo[:, kb, :], ps[:, 0:N_MEM], memt_hi[:, kb, :], G_MEM
                    else:
                        dst, src, hi, g0 = nt_lo[:, kb, :], ps[:], nt_hi[:, kb, :], G_MIX
                    dve.scalar_tensor_tensor(dst, src, gain_t[:, g0 + kb:g0 + kb + 1], hi.bitcast(F32),
                                             ALU.mult, ALU.subtract).then_inc(acc_free[bank_of[a]], 1)
                elif kind == "uq":
                    if args[0] == 0:
                        dve.wait_ge(rope_in, 32)
                    n_hi += 1
                    dve.wait_ge(hi_done, n_hi)
                    rotate(q_mla[NOPE:MLA_QK, args[0], :], ps[NOPE:MLA_QK, :], rope_cs[NOPE:MLA_QK, 0, :],
                           rope_cs[NOPE:MLA_QK, 1, :]).then_inc(acc_free[bank_of[a]], 1)
                    dve.wait_ge(acc_free[bank_of[a]], use_of[a] + 1)
                elif kind == "gate":
                    br_n, d, _ = args
                    i = n_gate % 4
                    dve.wait_ge(acc_free[bank_of[a]], use_of[a] + 1)
                    if br_n == 0:
                        dve.tensor_tensor(merged[:, d, :], branch_o[i][:], gate_s[n_gate % 2][:], ALU.mult).then_inc(gate_used, 1)
                    else:
                        link(dve.tensor_tensor(branch_o[i][:], branch_o[i][:], gate_s[n_gate % 2][:], ALU.mult))
                        dve.tensor_tensor(merged[:, d, :], merged[:, d, :], branch_o[i][:], ALU.add).then_inc(gate_used, 1)
                    n_gate += 1
                    dve.wait_ge(gate_used, n_gate)
                    if br_n == 2:
                        dve.wait_ge(merged_hi, d + 1)
                        dve.tensor_tensor(m_lo[:, d, :], merged[:, d, :], m_hi[:, d, :].bitcast(F32), ALU.subtract).then_inc(merged_lo, 1)
                elif kind == "out":
                    t, c = args
                    dve.wait_ge(acc_done, a + 1)
                    dve.wait_ge(resid_in, 16 * TB)
                    cols = slice(256 * c, 256 * c + 256)
                    dve.tensor_tensor(h_tok[:, t, cols], ps[:, 0:256], h_tok[:, t, cols], ALU.add).then_inc(acc_free[bank_of[a]], 1)
            dve.wait_ge(hsq_done, 4 * TB)
            dve.tensor_reduce(stat[:, 16:16 + TB], h_part[:], AX.X, ALU.add).then_inc(hsum_ready, 1)
            dve.wait_ge(hroot_done, 1)
            inverse(stat[:, 20:20 + TB])

            def scale_h(tiles):
                for t in tiles:
                    dve.tensor_scalar(hr_tok[:, t, :], h_tok[:, t, :], stat[:, 20 + t:21 + t], None, ALU.mult).then_inc(hr_ready, 1)

            scale_h((0, 1))
            dve.wait_ge(bias_in, 16)
            dve.wait_ge(logit_tok, 1)
            for t in range(TB):
                last = dve.scalar_tensor_tensor(aff[:, t, :], bank[1][:, N_EXP * t:N_EXP * t + N_EXP], stat[:, 20 + t:21 + t], route_b[:],
                                                ALU.mult, ALU.add)
            link(last)
            link(dve.tensor_reduce(row_stat[:, 0, :], aff[:], AX.X, ALU.max))
            dve.tensor_tensor(aff[:], aff[:], row_stat[:, 0, :].unsqueeze(2).broadcast_to([P, TB, N_EXP]), ALU.subtract).then_inc(soft_in, 1)
            scale_h((2,))
            dve.wait_ge(soft_exp, 1)
            link(dve.tensor_reduce(row_stat[:, 1, :], aff[:], AX.X, ALU.add))
            link(dve.reciprocal(row_stat[:, 2, :], row_stat[:, 1, :]))
            dve.tensor_tensor(aff[:], aff[:], row_stat[:, 2, :].unsqueeze(2).broadcast_to([P, TB, N_EXP]), ALU.mult).then_inc(aff_ready, 1)
            scale_h((3,))
            dve.wait_ge(aff_ps, 1)
            for r in range(CAP // 8):
                v8, i8 = top_v[:, 8 * r:8 * r + 8], top_i[:, 8 * r:8 * r + 8]
                left = bank[2][0:N_EXP, :] if r == 0 else aff_t[:]
                link(dve.max(v8, left))
                link(dve.max_index(i8, v8, left))
                if r < CAP // 8 - 1:
                    link(dve.match_replace(aff_t[:], v8, left, -1.0))
            for r in range(2):
                last = dve.tensor_copy(top_f[:, CAP * r:CAP * r + CAP], top_i[:])
            last.then_inc(top_ready, 1)
            dve.tensor_copy(top_v[:, CAP:2 * CAP], top_v[:, 0:CAP]).then_inc(top_ready, 1)
            dve.wait_ge(top_ps, 1)
            for i in range(2):
                last = dve.tensor_copy(slot_tok[CAP * i:CAP * i + CAP, :], bank[3][CAP * i:CAP * i + CAP, N_EXP + i:2 * N_EXP:2])
            last.then_inc(slots_ready, 1)
            dve.tensor_copy(slot_gain[:], bank[3][:, 0:N_EXP])
            link(dve.tensor_copy(slot_id[:], bank[3][:, N_EXP:2 * N_EXP]))

            def gained_rows(j):
                for b in range(2):
                    dve.wait_ge(xs_tr, 2 * j + (b + 1))
                    g4 = gain_t[:, G_FFN + 4 * b:G_FFN + 4 * b + 4].unsqueeze(2).broadcast_to([P, 4, P])
                    dve.tensor_tensor(xs_t[:, 4 * b:4 * b + 4, :], bank[6 + b][:].rearrange("p (k n) -> p k n", k=4), g4, ALU.mult).then_inc(xs_t_ready, 1)

            def add_rows(e):
                for t in range(TB):
                    dve.wait_ge(comb_ps, TB * e + (t + 1))
                    for hf in range(2):
                        cols = slice(HALF * hf, HALF * hf + HALF)
                        dve.tensor_tensor(h_tok[:, t, cols], tok_banks(e, t)[hf][:], h_tok[:, t, cols], ALU.add).then_inc(summed, 1)

            def pair(j, first=False, more=True):
                for i in range(2):
                    e = 2 * j + i
                    dve.wait_ge(sig_ready, e + 1)
                    dve.tensor_tensor(hidden[:], silu_s[:], bank[0][:], ALU.mult).then_inc(silu_ready, 1)
                    if not (first and i == 0):
                        add_rows(e - 1)
                    dve.wait_ge(silu_ready, e + 1)
                    dve.wait_ge(up_mm, e + 1)
                    dve.tensor_tensor(hidden[:], hidden[:], bank[1][:], ALU.mult).then_inc(hid_ready, 1)
                    dve.tensor_scalar(one_hot[:], tok_row[:], slot_id[:, bass.ds(e, 1)], None, ALU.is_equal).then_inc(hot_ready, 1)
                    if i == 1 and more:
                        gained_rows(j + 1)
                    dve.wait_ge(y_hi_ready, e + 1)
                    dve.scalar_tensor_tensor(ye_lo[:], bank[4][:], slot_gain[:, bass.ds(e, 1)], ye_hi[:].bitcast(F32),
                                             ALU.mult, ALU.subtract).then_inc(y_ready, 1)

            dve.wait_ge(tok_ready, 1)
            gained_rows(0)
            pair(0, first=True)
            with dve.Fori(1, PAIRS - 1) as j:
                pair(j)
            pair(PAIRS - 1, more=False)
            add_rows(N_EXP - 1)
            dve.wait_ge(fin_g_in, 16)
            for t in range(TB):
                dve.wait_ge(fin_root, t + 1)
                link(dve.reciprocal(stat[:, 40 + t:41 + t], stat[:, 36 + t:37 + t]))
                dve.scalar_tensor_tensor(h_tok[:, t, :], h_tok[:, t, :], stat[:, 40 + t:41 + t], fin_g[:], ALU.mult, ALU.mult).then_inc(fin_ready, 1)


INPUTS = ["x", "mem", "g_mix", "w_in", "na_rpb", "mla_q_norm", "w_mla_uq", "mla_kv_norm", "w_mla_ukv", "g_mem",
          "w_mem_kv", "w_o_na", "w_o_mla", "w_o_mem", "w_out", "g_ffn", "w_router", "b_router", "w_gate", "w_up",
          "w_down", "g_final"]


def shape_constants():
    t = np.arange(S)
    col, row = t // ROWS, t % ROWS
    d = ROPE // 2
    inv = (ROPE_BASE ** (-np.arange(0, d, 2, dtype=np.float32) / d)).astype(np.float32)
    cos, sin = np.zeros((ROPE, S), np.float32), np.zeros((ROPE, S), np.float32)
    for part, pos in enumerate((row, col)):
        ang = (pos.astype(np.float32)[None, :] * inv[:, None]).astype(np.float32)
        r0 = d * part
        cos[r0:r0 + d // 2] = cos[r0 + d // 2:r0 + d] = np.cos(ang)
        sin[r0:r0 + d // 2] = -np.sin(ang)
        sin[r0 + d // 2:r0 + d] = np.sin(ang)
    return {"rope_cos": cos, "rope_sin": sin}


def kernel(**inputs):
    import concourse.bacc as bacc
    from concourse.bass_utils import run_bass_kernel_spmd

    nc = bacc.Bacc("TRN2", target_bir_lowering=False, num_devices=1)
    arrays, aps = {}, {}
    given = {name: np.ascontiguousarray(inputs[name]) for name in INPUTS}
    given.update(shape_constants())
    for name, a in given.items():
        arrays[f"in_{name}"] = a
        aps[name] = nc.dram_tensor(f"in_{name}", a.shape, mybir.dt.from_np(a.dtype), kind="ExternalInput").ap()
    out = nc.dram_tensor("out", (1, S, D), F32, kind="ExternalOutput").ap()
    build(nc, aps, out)
    return run_bass_kernel_spmd(nc, [arrays], core_ids=[0]).results[0]["out"]
```
